# Optimizing a Trainium2 kernel written in Bass

```python
import math
import jax, jax.numpy as jnp
from jax import lax
import numpy as np

D_MODEL = 1024
BATCH = 1
SEQ = 256
DEPTH = 2

N_MIXERS = 2
N_CONV_LAYERS = (DEPTH + 1) // 2
N_ATTN_LAYERS = DEPTH // 2
N_HEADS = 16
HEAD_DIM = D_MODEL // N_HEADS
MOBA_BLOCK = 256
MOBA_TOP_K = 3
Q_CHUNK = 64
CONV_WIDTH = 31
D_FF = 4 * D_MODEL
N_MOD = 6
EPS = 1e-6


def rms_norm(x, g):
    xf = x.astype(jnp.float32)
    y = xf * lax.rsqrt(jnp.mean(xf * xf, axis=-1, keepdims=True) + EPS)
    return (y * g.astype(jnp.float32)).astype(x.dtype)

def layer_norm(x, g, b):
    xf = x.astype(jnp.float32)
    mu = jnp.mean(xf, axis=-1, keepdims=True)
    xc = xf - mu
    var = jnp.mean(xc * xc, axis=-1, keepdims=True)
    y = xc * lax.rsqrt(var + EPS) * g.astype(jnp.float32) + b.astype(jnp.float32)
    return y.astype(x.dtype)

def alibi_slopes(n_heads):
    return jnp.asarray(2.0 ** (-8.0 * np.arange(1, n_heads + 1) / n_heads), dtype=jnp.float32)

def conformer_conv(h, w_in, b_in, dw, dw_b, ln_g, ln_b, w_out, b_out):
    d = h.shape[-1]
    a, g = jnp.split(h @ w_in + b_in, 2, axis=-1)
    u = a * jax.nn.sigmoid(g)
    u = lax.conv_general_dilated(
        u, dw[:, None, :].astype(u.dtype), window_strides=(1,),
        padding=((CONV_WIDTH - 1, 0),),
        dimension_numbers=('NWC', 'WIO', 'NWC'),
        feature_group_count=d) + dw_b
    u = jax.nn.silu(layer_norm(u, ln_g, ln_b))
    return u @ w_out + b_out

def moba_attention(h, w_qkv, q_norm_g, k_norm_g, w_o):
    B, S, D = h.shape
    H, DH = N_HEADS, HEAD_DIM
    q, k, v = jnp.split(h @ w_qkv, 3, axis=-1)
    to_heads = lambda z: z.reshape(B, S, H, DH).transpose(0, 2, 1, 3)
    q = rms_norm(to_heads(q), q_norm_g)
    k = rms_norm(to_heads(k), k_norm_g)
    v = to_heads(v)

    nb = -(-S // MOBA_BLOCK)
    s_pad = nb * MOBA_BLOCK
    pad = ((0, 0), (0, 0), (0, s_pad - S), (0, 0))
    q, k, v = jnp.pad(q, pad), jnp.pad(k, pad), jnp.pad(v, pad)
    k_blocks = k.reshape(B, H, nb, MOBA_BLOCK, DH)
    v_blocks = v.reshape(B, H, nb, MOBA_BLOCK, DH)
    k_mean = jnp.mean(k_blocks.astype(jnp.float32), axis=3)

    topk = min(MOBA_TOP_K, nb)
    slopes = alibi_slopes(H)
    scale = 1.0 / math.sqrt(DH)
    n_chunks = s_pad // Q_CHUNK
    q_chunks = q.reshape(B, H, n_chunks, Q_CHUNK, DH).transpose(2, 0, 1, 3, 4)
    bi = jnp.arange(B)[:, None, None, None]
    hi = jnp.arange(H)[None, :, None, None]
    blk_ids = jnp.arange(nb)
    in_block = jnp.arange(MOBA_BLOCK)

    def chunk_fn(args):
        qc, ci = args
        t = ci * Q_CHUNK + jnp.arange(Q_CHUNK)
        blk = (ci * Q_CHUNK) // MOBA_BLOCK
        gate = jnp.einsum('bhqd,bhnd->bhqn', qc.astype(jnp.float32), k_mean)
        gate = jnp.where(blk_ids < blk, gate, -jnp.inf)
        gate_val, sel = lax.top_k(gate, topk)
        sel_ok = jnp.isfinite(gate_val)
        k_sel = k_blocks[bi, hi, sel]
        v_sel = v_blocks[bi, hi, sel]
        s_sel = jnp.einsum('bhqd,bhqcsd->bhqcs', qc, k_sel).astype(jnp.float32) * scale
        pos_sel = sel[..., None] * MOBA_BLOCK + in_block
        dist_sel = t[None, None, :, None, None] - pos_sel
        s_sel = s_sel - slopes[None, :, None, None, None] * dist_sel
        s_sel = jnp.where(sel_ok[..., None], s_sel, -jnp.inf)
        k_own = lax.dynamic_slice_in_dim(k, blk * MOBA_BLOCK, MOBA_BLOCK, axis=2)
        v_own = lax.dynamic_slice_in_dim(v, blk * MOBA_BLOCK, MOBA_BLOCK, axis=2)
        s_own = jnp.einsum('bhqd,bhsd->bhqs', qc, k_own).astype(jnp.float32) * scale
        dist_own = t[:, None] - (blk * MOBA_BLOCK + in_block)[None, :]
        s_own = jnp.where(dist_own >= 0, s_own - slopes[None, :, None, None] * dist_own, -jnp.inf)
        scores = jnp.concatenate([s_sel.reshape(B, H, Q_CHUNK, topk * MOBA_BLOCK), s_own], axis=-1)
        p = jax.nn.softmax(scores, axis=-1)
        p_sel = p[..., :topk * MOBA_BLOCK].reshape(B, H, Q_CHUNK, topk, MOBA_BLOCK).astype(v.dtype)
        p_own = p[..., topk * MOBA_BLOCK:].astype(v.dtype)
        return (jnp.einsum('bhqcs,bhqcsd->bhqd', p_sel, v_sel)
                + jnp.einsum('bhqs,bhsd->bhqd', p_own, v_own))

    out = lax.map(chunk_fn, (q_chunks, jnp.arange(n_chunks)))
    out = out.transpose(1, 2, 0, 3, 4).reshape(B, H, s_pad, DH)[:, :, :S]
    out = out.transpose(0, 2, 1, 3).reshape(B, S, D)
    return out @ w_o

def first_inputs(seed: int = 0) -> dict:
    key = jax.random.key(seed)
    ks = iter(jax.random.split(key, 32))
    nrm = lambda shape, s: jax.random.normal(next(ks), shape, jnp.float32) * s
    D = D_MODEL
    return {
        "x": nrm((BATCH, SEQ, D), 1.0),
        "c": nrm((BATCH, D), 1.0),
        "ada_w": nrm((DEPTH, D, N_MOD * D), 0.5 * D ** -0.5),
        "ada_b": nrm((DEPTH, N_MOD * D), 0.02),
        "mix_norm_g": 1.0 + nrm((DEPTH, D), 0.1),
        "mlp_norm_g": 1.0 + nrm((DEPTH, D), 0.1),
        "conv_w_in": nrm((N_CONV_LAYERS, D, 2 * D), D ** -0.5),
        "conv_b_in": nrm((N_CONV_LAYERS, 2 * D), 0.02),
        "conv_dw": nrm((N_CONV_LAYERS, CONV_WIDTH, D), CONV_WIDTH ** -0.5),
        "conv_dw_b": nrm((N_CONV_LAYERS, D), 0.02),
        "conv_ln_g": 1.0 + nrm((N_CONV_LAYERS, D), 0.1),
        "conv_ln_b": nrm((N_CONV_LAYERS, D), 0.02),
        "conv_w_out": nrm((N_CONV_LAYERS, D, D), D ** -0.5),
        "conv_b_out": nrm((N_CONV_LAYERS, D), 0.02),
        "attn_w_qkv": nrm((N_ATTN_LAYERS, D, 3 * D), D ** -0.5),
        "attn_q_norm_g": 1.0 + nrm((N_ATTN_LAYERS, HEAD_DIM), 0.1),
        "attn_k_norm_g": 1.0 + nrm((N_ATTN_LAYERS, HEAD_DIM), 0.1),
        "attn_w_o": nrm((N_ATTN_LAYERS, D, D), D ** -0.5),
        "mlp_w1": nrm((DEPTH, D, D_FF), D ** -0.5),
        "mlp_w2": nrm((DEPTH, D_FF, D), D_FF ** -0.5),
    }

def first_block(x, c, ada_w, ada_b, mix_norm_g, mlp_norm_g,
              conv_w_in, conv_b_in, conv_dw, conv_dw_b, conv_ln_g, conv_ln_b, conv_w_out, conv_b_out,
              attn_w_qkv, attn_q_norm_g, attn_k_norm_g, attn_w_o,
              mlp_w1, mlp_w2):
    cond = jax.nn.silu(c)
    for i in range(DEPTH):
        mod = cond @ ada_w[i] + ada_b[i]
        sh1, sc1, g1, sh2, sc2, g2 = [m[:, None, :] for m in jnp.split(mod, N_MOD, axis=-1)]
        h = rms_norm(x, mix_norm_g[i]) * (1.0 + sc1) + sh1
        j = i // N_MIXERS
        if i % N_MIXERS == 0:
            y = conformer_conv(h, conv_w_in[j], conv_b_in[j], conv_dw[j], conv_dw_b[j],
                               conv_ln_g[j], conv_ln_b[j], conv_w_out[j], conv_b_out[j])
        else:
            y = moba_attention(h, attn_w_qkv[j], attn_q_norm_g[j], attn_k_norm_g[j], attn_w_o[j])
        x = x + g1 * y
        h = rms_norm(x, mlp_norm_g[i]) * (1.0 + sc2) + sh2
        x = x + g2 * (jnp.square(jax.nn.relu(h @ mlp_w1[i])) @ mlp_w2[i])
    return x


GRID_W = 64
CTX_LEN = 256
CHUNK = 128
A_WIDTH = 2 * D_MODEL
A_GROUPS = 8
A_GW = A_WIDTH // A_GROUPS
HEAD_DIM_2 = 64
N_HEADS_2 = D_MODEL // HEAD_DIM_2
N_KV_HEADS = N_HEADS_2 // 4
GQA_GROUP = N_HEADS_2 // N_KV_HEADS
B_WIDTH = N_HEADS_2 * HEAD_DIM_2
KV_WIDTH = N_KV_HEADS * HEAD_DIM_2
WINDOW = 128
ATT_BLOCK = 128
BAND = ATT_BLOCK + 2 * WINDOW
ROPE_AXIS_DIM = HEAD_DIM_2 // 2
ROPE_BASE = 10000.0
LN_EPS = 1e-5
NEG_INF = -1e30


def layer_norm_2(x, g, b):
    xf = x.astype(jnp.float32)
    mu = jnp.mean(xf, axis=-1, keepdims=True)
    var = jnp.mean(jnp.square(xf - mu), axis=-1, keepdims=True)
    y = (xf - mu) * lax.rsqrt(var + LN_EPS) * g.astype(jnp.float32) + b.astype(jnp.float32)
    return y.astype(x.dtype)

def chunk_spatial_mix(v, w_s, b_s):
    bsz, length, _ = v.shape
    vc = v.reshape(bsz, length // CHUNK, CHUNK, A_GROUPS, A_GW)
    s = jnp.einsum('gpq,bnqgc->bnpgc', w_s, vc) + b_s.T[None, None, :, :, None]
    return s.reshape(bsz, length, A_WIDTH)

def mixer_a(h, w_in, ln_g, ln_b, w_s, b_s, w_out):
    u, v, z = jnp.split(h @ w_in, 3, axis=-1)
    u = jax.nn.gelu(u)
    v = layer_norm_2(jax.nn.gelu(v), ln_g, ln_b)
    y = u * chunk_spatial_mix(v, w_s, b_s)
    return (y * jax.nn.silu(z)) @ w_out

def axial_rope_angles(length):
    rows = length // GRID_W
    row = jnp.repeat(jnp.arange(rows), GRID_W).astype(jnp.float32)
    col = jnp.tile(jnp.arange(GRID_W), rows).astype(jnp.float32)
    n_freq = ROPE_AXIS_DIM // 2
    inv = ROPE_BASE ** (-jnp.arange(n_freq, dtype=jnp.float32) / n_freq)
    return row[:, None] * inv[None, :], col[:, None] * inv[None, :]

def rotate_axis(x, ang):
    x1, x2 = jnp.split(x, 2, axis=-1)
    cos = jnp.cos(ang)[None, :, None, :].astype(x.dtype)
    sin = jnp.sin(ang)[None, :, None, :].astype(x.dtype)
    return jnp.concatenate([x1 * cos - x2 * sin, x2 * cos + x1 * sin], axis=-1)

def apply_axial_rope(x, ang_row, ang_col):
    xr, xc = jnp.split(x, 2, axis=-1)
    return jnp.concatenate([rotate_axis(xr, ang_row), rotate_axis(xc, ang_col)], axis=-1)

def project_qkvz(h, w_in):
    bsz, length, _ = h.shape
    q, k, v, z = jnp.split(h @ w_in, [B_WIDTH, B_WIDTH + KV_WIDTH, B_WIDTH + 2 * KV_WIDTH], axis=-1)
    return (q.reshape(bsz, length, N_HEADS_2, HEAD_DIM_2),
            k.reshape(bsz, length, N_KV_HEADS, HEAD_DIM_2),
            v.reshape(bsz, length, N_KV_HEADS, HEAD_DIM_2), z)

def project_kv(h, w_in):
    bsz, length, _ = h.shape
    k, v = jnp.split(h @ w_in[:, B_WIDTH:B_WIDTH + 2 * KV_WIDTH], 2, axis=-1)
    return (k.reshape(bsz, length, N_KV_HEADS, HEAD_DIM_2),
            v.reshape(bsz, length, N_KV_HEADS, HEAD_DIM_2))

def windowed_attention_with_context(q, k, v, k_ctx, v_ctx, sink):
    bsz, length = q.shape[:2]
    n_ctx = k_ctx.shape[1]
    nb = length // ATT_BLOCK
    scale = HEAD_DIM_2 ** -0.5
    qg = q.reshape(bsz, length, N_KV_HEADS, GQA_GROUP, HEAD_DIM_2)
    pad = ((0, 0), (WINDOW, WINDOW), (0, 0), (0, 0))
    k_pad = jnp.pad(k, pad)
    v_pad = jnp.pad(v, pad)
    sink_l = sink.astype(jnp.float32).reshape(1, N_KV_HEADS, GQA_GROUP, 1, 1)
    qi = jnp.arange(ATT_BLOCK)[:, None]
    kj = jnp.arange(BAND)[None, :]
    rel = kj - WINDOW - qi

    def block(i):
        start = i * ATT_BLOCK
        qb = lax.dynamic_slice_in_dim(qg, start, ATT_BLOCK, axis=1)
        kb = lax.dynamic_slice_in_dim(k_pad, start, BAND, axis=1)
        vb = lax.dynamic_slice_in_dim(v_pad, start, BAND, axis=1)
        key_pos = start - WINDOW + kj
        valid = (jnp.abs(rel) <= WINDOW) & (key_pos >= 0) & (key_pos < length)
        s_loc = jnp.einsum('bqhgd,bkhd->bhgqk', qb, kb).astype(jnp.float32) * scale
        s_loc = jnp.where(valid, s_loc, NEG_INF)
        s_ctx = jnp.einsum('bqhgd,bkhd->bhgqk', qb, k_ctx).astype(jnp.float32) * scale
        s_sink = jnp.broadcast_to(sink_l, s_loc.shape[:-1] + (1,))
        p = jax.nn.softmax(jnp.concatenate([s_loc, s_ctx, s_sink], axis=-1), axis=-1)
        p_loc = p[..., :BAND].astype(v.dtype)
        p_ctx = p[..., BAND:BAND + n_ctx].astype(v.dtype)
        return (jnp.einsum('bhgqk,bkhd->bqhgd', p_loc, vb)
                + jnp.einsum('bhgqk,bkhd->bqhgd', p_ctx, v_ctx))

    out = lax.map(block, jnp.arange(nb))
    return jnp.moveaxis(out, 0, 1).reshape(bsz, length, B_WIDTH)

def context_attention(q_ctx, k_ctx, v_ctx, sink):
    bsz, n_ctx = q_ctx.shape[:2]
    scale = HEAD_DIM_2 ** -0.5
    qg = q_ctx.reshape(bsz, n_ctx, N_KV_HEADS, GQA_GROUP, HEAD_DIM_2)
    s = jnp.einsum('bqhgd,bkhd->bhgqk', qg, k_ctx).astype(jnp.float32) * scale
    s_sink = jnp.broadcast_to(sink.astype(jnp.float32).reshape(1, N_KV_HEADS, GQA_GROUP, 1, 1),
                              s.shape[:-1] + (1,))
    p = jax.nn.softmax(jnp.concatenate([s, s_sink], axis=-1), axis=-1)
    o = jnp.einsum('bhgqk,bkhd->bqhgd', p[..., :n_ctx].astype(v_ctx.dtype), v_ctx)
    return o.reshape(bsz, n_ctx, B_WIDTH)

def mixer_b(h, hc, w_in, sink, w_out, ang_row, ang_col, need_ctx_out):
    q, k, v, z = project_qkvz(h, w_in)
    q = apply_axial_rope(q, ang_row, ang_col)
    k = apply_axial_rope(k, ang_row, ang_col)
    if need_ctx_out:
        qc, kc, vc, zc = project_qkvz(hc, w_in)
    else:
        kc, vc = project_kv(hc, w_in)
    o = windowed_attention_with_context(q, k, v, kc, vc, sink)
    out = (o * jax.nn.silu(z)) @ w_out
    out_c = None
    if need_ctx_out:
        oc = context_attention(qc, kc, vc, sink)
        out_c = (oc * jax.nn.silu(zc)) @ w_out
    return out, out_c

def second_inputs(seed: int = 0) -> dict:
    key = jax.random.key(seed)
    ks = jax.random.split(key, 20)
    n_a = (DEPTH + N_MIXERS - 1) // N_MIXERS
    n_b = DEPTH // N_MIXERS
    beta = (8.0 * DEPTH) ** -0.25
    nrm = jax.random.normal
    f32 = jnp.float32
    return {
        "x": nrm(ks[0], (BATCH, SEQ, D_MODEL), f32),
        "c": nrm(ks[1], (BATCH, D_MODEL), f32),
        "ctx": nrm(ks[2], (BATCH, CTX_LEN, D_MODEL), f32),
        "c_ctx": nrm(ks[3], (D_MODEL,), f32),
        "ada_w": nrm(ks[4], (DEPTH, D_MODEL, 3 * D_MODEL), f32) * (0.5 * D_MODEL ** -0.5),
        "ada_b": nrm(ks[5], (DEPTH, 3 * D_MODEL), f32) * 0.01,
        "ln_g": 1.0 + 0.05 * nrm(ks[6], (DEPTH, D_MODEL), f32),
        "ln_b": 0.01 * nrm(ks[7], (DEPTH, D_MODEL), f32),
        "a_w_in": nrm(ks[8], (n_a, D_MODEL, 3 * A_WIDTH), f32) * D_MODEL ** -0.5,
        "a_ln_g": 1.0 + 0.05 * nrm(ks[9], (n_a, A_WIDTH), f32),
        "a_ln_b": 0.01 * nrm(ks[10], (n_a, A_WIDTH), f32),
        "a_w_s": nrm(ks[11], (n_a, A_GROUPS, CHUNK, CHUNK), f32) * CHUNK ** -0.5,
        "a_b_s": 1.0 + 0.05 * nrm(ks[12], (n_a, A_GROUPS, CHUNK), f32),
        "a_w_out": nrm(ks[13], (n_a, A_WIDTH, D_MODEL), f32) * (A_WIDTH ** -0.5 * beta),
        "b_w_in": nrm(ks[14], (n_b, D_MODEL, 2 * B_WIDTH + 2 * KV_WIDTH), f32) * D_MODEL ** -0.5,
        "b_sink": 0.5 * nrm(ks[15], (n_b, N_HEADS_2), f32),
        "b_w_out": nrm(ks[16], (n_b, B_WIDTH, D_MODEL), f32) * (B_WIDTH ** -0.5 * beta),
    }

def second_block(x, c, ctx, c_ctx, ada_w, ada_b, ln_g, ln_b,
              a_w_in, a_ln_g, a_ln_b, a_w_s, a_b_s, a_w_out,
              b_w_in, b_sink, b_w_out):
    alpha = (2.0 * DEPTH) ** 0.25
    length = x.shape[1]
    ang_row, ang_col = axial_rope_angles(length)
    cond = jax.nn.silu(c)
    cond_ctx = jax.nn.silu(c_ctx)
    for i in range(DEPTH):
        j = i // N_MIXERS
        need_ctx_out = i < DEPTH - 1
        shift, scale, gate = jnp.split(cond @ ada_w[i] + ada_b[i], 3, axis=-1)
        shift_c, scale_c, gate_c = jnp.split(cond_ctx @ ada_w[i] + ada_b[i], 3, axis=-1)
        h = x * (1.0 + scale[:, None, :]) + shift[:, None, :]
        hc = ctx * (1.0 + scale_c) + shift_c
        if i % N_MIXERS == 0:
            out = mixer_a(h, a_w_in[j], a_ln_g[j], a_ln_b[j], a_w_s[j], a_b_s[j], a_w_out[j])
            out_c = (mixer_a(hc, a_w_in[j], a_ln_g[j], a_ln_b[j], a_w_s[j], a_b_s[j], a_w_out[j])
                     if need_ctx_out else None)
        else:
            out, out_c = mixer_b(h, hc, b_w_in[j], b_sink[j], b_w_out[j], ang_row, ang_col, need_ctx_out)
        x = layer_norm_2(alpha * x + gate[:, None, :] * out, ln_g[i], ln_b[i])
        if need_ctx_out:
            ctx = layer_norm_2(alpha * ctx + gate_c * out_c, ln_g[i], ln_b[i])
    return x


def setup_inputs(seed=0):
    out = dict(first_inputs(seed))
    for name, value in second_inputs(seed + 1).items():
        if name != "x":
            out[name + "_2"] = value
    return out


def reference(
    x, c, ada_w, ada_b, mix_norm_g, mlp_norm_g, conv_w_in, conv_b_in, conv_dw, conv_dw_b,
    conv_ln_g, conv_ln_b, conv_w_out, conv_b_out, attn_w_qkv, attn_q_norm_g, attn_k_norm_g,
    attn_w_o, mlp_w1, mlp_w2, c_2, ctx_2, c_ctx_2, ada_w_2, ada_b_2, ln_g_2, ln_b_2, a_w_in_2,
    a_ln_g_2, a_ln_b_2, a_w_s_2, a_b_s_2, a_w_out_2, b_w_in_2, b_sink_2, b_w_out_2,
):
    x = first_block(
        x, c, ada_w, ada_b, mix_norm_g, mlp_norm_g, conv_w_in, conv_b_in, conv_dw, conv_dw_b,
        conv_ln_g, conv_ln_b, conv_w_out, conv_b_out, attn_w_qkv, attn_q_norm_g, attn_k_norm_g,
        attn_w_o, mlp_w1, mlp_w2,
    )
    return second_block(
        x, c_2, ctx_2, c_ctx_2, ada_w_2, ada_b_2, ln_g_2, ln_b_2, a_w_in_2, a_ln_g_2, a_ln_b_2,
        a_w_s_2, a_b_s_2, a_w_out_2, b_w_in_2, b_sink_2, b_w_out_2,
    )


_drawn_inputs = setup_inputs


def setup_inputs(seed=0):
    import zlib

    import numpy as np

    out = dict(_drawn_inputs(seed))
    spreads = {}
    factors = {'conv_b_in': 8.0,
     'conv_dw_b': 7.645,
     'conv_ln_b': 8.0,
     'conv_b_out': 8.0,
     'attn_q_norm_g': 8.0,
     'attn_k_norm_g': 6.382,
     'ctx_2': 8.0,
     'c_ctx_2': 4.108,
     'ada_b_2': 8.0,
     'ln_b_2': 4.027,
     'a_ln_g_2': 8.0,
     'a_ln_b_2': 8.0,
     'a_b_s_2': 8.0,
     'b_w_in_2': 2.703,
     'b_sink_2': 64.0,
     'b_w_out_2': 2.768}
    for name, (base, spread) in spreads.items():
        noise = np.random.default_rng([zlib.crc32(name.encode()), seed]).standard_normal(out[name].shape)
        drawn = base * np.exp(spread * noise) if base else spread * noise
        out[name] = __import__('jax').numpy.asarray(drawn.astype(out[name].dtype))
    for name, factor in factors.items():
        out[name] = (out[name] * factor).astype(out[name].dtype)
    return out
```

```python
import math
from contextlib import ExitStack

import numpy as np

import concourse.bass as bass
from concourse import mybir

P = 128
D = 1024
KT = D // P
T = 256
UC = 256
UNIT = KT * UC
RING = 4
SPLITS = 2
PAIRS = 3
HEADS = 16
DH = D // HEADS
KV_HEADS = 4
TAPS = 31
PAD = TAPS - 1
ALPHA = math.sqrt(2.0)
EPS = 1e-6
LN_EPS = 1e-5
NEG = -1e30
SCALE = 1.0 / math.sqrt(DH)

F32 = mybir.dt.float32
F32R = mybir.dt.float32r
ALU = mybir.AluOpType
ACT = mybir.ActivationFunctionType
AX = mybir.AxisListType.X



def mlp_units(m):
    order = [("w1", 0), ("w1", 1), ("w2", 0), ("w1", 2), ("w2", 1), ("w1", 3), ("w2", 2), ("w2", 3)]
    return [(kind, m, q, j) for kind, q in order for j in range(4)]


UNITS = []
for j in range(4):
    UNITS += [("conv_a", j), ("conv_g", j)]
CONV_OUT = len(UNITS)
UNITS += [("conv_out", j) for j in range(4)]
MLP0 = len(UNITS)
UNITS += mlp_units(0)
QKV = len(UNITS)
UNITS += [("q", j) for j in range(4)] + [("k", j) for j in range(4)] + [("v", j) for j in range(4)]
WO = len(UNITS)
UNITS += [("wo", j) for j in range(4)]
MLP1 = len(UNITS)
UNITS += mlp_units(1)
MIX_A = len(UNITS)
UNITS += [("a_v", j) for j in range(8)]
for half in range(2):
    for j in range(4):
        UNITS += [("a_u", 4 * half + j), ("a_z", 4 * half + j)]
    UNITS += [("a_out", half, j) for j in range(4)]
MIX_B = len(UNITS)
UNITS += [("b_k", 0), ("b_v", 0)] + [("b_q", j) for j in range(4)] + [("b_z", j) for j in range(4)]
B_OUT = len(UNITS)
UNITS += [("b_out", j) for j in range(4)]
NW = len(UNITS)

VECTORS = [(1, layer, part) for layer in range(2) for part in range(6)]
VECTORS += [(2, layer, part) for layer in range(2) for part in range(3)]

MOD_BEFORE = [0] * NW
MOD_BEFORE[0] = 8 + 1
for s in range(1, 12):
    MOD_BEFORE[s] = 1
for s in range(12, 16):
    MOD_BEFORE[s] = 1
for s in range(16, 44):
    MOD_BEFORE[s] = 1 if (s - 16) % 7 in (0, 1, 3, 4, 6) else 0
for s in range(56, 60):
    MOD_BEFORE[s] = 1
for s in range(60, 92):
    MOD_BEFORE[s] = 1 if s % 8 in (0, 3, 6) else 0
for s in (92, 93, 94, 95, 102, 104, 106, 108, 114, 116, 118, 120):
    MOD_BEFORE[s] = 1
assert sum(MOD_BEFORE) == 4 * len(VECTORS)

STREAM = []
WHERE = []
REDUCE_AFTER = {}
_done = 0
for s in range(NW):
    for _ in range(MOD_BEFORE[s]):
        STREAM.append(("mod", _done // 4, _done % 4))
        _done += 1
        if _done % 4 == 0 and _done > 8:
            REDUCE_AFTER.setdefault(s, []).append(_done // 4 - 1)
    WHERE.append(len(STREAM))
    STREAM.append(("w", s))
NS = len(STREAM)


def mod_ops(vi):
    block, layer, part = VECTORS[vi]
    if block == 2:
        return 2
    return 2 if part in (1, 4) or (layer == 0 and part == 2) else 1


MOD_DONE = [sum(mod_ops(i) for i in range(vi + 1)) for vi in range(len(VECTORS))]

BY_ACT = {"w1", "q", "k", "v", "a_v", "b_k", "b_v", "b_q"}
WITH_NEXT = {"conv_a", "a_u"}
UPDATES = {"conv_out": 2, "w2": 2, "wo": 2, "a_out": 4, "b_out": 2}
DRAINED = []
_n = {"act": 0, "dve": 0, "x": 0}
for u in UNITS:
    who = "act" if u[0] in BY_ACT else "x" if u[0] in UPDATES else "dve"
    if u[0] in WITH_NEXT:
        DRAINED.append((who, _n[who] + 1))
    else:
        _n[who] += UPDATES.get(u[0], 1)
        DRAINED.append((who, _n[who]))

XU_CONV = 0
XU_MLP0 = XU_CONV + 8
XU_WO = XU_MLP0 + 32
XU_MLP1 = XU_WO + 8
XU_A = XU_MLP1 + 32
XU_B = XU_A + 32
XU_END = XU_B + 8

SET_SIZE = [8, 8, 8, 8, 8, 8, 16, 16, 8]
SET = [sum(SET_SIZE[:i]) for i in range(len(SET_SIZE) + 1)]
FIRST_OF_SET = {0: 0, CONV_OUT: 1, MLP0: 2, QKV: 3, WO: 4, MLP1: 5, MIX_A: 6, MIX_B: 7, B_OUT: 8}

LN_INDEX = {1: 0, 5: 1, 6: 2, 7: 3}
STAT_DONE = []
_m = 0
for n in range(8):
    _m += 2 if n in LN_INDEX else 1
    STAT_DONE.append(_m)

COLS = {}
_c = 0
for _name, _k in (
    ("c", 8), ("c_2", 8), ("c_ctx", 8), ("ada_b", 96), ("ada_b_2", 48), ("mix_g", 16), ("mlp_g", 16),
    ("conv_b_in", 16), ("conv_dw", TAPS * 8), ("conv_dw_b", 8), ("conv_ln_g", 8), ("conv_ln_b", 8),
    ("conv_b_out", 8), ("qn_g", 1), ("kn_g", 1), ("ln_g_2", 16), ("ln_b_2", 16), ("a_ln_g", 16),
    ("a_ln_b", 16), ("sink", HEADS),
):
    COLS[_name] = _c
    _c += _k
NCOL = _c

CONST = {}
_c = 0
for _name, _k in (("ident", P), ("ones", P), ("head_ones", P), ("perm", P), ("alibi", 3 * P),
                  ("window", 4 * T), ("cos", T), ("sin", T)):
    CONST[_name] = _c
    _c += _k
NCONST = _c
RESIDENT = CONST["alibi"]


def f_index(w):
    return sum(1 for u in UNITS[:w] if u[0] == "w1")


def head_of(i):
    k, off = i // 4, (i // 2) % 2
    return 4 * (2 * (k // 4) + off) + k % 4


def build(nc, stream, cols_in, const_in, x_in, ctx_in, ws_in, bs_in, out):
    with ExitStack() as ctx:
        def sb(name, shape, dt=F32):
            return ctx.enter_context(nc.sbuf_tensor(name, shape, dt))

        def sem(name):
            return ctx.enter_context(nc.semaphore(name))

        raw = sb("raw", [P, RING, UNIT])
        w_hi = sb("w_hi", [P, SPLITS, KT, UC], F32R)
        w_lo = sb("w_lo", [P, SPLITS, KT, UC], F32R)
        X = sb("X", [P, KT, T])
        C = sb("C", [P, KT, T])
        XH = sb("XH", [P, KT, 2 * T], F32R)
        XL = sb("XL", [P, KT, 2 * T], F32R)
        FH = sb("FH", [P, 2 * KT * T], F32R)
        FL = sb("FL", [P, 2 * KT * T], F32R)
        V = sb("V", [P, 8192])
        HT = sb("HT", [P, KT * T])
        acc = sb("acc", [P, 2, D])
        EV = sb("EV", [P, 2, 2 * T])
        WS = sb("WS", [P, 8, P])
        BS = sb("BS", [P, 8, P])
        SM = sb("SM", [P, 2, 2 * T])
        RR = sb("RR", [P, 2, P])
        col = sb("col", [P, NCOL])
        con = sb("con", [P, RESIDENT])
        cond = sb("cond", [P, 24])
        cond_t = sb("cond_t", [P, 24])
        half_b = sb("half_b", [P, 16])
        mod1 = sb("mod1", [P, 12, KT])
        mod2 = sb("mod2", [P, 6, 2, KT])
        gate_b = sb("gate_b", [P, KT])
        MU = sb("MU", [P, T])
        VAR = sb("VAR", [P, T])
        RSTD = sb("RSTD", [P, T])
        QV = SM[:, 0, :]
        bst = sb("bst", [P, 4, 8, 6])
        mv = sb("mv", [P, 4, 2])
        vr = sb("vr", [P, 4])
        sm = sb("sm", [P, 3, 12])

        prod = ctx.enter_context(nc.psum_tensor("prod", [P, PAIRS, 1024], F32))
        misc = ctx.enter_context(nc.psum_tensor("misc", [P, 2, 512], F32))

        ident = con[:, CONST["ident"]:CONST["ident"] + P]
        ones = con[:, CONST["ones"]:CONST["ones"] + P]
        head_ones = con[:, CONST["head_ones"]:CONST["head_ones"] + P]
        perm = con[:, CONST["perm"]:CONST["perm"] + P]
        alibi = SM[:, 1, 0:3 * P]
        window = SM[:, :, :]
        cos_t = WS[:, 0:2, :].rearrange("p a b -> p (a b)")
        sin_t = WS[:, 2:4, :].rearrange("p a b -> p (a b)")

        def cl(name, i=0, n=1):
            return col[:, COLS[name] + i:COLS[name] + i + n]

        U = V[:, 0:KT * (T + PAD)].rearrange("p (k t) -> p k t", k=KT)
        CV = V[:, 2304:2304 + 2048].rearrange("p (k t) -> p k t", k=KT)
        TS = V[:, 4352:4352 + 2048].rearrange("p (k t) -> p k t", k=KT)
        Q = V[:, 0:2048].rearrange("p (k t) -> p k t", k=KT)
        K1 = V[:, 2048:4096].rearrange("p (k t) -> p k t", k=KT)
        V1 = V[:, 4096:6144].rearrange("p (t c) -> p t c", t=2)
        VA = V[:, :].rearrange("p (t c) -> p t c", t=4)
        K2 = V[:, 2048:3072].rearrange("p (k t) -> p k t", k=2)
        V2 = V[:, 3072:4096].rearrange("p (t c) -> p t c", t=4)
        SZ = V[:, 4096:6144].rearrange("p (k t) -> p k t", k=KT)
        H2 = V[:, 6144:8192].rearrange("p (k t) -> p k t", k=KT)
        H = HT[:, :].rearrange("p (k t) -> p k t", k=KT)
        GU = HT[:, 0:1024]
        TZ = HT[:, 1024:2048]
        RSB = EV[:, :, :].rearrange("p a (b c) -> p (a b) c", c=P)
        F_hi = FH[:, :].rearrange("p (b k t) -> p b k t", b=2, k=KT)
        F_lo = FL[:, :].rearrange("p (b k t) -> p b k t", b=2, k=KT)
        G_hi = FH[:, :].rearrange("p (k t) -> p k t", k=KT)
        G_lo = FL[:, :].rearrange("p (k t) -> p k t", k=KT)
        flat = C[:, :, :].rearrange("p k t -> p (k t)")
        S1 = flat[:, 0:3 * 384].rearrange("p (b n) -> p b n", b=3)
        PT1 = flat[:, 1152:1152 + 2 * 384].rearrange("p (b n) -> p b n", b=2)
        S2 = flat[:, 0:3 * 512].rearrange("p (b n) -> p b n", b=3)
        PT2 = V[:, 6144:6144 + 2 * 512].rearrange("p (b n) -> p b n", b=2)

        params_loaded = sem("params_loaded")
        x_loaded = sem("x_loaded")
        ctx_loaded = sem("ctx_loaded")
        tables_loaded = sem("tables_loaded")
        slot_loaded = [sem(f"slot_loaded{r}") for r in range(RING)]
        out_stored = sem("out_stored")
        unit_consumed = sem("unit_consumed")
        weight_hi = sem("weight_hi")
        unit_done = sem("unit_done")
        cond_tanh = sem("cond_tanh")
        cond_ready = sem("cond_ready")
        half_ready = sem("half_ready")
        acc_step = sem("acc_step")
        acc_reduced = sem("acc_reduced")
        mod_step = sem("mod_step")
        sq_ready = sem("sq_ready")
        stat_done = sem("stat_done")
        mean_ready = sem("mean_ready")
        centred = sem("centred")
        var_prep = sem("var_prep")
        rstd_ready = sem("rstd_ready")
        h_scaled = sem("h_scaled")
        h_final = sem("h_final")
        acts_hi = sem("acts_hi")
        acts_lo = sem("acts_lo")
        x_updated = sem("x_updated")
        drained = {"act": sem("drained_act"), "dve": sem("drained_dve"), "x": x_updated}
        x_scaled = sem("x_scaled")
        padded = sem("padded")
        gate_tanh = sem("gate_tanh")
        gate_half = sem("gate_half")
        conv_step = sem("conv_step")
        silu_tanh = sem("silu_tanh")
        silu_step = sem("silu_step")
        y_ready = sem("y_ready")
        f_relu = sem("f_relu")
        f_hi = sem("f_hi")
        f_sq = sem("f_sq")
        f_lo = sem("f_lo")
        qk_sum = sem("qk_sum")
        qk_prep = sem("qk_prep")
        qk_rstd = sem("qk_rstd")
        qk_final = sem("qk_final")
        scored = sem("scored")
        z_ready = sem("z_ready")
        max_ready = sem("max_ready")
        exp_done = sem("exp_done")
        p_ready = sem("p_ready")
        p_turned = sem("p_turned")
        pt_copied = sem("pt_copied")
        head_out = sem("head_out")
        o_gated = sem("o_gated")
        row_sums = sem("row_sums")
        row_copied = sem("row_copied")
        v_stats = sem("v_stats")
        v_prep = sem("v_prep")
        v_rstd = sem("v_rstd")
        v_normed = sem("v_normed")
        mixed = sem("mixed")
        g_act = sem("g_act")
        g_dve = sem("g_dve")
        g_hi = sem("g_hi")
        g_lo = sem("g_lo")
        z_tanh = sem("z_tanh")
        z_half = sem("z_half")
        turned = sem("turned")
        roped = sem("roped")

        block = ctx.enter_context(nc.Block())

        def pair(w):
            return prod[:, w % PAIRS, :]

        def tiles(w, n):
            return pair(w).rearrange("p (i t) -> p i t", i=2)[:, :, 0:n]

        @block.sync
        def _(sp):
            sp.dma_start(col[:, :], cols_in).then_inc(params_loaded, 16)
            sp.dma_start(con[:, :], const_in[:, 0:RESIDENT]).then_inc(params_loaded, 16)
            sp.dma_start(raw[:, 0, :], stream[0]).then_inc(slot_loaded[0], 16)
            sp.dma_start(X[:, :, :], x_in).then_inc(x_loaded, 16)
            for n in range(1, NS):
                if n >= RING:
                    sp.wait_ge(unit_consumed, n - RING + 1)
                sp.dma_start(raw[:, n % RING, :], stream[n]).then_inc(slot_loaded[n % RING], 16)
                if n == WHERE[MLP1 + RING]:
                    sp.wait_ge(acts_lo, SET[5])
                    sp.dma_start(C[:, :, :], ctx_in).then_inc(ctx_loaded, 16)
                if n == RING:
                    sp.dma_start(WS[:, :, :], ws_in).then_inc(params_loaded, 16)
                    sp.dma_start(BS[:, :, :], bs_in).then_inc(params_loaded, 16)
                    sp.dma_start(alibi, const_in[:, CONST["alibi"]:CONST["window"]])\
                        .then_inc(params_loaded, 16)
                if n == WHERE[MIX_B + 2]:
                    sp.wait_ge(g_lo, 8)
                    sp.dma_start(SM[:, :, :].rearrange("p a b -> p (a b)"),
                                 const_in[:, CONST["window"]:CONST["cos"]]).then_inc(tables_loaded, 16)
                    sp.dma_start(WS[:, 0:4, :].rearrange("p a b -> p (a b)"),
                                 const_in[:, CONST["cos"]:NCONST]).then_inc(tables_loaded, 16)
            sp.wait_ge(h_final, 24)
            sp.dma_start(out, H[:, :, :]).then_inc(out_stored, 16)
            sp.wait_ge(out_stored, 16)

        @block.scalar
        def _(act):
            A = nc.scalar.activation

            def split_hi(w):
                n = WHERE[w]
                act.wait_ge(slot_loaded[n % RING], 16 * (n // RING + 1))
                if w >= SPLITS:
                    act.wait_ge(unit_done, w - SPLITS + 1)
                A(w_hi[:, w % SPLITS, :, :].rearrange("p k c -> p (k c)"), raw[:, n % RING, :],
                  ACT.Copy).then_inc(weight_hi, 1)

            def squares(n, src, dst, ready):
                for k in range(KT):
                    ready(k)
                    A(dst[:, k, :], src[:, k, :], ACT.Square).then_inc(sq_ready, 1)

            def rstd(n):
                act.wait_ge(var_prep, 2 * (n + 1))
                A(RSTD[:, :], VAR[:, :], ACT.Sqrt).then_inc(rstd_ready, 1)

            def biased_hi(n, s, bias):
                for k in range(KT):
                    act.wait_ge(h_scaled, 8 * n + k + 1)
                    A(XH[:, k, 0:T], H[:, k, :], ACT.Identity, bias=bias(k)).then_inc(acts_hi, 1)

            def rms(n, s, bias, updates):
                def ready(k):
                    if updates:
                        act.wait_ge(x_updated, updates + k + 1)
                squares(n, X, H, ready)
                rstd(n)
                biased_hi(n, s, bias)

            def drain(w):
                u = UNITS[w]
                kind = u[0]
                if kind in ("conv_a", "a_u"):
                    return
                act.wait_ge(unit_done, w + 1)
                e = EV[:, w % 2, :]
                if kind == "conv_g":
                    j = u[1]
                    for i in range(2):
                        if j >= 1:
                            act.wait_ge(drained["dve"], DRAINED[w - 2][1])
                        A(EV[:, j % 2, i * T:(i + 1) * T], tiles(w, T)[:, i, :], ACT.Tanh,
                          bias=half_b[:, 2 * j + i:2 * j + i + 1], scale=0.5).then_inc(gate_tanh, 1)
                elif kind == "conv_out":
                    j = u[1]
                    act.wait_ge(mod_step, MOD_DONE[2])
                    if j < 2:
                        act.wait_ge(drained["dve"], DRAINED[CONV_OUT - 1][1])
                    for i in range(2):
                        k = 2 * j + i
                        if j >= 2:
                            act.wait_ge(x_updated, XU_CONV + 2 * (j - 1))
                        ins = A(e[:, i * T:(i + 1) * T], tiles(w, T)[:, i, :], ACT.Identity,
                                bias=gate_b[:, k:k + 1], scale=mod1[:, 2, k:k + 1])
                        ins.then_inc(y_ready, 1)
                elif kind == "w1":
                    f = f_index(w)
                    if f >= 2:
                        act.wait_ge(f_lo, f - 1)
                    A(e.rearrange("p (i t) -> p i t", i=2), tiles(w, T), ACT.Relu)\
                        .then_inc(drained["act"], 1)
                    act.wait_ge(drained["act"], DRAINED[w][1])
                    A(F_hi[:, u[2] % 2, 2 * u[3]:2 * u[3] + 2, :],
                      e.rearrange("p (i t) -> p i t", i=2), ACT.Square).then_inc(f_hi, 1)
                elif kind in ("q", "k"):
                    j = u[1]
                    dst, sq = (Q, H) if kind == "q" else (K1, C)
                    A(dst[:, 2 * j:2 * j + 2, :], tiles(w, T), ACT.Copy)
                    A(sq[:, 2 * j:2 * j + 2, :], tiles(w, T), ACT.Square).then_inc(drained["act"], 1)
                elif kind == "v":
                    j = u[1]
                    A(V1[:, :, UC * j:UC * (j + 1)],
                      pair(w)[:, 0:2 * UC].rearrange("p (t c) -> p t c", t=2), ACT.Copy)\
                        .then_inc(drained["act"], 1)
                    for b in (2 * j, 2 * j + 1):
                        act.wait_ge(qk_prep, 2 * (b + 1))
                        A(QV[:, :], QV[:, :], ACT.Sqrt).then_inc(qk_rstd, 1)
                elif kind == "a_v":
                    j = u[1]
                    A(VA[:, :, UC * j:UC * (j + 1)], pair(w).rearrange("p (t c) -> p t c", t=4),
                      ACT.Gelu_apprx_tanh).then_inc(drained["act"], 1)
                    if j == 7:
                        act.wait_ge(v_prep, 6)
                        A(vr[:, :], vr[:, :], ACT.Sqrt).then_inc(v_rstd, 1)
                elif kind == "a_z":
                    j = u[1]
                    if j >= 1:
                        act.wait_ge(g_lo, j)
                    A(GU, pair(w - 1), ACT.Gelu_apprx_tanh).then_inc(g_act, 1)
                    A(TZ, pair(w), ACT.Tanh, scale=0.5).then_inc(g_act, 1)
                    act.wait_ge(g_dve, 7 * (j + 1))
                    if j == 4:
                        act.wait_ge(unit_done, MIX_A + 20)
                    A(G_hi[:, 2 * (j % 4):2 * (j % 4) + 2, :], GU.rearrange("p (i t) -> p i t", i=2),
                      ACT.Copy).then_inc(g_hi, 1)
                elif kind == "b_k":
                    A(K2[:, :, :], tiles(w, 2 * T), ACT.Copy).then_inc(drained["act"], 1)
                elif kind == "b_v":
                    A(V2[:, :, :], pair(w).rearrange("p (t c) -> p t c", t=4), ACT.Copy)\
                        .then_inc(drained["act"], 1)
                elif kind == "b_q":
                    j = u[1]
                    A(Q[:, 2 * j:2 * j + 2, :], tiles(w, T), ACT.Copy).then_inc(drained["act"], 1)
                elif kind == "b_z":
                    j = u[1]
                    if j >= 2:
                        act.wait_ge(drained["dve"], DRAINED[w - 2][1])
                    A(e.rearrange("p (i t) -> p i t", i=2), tiles(w, T), ACT.Tanh, scale=0.5)\
                        .then_inc(z_tanh, 1)

            def attention_1():
                for i in range(HEADS + 3):
                    if i < HEADS:
                        slope = 2.0 ** (-8.0 * (i + 1) / HEADS)
                        b = i % 3
                        act.wait_ge(max_ready, 3 * (i + 1))
                        for t, (a, c) in enumerate(((0, P), (P, 3 * P))):
                            A(S1[:, b, a:c], S1[:, b, a:c], ACT.Exp, bias=sm[:, b, 2 + t:3 + t],
                              scale=slope, accum_out=sm[:, b, 4 + t:5 + t]).then_inc(exp_done, 1)
                    if 2 <= i < HEADS + 2:
                        h = i - 2
                        act.wait_ge(p_turned, h + 1)
                        A(PT1[:, h % 2, :], prod[:, 1, 512 * (h % 2):512 * (h % 2) + 3 * P],
                          ACT.Copy).then_inc(pt_copied, 1)
                    if i >= 4 and i % 2 == 0:
                        k = (i - 4) // 2
                        act.wait_ge(head_out, 2 * (k + 1))
                        A(XH[:, k, 0:T], prod[:, 2, 512 * (k % 2):512 * (k % 2) + T], ACT.Copy)\
                            .then_inc(acts_hi, 1)

            def attention_2():
                NI = 2 * HEADS
                for i in range(NI + 4):
                    if i < NI:
                        b = i % 3
                        act.wait_ge(max_ready, 3 * HEADS + 2 * (i + 1))
                        A(S2[:, b, :], S2[:, b, :], ACT.Exp, bias=sm[:, b, 2:3],
                          accum_out=sm[:, b, 4:5]).then_inc(exp_done, 1)
                        A(sm[:, b, 5:6], cl("sink", head_of(i)), ACT.Exp, bias=sm[:, b, 2:3])\
                            .then_inc(exp_done, 1)
                    if 2 <= i < NI + 2:
                        h = i - 2
                        act.wait_ge(p_turned, HEADS + h + 1)
                        A(PT2[:, h % 2, :], prod[:, 1, 512 * (h % 2):512 * (h % 2) + 512], ACT.Copy)\
                            .then_inc(pt_copied, 1)
                    if i >= 7 and (i - 7) % 4 == 0:
                        k = (i - 7) // 4
                        act.wait_ge(o_gated, k + 1)
                        A(XH[:, k, 0:T], H[:, k, :], ACT.Copy).then_inc(acts_hi, 1)

            def boundary(n):
                if n == 0:
                    rms(0, 0, lambda k: mod1[:, 0, k:k + 1], 0)
                elif n == CONV_OUT:
                    squares(1, CV, H, lambda k: act.wait_ge(centred, k + 1))
                    rstd(1)
                    for k in range(KT):
                        act.wait_ge(h_scaled, 8 + k + 1)
                        A(TS[:, k, :], H[:, k, :], ACT.Tanh, bias=half_b[:, 8 + k:9 + k], scale=0.5)\
                            .then_inc(silu_tanh, 1)
                    for k in range(KT):
                        act.wait_ge(silu_step, 8 + k + 1)
                        A(XH[:, k, 0:T], TS[:, k, :], ACT.Copy).then_inc(acts_hi, 1)
                elif n == MLP0:
                    rms_late(2, 2, 3, XU_CONV)
                elif n == QKV:
                    rms_late(3, 3, 6, XU_MLP0 + 24)
                elif n == WO:
                    attention_1()
                elif n == MLP1:
                    rms_late(4, 5, 9, XU_WO)
                elif n == MIX_A:
                    act.wait_ge(row_sums, 1)
                    act.wait_ge(f_lo, 32)
                    act.wait_ge(mod_step, MOD_DONE[14])
                    A(RSB, misc[:, :, :].rearrange("p a (b c) -> p (a b) c", c=P), ACT.Copy)\
                        .then_inc(row_copied, 1)
                    act.wait_ge(unit_done, MIX_A)
                    for k in range(KT):
                        act.wait_ge(x_updated, XU_MLP1 + 24 + k + 1)
                        A(XH[:, k, 0:T], X[:, k, :], ACT.Identity, bias=mod2[:, 0, 0, k:k + 1],
                          scale=mod2[:, 1, 0, k:k + 1]).then_inc(acts_hi, 1)
                    act.wait_ge(ctx_loaded, 16)
                    for k in range(KT):
                        A(XH[:, k, T:2 * T], C[:, k, :], ACT.Identity, bias=mod2[:, 0, 1, k:k + 1],
                          scale=mod2[:, 1, 1, k:k + 1]).then_inc(acts_hi, 1)
                    act.wait_ge(acts_lo, SET[7])
                    A(X[:, :, :], X[:, :, :], ACT.Copy, scale=ALPHA).then_inc(x_scaled, 1)
                    A(C[:, :, :], C[:, :, :], ACT.Copy, scale=ALPHA).then_inc(x_scaled, 1)
                elif n == MIX_B:
                    for m, (src, dst) in enumerate(((X, H), (C, H2))):
                        squares(5 + m, src, dst, lambda k: act.wait_ge(centred, 8 + 8 * m + k + 1))
                        rstd(5 + m)
                        for k in range(KT):
                            act.wait_ge(h_final, 8 * m + k + 1)
                            A(XH[:, k, m * T:(m + 1) * T], src[:, k, :], ACT.Identity,
                              bias=mod2[:, 3, m, k:k + 1], scale=mod2[:, 4, m, k:k + 1])\
                                .then_inc(acts_hi, 1)
                    act.wait_ge(acts_lo, SET[8])
                    A(X[:, :, :], X[:, :, :], ACT.Copy, scale=ALPHA).then_inc(x_scaled, 1)
                elif n == B_OUT:
                    attention_2()

            def rms_late(n, s, shift, updates):
                act.wait_ge(unit_done, {2: MLP0, 3: QKV, 4: MLP1}[n])
                squares(n, X, H, lambda k: act.wait_ge(x_updated, updates + k + 1))
                rstd(n)
                biased_hi(n, s, lambda k: mod1[:, shift, k:k + 1])

            act.wait_ge(params_loaded, 32)
            A(cond_t[:, :], col[:, COLS["c"]:COLS["c"] + 24], ACT.Tanh, scale=0.5)\
                .then_inc(cond_tanh, 1)
            A(half_b[:, 0:8], cl("conv_b_in", 8, 8), ACT.Copy, scale=0.5).then_inc(half_ready, 1)
            A(half_b[:, 8:16], cl("conv_ln_b", 0, 8), ACT.Copy, scale=0.5).then_inc(half_ready, 1)
            act.wait_ge(half_ready, 2)
            act.wait_ge(x_loaded, 16)
            for s in range(NW + 2):
                if s < NW:
                    split_hi(s)
                if s >= 2:
                    drain(s - 2)
                if s - 1 in FIRST_OF_SET:
                    boundary(s - 1)
            squares(7, X, H, lambda k: act.wait_ge(centred, 24 + k + 1))
            rstd(7)

        @block.vector
        def _(dve):
            vec = nc.vector
            stt, ts, tt = vec.scalar_tensor_tensor, vec.tensor_scalar, vec.tensor_tensor
            count = {"acc": 0, "x": 0, "mod": 0}
            acc_last = {}

            def split_lo(w):
                n = WHERE[w]
                dve.wait_ge(weight_hi, w + 1)
                tt(w_lo[:, w % SPLITS, :, :].rearrange("p k c -> p (k c)"), raw[:, n % RING, :],
                   w_hi[:, w % SPLITS, :, :].rearrange("p k c -> p (k c)").bitcast(F32),
                   ALU.subtract).then_inc(unit_consumed, 1)

            def accumulate(n):
                _, vi, quarter = STREAM[n]
                block_no = VECTORS[vi][0]
                dve.wait_ge(slot_loaded[n % RING], 16 * (n // RING + 1))
                sums = [(vi % 2, 0)] if block_no == 1 else [(0, 8), (1, 16)]
                if quarter == 0 and vi >= 2:
                    dve.wait_ge(acc_reduced, vi - 1 if block_no == 1 else vi)
                for i in range(2):
                    k = 2 * quarter + i
                    for b, c0 in sums:
                        src = raw[:, n % RING, i * D:(i + 1) * D]
                        c = cond[:, c0 + k:c0 + k + 1]
                        if k == 0:
                            ins = ts(acc[:, b, :], src, c, None, ALU.mult)
                        else:
                            s, v = acc_last[b]
                            dve.wait_ge(s, v)
                            ins = stt(out=acc[:, b, :], in0=src, scalar=c, in1=acc[:, b, :],
                                      op0=ALU.mult, op1=ALU.add)
                        if i == 1 and b == sums[-1][0]:
                            ins.then_inc(unit_consumed, 1)
                            acc_last[b] = (unit_consumed, n + 1)
                        else:
                            ins.then_inc(acc_step, 1)
                            count["acc"] += 1
                            acc_last[b] = (acc_step, count["acc"])

            def step(ins):
                ins.then_inc(mod_step, 1)
                count["mod"] += 1

            def finish_vector(vi):
                block_no, layer, part = VECTORS[vi]
                dve.wait_ge(acc_reduced, vi + 1)
                if block_no == 1:
                    got = misc[:, 1, 0:8]
                    m = mod1[:, 6 * layer + part, :]
                    b = cl("ada_b", 8 * (6 * layer + part), 8)
                    if part in (1, 4):
                        step(stt(out=m, in0=got, scalar=1.0, in1=b, op0=ALU.add, op1=ALU.add))
                        dve.wait_ge(mod_step, count["mod"])
                        step(tt(m, m, cl("mix_g" if part == 1 else "mlp_g", 8 * layer, 8), ALU.mult))
                    else:
                        step(tt(m, got, b, ALU.add))
                    if layer == 0 and part == 2:
                        dve.wait_ge(mod_step, count["mod"])
                        step(tt(gate_b[:, :], m, cl("conv_b_out", 0, 8), ALU.mult))
                else:
                    for i in range(2):
                        got = misc[:, 1, 8 * i:8 * i + 8]
                        b = cl("ada_b_2", 8 * (3 * layer + part), 8)
                        step(stt(out=mod2[:, 3 * layer + part, i, :], in0=got,
                                 scalar=1.0 if part == 1 else 0.0, in1=b, op0=ALU.add, op1=ALU.add))
                assert count["mod"] == MOD_DONE[vi]

            def update_x(ins_of):
                if count["x"] >= 1:
                    dve.wait_ge(x_updated, max(1, count["x"] - 7))
                ins_of().then_inc(x_updated, 1)
                count["x"] += 1

            def centre(n, src):
                m = LN_INDEX[n]
                dve.wait_ge(stat_done, STAT_DONE[n] - 1)
                ts(MU[:, :], misc[:, 0, T:2 * T], 1.0 / D, None, ALU.mult).then_inc(mean_ready, 1)
                dve.wait_ge(mean_ready, m + 1)
                for k in range(KT):
                    tt(src[:, k, :], src[:, k, :], MU[:, :], ALU.subtract).then_inc(centred, 1)

            def scale_rows(n, src, dst, gain, eps):
                dve.wait_ge(stat_done, STAT_DONE[n])
                ts(VAR[:, :], misc[:, 0, 0:T], 1.0 / D, eps, ALU.mult, ALU.add).then_inc(var_prep, 1)
                dve.wait_ge(var_prep, 2 * n + 1)
                vec.reciprocal(VAR[:, :], VAR[:, :]).then_inc(var_prep, 1)
                dve.wait_ge(rstd_ready, n + 1)
                for k in range(KT):
                    stt(out=dst[:, k, :], in0=src[:, k, :], scalar=gain(k), in1=RSTD[:, :],
                        op0=ALU.mult, op1=ALU.mult).then_inc(h_scaled, 1)

            def biased_lo(s, bias):
                for k in range(KT):
                    dve.wait_ge(acts_hi, SET[s] + k + 1)
                    stt(out=XL[:, k, 0:T], in0=H[:, k, :], scalar=bias(k),
                        in1=XH[:, k, 0:T].bitcast(F32), op0=ALU.add, op1=ALU.subtract)\
                        .then_inc(acts_lo, 1)

            def rms(n, s, scale, shift):
                scale_rows(n, X, H, lambda k: mod1[:, scale, k:k + 1], EPS)
                biased_lo(s, lambda k: mod1[:, shift, k:k + 1])

            def conv_pair(j):
                for tap in range(TAPS):
                    for i in range(2):
                        k = 2 * j + i
                        d = cl("conv_dw", 8 * tap + k)
                        if tap == 0:
                            ins = ts(CV[:, k, :], U[:, k, 0:T], d, cl("conv_dw_b", k),
                                     ALU.mult, ALU.add)
                        else:
                            dve.wait_ge(conv_step, 62 * j + 2 * (tap - 1) + i + 1)
                            ins = stt(out=CV[:, k, :], in0=U[:, k, tap:tap + T], scalar=d,
                                      in1=CV[:, k, :], op0=ALU.mult, op1=ALU.add)
                        ins.then_inc(conv_step, 1)

            def drain(w):
                u = UNITS[w]
                kind = u[0]
                if kind in ("conv_a", "a_u"):
                    return
                e = EV[:, w % 2, :]
                ei = e.rearrange("p (i t) -> p i t", i=2)
                if kind == "conv_g":
                    j = u[1]
                    g = EV[:, j % 2, :]
                    dve.wait_ge(gate_tanh, 2 * (j + 1))
                    ts(g, g, 0.5, 0.5, ALU.mult, ALU.add).then_inc(gate_half, 1)
                    dve.wait_ge(gate_half, j + 1)
                    for i in range(2):
                        k = 2 * j + i
                        ins = stt(out=U[:, k, PAD:PAD + T], in0=tiles(w - 1, T)[:, i, :],
                                  scalar=cl("conv_b_in", k), in1=g[:, i * T:(i + 1) * T],
                                  op0=ALU.add, op1=ALU.mult)
                    ins.then_inc(drained["dve"], 1)
                    dve.wait_ge(drained["dve"], DRAINED[w][1])
                    conv_pair(j)
                elif kind == "conv_out":
                    j = u[1]
                    for i in range(2):
                        k = 2 * j + i
                        dve.wait_ge(y_ready, k + 1)
                        update_x(lambda: tt(X[:, k, :], X[:, k, :], e[:, i * T:(i + 1) * T],
                                                  ALU.add))
                elif kind == "w1":
                    f = f_index(w)
                    dve.wait_ge(f_hi, f + 1)
                    tt(e, e, e, ALU.mult).then_inc(f_sq, 1)
                    dve.wait_ge(f_sq, f + 1)
                    fl = F_lo[:, u[2] % 2, 2 * u[3]:2 * u[3] + 2, :]
                    fh = F_hi[:, u[2] % 2, 2 * u[3]:2 * u[3] + 2, :]
                    tt(fl, ei, fh.bitcast(F32), ALU.subtract).then_inc(f_lo, 1)
                elif kind in ("w2", "wo", "b_out"):
                    dve.wait_ge(unit_done, w + 1)
                    j = u[-1]
                    for i in range(2):
                        k = 2 * j + i
                        if kind == "w2":
                            g = mod1[:, 6 * u[1] + 5, k:k + 1]
                        elif kind == "wo":
                            g = mod1[:, 8, k:k + 1]
                        else:
                            g = mod2[:, 5, 0, k:k + 1]
                            dve.wait_ge(x_scaled, 3)
                        update_x(lambda: stt(out=X[:, k, :], in0=tiles(w, T)[:, i, :],
                                                   scalar=g, in1=X[:, k, :], op0=ALU.mult,
                                                   op1=ALU.add))
                elif kind == "v":
                    for b in (2 * u[1], 2 * u[1] + 1):
                        dst = (Q if b < 4 else K1)[:, 2 * (b % 4):2 * (b % 4) + 2, :]
                        dve.wait_ge(qk_sum, b + 1)
                        ts(QV[:, :], misc[:, 0, :], 1.0 / DH, EPS, ALU.mult, ALU.add)\
                            .then_inc(qk_prep, 1)
                        dve.wait_ge(qk_prep, 2 * b + 1)
                        vec.reciprocal(QV[:, :], QV[:, :]).then_inc(qk_prep, 1)
                        dve.wait_ge(qk_rstd, b + 1)
                        stt(out=dst, in0=dst, scalar=cl("qn_g" if b < 4 else "kn_g"),
                            in1=QV[:, :].rearrange("p (i t) -> p i t", i=2), op0=ALU.mult,
                            op1=ALU.mult).then_inc(qk_final, 1)
                        dve.wait_ge(qk_final, b + 1)
                elif kind == "a_v":
                    j = u[1]
                    dve.wait_ge(drained["act"], DRAINED[w][1])
                    for t in range(4):
                        vec.bn_stats(bst[:, t, j, :], VA[:, t, UC * j:UC * (j + 1)])\
                            .then_inc(v_stats, 1)
                    if j == 7:
                        norm_values()
                elif kind == "a_z":
                    mix_pair(u[1], w)
                elif kind == "a_out":
                    half, j = u[1], u[2]
                    dve.wait_ge(unit_done, w + 1)
                    dve.wait_ge(x_scaled, 2)
                    for m, buf in enumerate((X, C)):
                        for i in range(2):
                            k = 2 * j + i
                            update_x(lambda: stt(
                                out=buf[:, k, :], in0=tiles(w, 2 * T)[:, i, m * T:(m + 1) * T],
                                scalar=mod2[:, 2, m, k:k + 1], in1=buf[:, k, :],
                                op0=ALU.mult, op1=ALU.add))
                elif kind == "b_z":
                    j = u[1]
                    dve.wait_ge(z_tanh, j + 1)
                    ts(e, e, 0.5, 0.5, ALU.mult, ALU.add).then_inc(z_half, 1)
                    dve.wait_ge(z_half, j + 1)
                    tt(SZ[:, 2 * j:2 * j + 2, :], tiles(w, T), ei, ALU.mult)\
                        .then_inc(drained["dve"], 1)
                    rope(0, Q[:, 2 * j:2 * j + 2, :], j, j if j == 0 else j + 1)
                    if j == 0:
                        rope(1, K2[:, :, 0:T], 0, 1)

            def rope(bank, dst, j, index):
                dve.wait_ge(tables_loaded, 32)
                dve.wait_ge(turned, index + 1)
                r = HT[:, 0:512].rearrange("p (i t) -> p i t", i=2)
                s2 = sin_t.unsqueeze(1).broadcast_to([P, 2, T])
                c2 = cos_t.unsqueeze(1).broadcast_to([P, 2, T])
                tt(r, misc[:, bank, :].rearrange("p (i t) -> p i t", i=2), s2, ALU.mult)\
                    .then_inc(roped, 1)
                tt(dst, dst, c2, ALU.mult).then_inc(roped, 1)
                dve.wait_ge(roped, 3 * index + 2)
                tt(dst, dst, r, ALU.add).then_inc(roped, 1)
                dve.wait_ge(roped, 3 * index + 3)

            def norm_values():
                dve.wait_ge(v_stats, 32)
                for t in range(4):
                    vec.bn_aggr(mv[:, t, :], bst[:, t, :, :]).then_inc(v_prep, 1)
                dve.wait_ge(v_prep, 4)
                ts(vr[:, :], mv[:, :, 1], LN_EPS, None, ALU.add).then_inc(v_prep, 1)
                dve.wait_ge(v_prep, 5)
                vec.reciprocal(vr[:, :], vr[:, :]).then_inc(v_prep, 1)
                dve.wait_ge(v_rstd, 1)
                for t in range(4):
                    ts(VA[:, t, :], VA[:, t, :], mv[:, t, 0:1], vr[:, t:t + 1], ALU.subtract,
                       ALU.mult).then_inc(v_normed, 1)

            def mix_pair(j, w):
                n = 7 * j
                for i in range(2):
                    stt(out=RR[:, i, :], in0=RSB[:, j, :], scalar=cl("a_ln_b", 2 * j + i),
                        in1=BS[:, j, :], op0=ALU.mult, op1=ALU.add).then_inc(g_dve, 1)
                dve.wait_ge(g_dve, n + 2)
                dve.wait_ge(mixed, j + 1)
                for i in range(2):
                    stt(out=SM[:, i, :].rearrange("p (c q) -> p c q", c=4),
                        in0=misc[:, i, :].rearrange("p (c q) -> p c q", c=4),
                        scalar=cl("a_ln_g", 2 * j + i),
                        in1=RR[:, i, :].unsqueeze(1).broadcast_to([P, 4, P]),
                        op0=ALU.mult, op1=ALU.add).then_inc(g_dve, 1)
                dve.wait_ge(g_dve, n + 4)
                dve.wait_ge(g_act, 2 * (j + 1))
                tt(GU, GU, SM[:, :, :].rearrange("p i t -> p (i t)"), ALU.mult).then_inc(g_dve, 1)
                ts(TZ, TZ, 0.5, 0.5, ALU.mult, ALU.add).then_inc(g_dve, 1)
                dve.wait_ge(g_dve, n + 6)
                tt(TZ, pair(w), TZ, ALU.mult).then_inc(drained["dve"], 1)
                dve.wait_ge(drained["dve"], DRAINED[w][1])
                tt(GU, GU, TZ, ALU.mult).then_inc(g_dve, 1)
                dve.wait_ge(g_dve, n + 7)
                dve.wait_ge(g_hi, j + 1)
                k = 2 * (j % 4)
                tt(G_lo[:, k:k + 2, :], GU.rearrange("p (i t) -> p i t", i=2),
                   G_hi[:, k:k + 2, :].bitcast(F32), ALU.subtract).then_inc(g_lo, 1)

            def attention_1():
                dve.wait_ge(params_loaded, 80)
                for i in range(HEADS + 4):
                    if i < HEADS:
                        slope = 2.0 ** (-8.0 * (i + 1) / HEADS)
                        b = i % 3
                        dve.wait_ge(scored, i + 1)
                        if i >= 3:
                            dve.wait_ge(p_turned, i - 2)
                        stt(out=S1[:, b, :], in0=prod[:, 0, 512 * (i % 2):512 * (i % 2) + 3 * P],
                            scalar=SCALE / slope, in1=alibi, op0=ALU.mult, op1=ALU.add)\
                            .then_inc(z_ready, 1)
                        dve.wait_ge(z_ready, i + 1)
                        vec.reduce_max(sm[:, b, 0:1], S1[:, b, 0:P], AX).then_inc(max_ready, 1)
                        vec.reduce_max(sm[:, b, 1:2], S1[:, b, P:3 * P], AX).then_inc(max_ready, 1)
                        dve.wait_ge(max_ready, 3 * i + 2)
                        ts(sm[:, b, 2:4], sm[:, b, 0:2], -slope, None, ALU.mult)\
                            .then_inc(max_ready, 1)
                    if 1 <= i <= HEADS:
                        h = i - 1
                        b = h % 3
                        dve.wait_ge(exp_done, 2 * (h + 1))
                        vec.reciprocal(sm[:, b, 6:8], sm[:, b, 4:6]).then_inc(p_ready, 1)
                        dve.wait_ge(p_ready, 3 * h + 1)
                        for t, (a, c) in enumerate(((0, P), (P, 3 * P))):
                            ts(S1[:, b, a:c], S1[:, b, a:c], sm[:, b, 6 + t:7 + t], None, ALU.mult)\
                                .then_inc(p_ready, 1)
                    if i >= 5 and i % 2 == 1:
                        k = (i - 5) // 2
                        dve.wait_ge(acts_hi, SET[4] + k + 1)
                        tt(XL[:, k, 0:T], prod[:, 2, 512 * (k % 2):512 * (k % 2) + T],
                           XH[:, k, 0:T].bitcast(F32), ALU.subtract).then_inc(acts_lo, 1)

            def attention_2():
                NI = 2 * HEADS
                for i in range(NI + 5):
                    if i < NI:
                        b = i % 3
                        dve.wait_ge(scored, HEADS + i + 1)
                        if i >= 3:
                            dve.wait_ge(p_turned, HEADS + i - 2)
                        vec.tensor_tensor_reduce(S2[:, b, :], prod[:, 0, 512 * (i % 2):512 * (i % 2) + 512],
                                                 window[:, i % 2, :], SCALE, cl("sink", head_of(i)),
                                                 ALU.add, ALU.max, sm[:, b, 0:1]).then_inc(max_ready, 1)
                        n = 3 * HEADS + 2 * i
                        dve.wait_ge(max_ready, n + 1)
                        ts(sm[:, b, 2:3], sm[:, b, 0:1], -1.0, None, ALU.mult)\
                            .then_inc(max_ready, 1)
                    if 1 <= i <= NI:
                        h = i - 1
                        b = h % 3
                        n = 3 * HEADS + 3 * h
                        dve.wait_ge(exp_done, 2 * HEADS + 2 * (h + 1))
                        tt(sm[:, b, 6:7], sm[:, b, 4:5], sm[:, b, 5:6], ALU.add)\
                            .then_inc(p_ready, 1)
                        dve.wait_ge(p_ready, n + 1)
                        vec.reciprocal(sm[:, b, 7:8], sm[:, b, 6:7]).then_inc(p_ready, 1)
                        dve.wait_ge(p_ready, n + 2)
                        ts(S2[:, b, :], S2[:, b, :], sm[:, b, 7:8], None, ALU.mult)\
                            .then_inc(p_ready, 1)
                    if i >= 7 and (i - 7) % 4 == 0 and (i - 7) // 4 < KT:
                        k = (i - 7) // 4
                        dve.wait_ge(head_out, HEADS + 4 * (k + 1))
                        tt(H[:, k, :], prod[:, 2, 512 * (k % 2):512 * (k % 2) + T], SZ[:, k, :],
                           ALU.mult).then_inc(o_gated, 1)
                    if i >= 8 and (i - 8) % 4 == 0:
                        k = (i - 8) // 4
                        dve.wait_ge(acts_hi, SET[8] + k + 1)
                        tt(XL[:, k, 0:T], H[:, k, :], XH[:, k, 0:T].bitcast(F32), ALU.subtract)\
                            .then_inc(acts_lo, 1)

            def boundary(n):
                if n == 0:
                    rms(0, 0, 1, 0)
                elif n == CONV_OUT:
                    centre(1, CV)
                    scale_rows(1, CV, H, lambda k: cl("conv_ln_g", k), EPS)
                    for k in range(KT):
                        dve.wait_ge(silu_tanh, k + 1)
                        ts(TS[:, k, :], TS[:, k, :], 0.5, 0.5, ALU.mult, ALU.add)\
                            .then_inc(silu_step, 1)
                    for k in range(KT):
                        dve.wait_ge(silu_step, 8 if k == 0 else 8 + k)
                        stt(out=TS[:, k, :], in0=H[:, k, :], scalar=cl("conv_ln_b", k),
                            in1=TS[:, k, :], op0=ALU.add, op1=ALU.mult).then_inc(silu_step, 1)
                    for k in range(KT):
                        dve.wait_ge(acts_hi, SET[1] + k + 1)
                        tt(XL[:, k, 0:T], TS[:, k, :], XH[:, k, 0:T].bitcast(F32), ALU.subtract)\
                            .then_inc(acts_lo, 1)
                elif n == MLP0:
                    rms(2, 2, 4, 3)
                elif n == QKV:
                    rms(3, 3, 7, 6)
                elif n == WO:
                    attention_1()
                elif n == MLP1:
                    rms(4, 5, 10, 9)
                elif n == MIX_A:
                    for m, buf in enumerate((X, C)):
                        if m:
                            dve.wait_ge(acts_lo, SET[6] + 8)
                        for k in range(KT):
                            if m == 0 and k == 0:
                                dve.wait_ge(x_updated, XU_A)
                            if m == 1 and k == 0:
                                dve.wait_ge(ctx_loaded, 16)
                            ts(H[:, k, :], buf[:, k, :], mod2[:, 1, m, k:k + 1],
                               mod2[:, 0, m, k:k + 1], ALU.mult, ALU.add).then_inc(h_scaled, 1)
                        for k in range(KT):
                            dve.wait_ge(h_scaled, 40 + 8 * m + k + 1)
                            dve.wait_ge(acts_hi, SET[6] + 8 * m + k + 1)
                            tt(XL[:, k, m * T:(m + 1) * T], H[:, k, :],
                               XH[:, k, m * T:(m + 1) * T].bitcast(F32), ALU.subtract)\
                                .then_inc(acts_lo, 1)
                elif n == MIX_B:
                    for m, (src, dst) in enumerate(((X, H), (C, H2))):
                        centre(5 + m, src)
                        base = 56 + 16 * m
                        scale_rows(5 + m, src, dst, lambda k: cl("ln_g_2", k), LN_EPS)
                        for k in range(KT):
                            dve.wait_ge(h_scaled, base + k + 1)
                            ts(src[:, k, :], dst[:, k, :], cl("ln_b_2", k), None, ALU.add)\
                                .then_inc(h_final, 1)
                        for k in range(KT):
                            dve.wait_ge(h_final, 8 * m + k + 1)
                            ts(dst[:, k, :], src[:, k, :], mod2[:, 4, m, k:k + 1],
                               mod2[:, 3, m, k:k + 1], ALU.mult, ALU.add).then_inc(h_scaled, 1)
                        for k in range(KT):
                            dve.wait_ge(h_scaled, base + 8 + k + 1)
                            dve.wait_ge(acts_hi, SET[7] + 8 * m + k + 1)
                            tt(XL[:, k, m * T:(m + 1) * T], dst[:, k, :],
                               XH[:, k, m * T:(m + 1) * T].bitcast(F32), ALU.subtract)\
                                .then_inc(acts_lo, 1)
                elif n == B_OUT:
                    attention_2()

            vec.memset(U[:, :, 0:PAD], 0.0).then_inc(padded, 1)
            dve.wait_ge(padded, 1)
            dve.wait_ge(params_loaded, 32)
            dve.wait_ge(cond_tanh, 1)
            ts(cond_t[:, :], cond_t[:, :], 0.5, 0.5, ALU.mult, ALU.add).then_inc(cond_ready, 1)
            dve.wait_ge(cond_ready, 1)
            tt(cond[:, :], cond_t[:, :], col[:, COLS["c"]:COLS["c"] + 24], ALU.mult)\
                .then_inc(cond_ready, 1)
            dve.wait_ge(cond_ready, 2)
            at = 0
            for s in range(NW + 2):
                if s < NW:
                    while at < WHERE[s]:
                        accumulate(at)
                        at += 1
                        if at in (4, 8):
                            finish_vector(at // 4 - 1)
                    split_lo(s)
                    at += 1
                if s >= 2:
                    drain(s - 2)
                    for vi in REDUCE_AFTER.get(s - 2, []):
                        finish_vector(vi)
                if s - 1 in FIRST_OF_SET:
                    dve.wait_ge(mod_step, max(1, count["mod"]))
                    if s > 2:
                        dve.wait_ge(unit_done, s - 1)
                    boundary(s - 1)
            centre(7, X)
            scale_rows(7, X, H, lambda k: cl("ln_g_2", 8 + k), LN_EPS)
            for k in range(KT):
                dve.wait_ge(h_scaled, 88 + k + 1)
                ts(H[:, k, :], H[:, k, :], cl("ln_b_2", 8 + k), None, ALU.add)\
                    .then_inc(h_final, 1)

        @block.tensor
        def _(pe):
            mm = nc.tensor.matmul

            def reduce_vector(vi):
                last = max(n for n, s in enumerate(STREAM) if s[0] == "mod" and s[1] == vi)
                pe.wait_ge(unit_consumed, last + 1)
                if vi:
                    pe.wait_ge(mod_step, MOD_DONE[vi - 1])
                if vi == 15:
                    pe.wait_ge(row_copied, 1)
                if mixed_now[0]:
                    pe.wait_ge(g_lo, mixed_now[0])
                sums = [vi % 2] if VECTORS[vi][0] == 1 else [0, 1]
                for i, b in enumerate(sums):
                    for k in range(KT):
                        ins = mm(misc[:, 1, 8 * i + k:8 * i + k + 1], acc[:, b, P * k:P * (k + 1)],
                                 ones[:, 0:1], start=True, stop=True)
                ins.then_inc(acc_reduced, 1)

            def sum_tiles(src, c, ready):
                for k in range(KT):
                    ready(k)
                    ins = mm(misc[:, 0, c:c + T], ones, src[:, k, :], start=(k == 0),
                             stop=(k == KT - 1))
                ins.then_inc(stat_done, 1)

            def sum_squares(n, src):
                sum_tiles(src, 0, lambda k: pe.wait_ge(sq_ready, 8 * n + k + 1))

            def three(out, lhs_hi, lhs_lo, rhs_hi, rhs_lo, start, stop):
                mm(out, lhs_hi, rhs_hi, start=start, stop=False)
                mm(out, lhs_hi, rhs_lo, start=False, stop=False)
                return mm(out, lhs_lo, rhs_hi, start=False, stop=stop)

            def unit(w):
                u = UNITS[w]
                kind = u[0]
                pe.wait_ge(unit_consumed, WHERE[w] + 1)
                if w >= PAIRS:
                    who, n = DRAINED[w - PAIRS]
                    pe.wait_ge(drained[who], n)
                wh, wl = w_hi[:, w % SPLITS], w_lo[:, w % SPLITS]
                s = FIRST_OF_SET.get(w)
                if w in (WO, B_OUT):
                    pe.wait_ge(acts_lo, SET[s + 1])

                def ready(k):
                    if s is not None:
                        wide = SET_SIZE[s] == 16
                        pe.wait_ge(acts_lo, SET[s] + (8 if wide else 0) + k + 1)

                if kind in ("v", "a_v", "b_v"):
                    nt = 2 if kind == "v" else 4
                    for t in range(nt):
                        for k in range(KT):
                            if t == 0:
                                ready(k)
                            ins = three(pair(w)[:, t * UC:(t + 1) * UC],
                                        XH[:, k, t * P:(t + 1) * P], XL[:, k, t * P:(t + 1) * P],
                                        wh[:, k, :], wl[:, k, :], k == 0, k == KT - 1)
                else:
                    if kind == "w2":
                        pe.wait_ge(f_lo, 16 * u[1] + 4 * (u[2] + 1))
                        hi, lo, nt = F_hi[:, u[2] % 2], F_lo[:, u[2] % 2], T
                    elif kind == "a_out":
                        pe.wait_ge(g_lo, 4 * (u[1] + 1))
                        hi, lo, nt = G_hi, G_lo, 2 * T
                    else:
                        nt = 2 * T if kind in ("a_u", "a_z", "b_k") else T
                        hi, lo = XH, XL
                    for i in range(2):
                        for k in range(KT):
                            if i == 0:
                                ready(k)
                            ins = three(tiles(w, nt)[:, i, :], wh[:, k, P * i:P * (i + 1)],
                                        wl[:, k, P * i:P * (i + 1)], hi[:, k, 0:nt], lo[:, k, 0:nt],
                                        k == 0, k == KT - 1)
                ins.then_inc(unit_done, 1)

            mixed_now = [0]

            def after(w):
                kind = UNITS[w][0]
                if kind == "v":
                    for b in (2 * UNITS[w][1], 2 * UNITS[w][1] + 1):
                        if b == 0:
                            pe.wait_ge(drained["act"], DRAINED[QKV + 7][1])
                        if b >= 1:
                            pe.wait_ge(qk_prep, 2 * b - 1)
                        src = (H if b < 4 else C)[:, 2 * (b % 4):2 * (b % 4) + 2, :]
                        mm(misc[:, 0, :], head_ones, src, start=True, stop=True).then_inc(qk_sum, 1)
                if kind == "a_z":
                    j = UNITS[w][1]
                    pe.wait_ge(v_normed, 4)
                    pe.wait_ge(mod_step, MOD_DONE[15 if w < MIX_A + 20 else 16])
                    if j >= 1:
                        pe.wait_ge(g_dve, 7 * (j - 1) + 4)
                    for i in range(2):
                        for t in range(4):
                            c = UC * j + P * i
                            ins = mm(misc[:, i, P * t:P * (t + 1)], VA[:, t, c:c + P], WS[:, j, :],
                                     start=True, stop=True)
                    ins.then_inc(mixed, 1)
                    mixed_now[0] = j + 1
                if kind == "b_z":
                    j = UNITS[w][1]
                    if j == 0:
                        pe.wait_ge(drained["act"], DRAINED[MIX_B + 5][1])
                    else:
                        pe.wait_ge(roped, 3 * (j + (j > 1)) - 2)
                    mm(misc[:, 0, :], perm, Q[:, 2 * j:2 * j + 2, :], start=True, stop=True)\
                        .then_inc(turned, 1)
                    if j == 0:
                        mm(misc[:, 1, :], perm, K2[:, :, 0:T], start=True, stop=True)\
                            .then_inc(turned, 1)

            def attention_1():
                pe.wait_ge(qk_final, 8)
                pe.wait_ge(drained["act"], DRAINED[WO - 1][1])
                for i in range(HEADS + 3):
                    if i < HEADS:
                        k, r = i // 2, 64 * (i % 2)
                        if i >= 2:
                            pe.wait_ge(z_ready, i - 1)
                        o = 512 * (i % 2)
                        q = Q[r:r + DH, k, :]
                        mm(prod[:, 0, o:o + P], q[:, 0:P], K1[r:r + DH, k, 0:P], start=True, stop=True)
                        mm(prod[:, 0, o + P:o + 3 * P], q[:, P:2 * P], K1[r:r + DH, k, :],
                           start=True, stop=True).then_inc(scored, 1)
                    if 2 <= i < HEADS + 2:
                        h = i - 2
                        pe.wait_ge(p_ready, 3 * (h + 1))
                        if h >= 2:
                            pe.wait_ge(pt_copied, h - 1)
                        turn(S1[:, h % 3, :], h % 2, 3)
                    if i >= 3:
                        h = i - 3
                        k, r, b = h // 2, 64 * (h % 2), h % 2
                        pe.wait_ge(pt_copied, h + 1)
                        if k >= 2:
                            pe.wait_ge(acts_lo, SET[4] + k - 1)
                        o = 512 * (k % 2)
                        v = V1[:, :, DH * h:DH * (h + 1)]
                        mm(prod[r:r + DH, 2, o:o + P], v[:, 0, :], PT1[:, b, 0:P], start=True, stop=True)
                        mm(prod[r:r + DH, 2, o + P:o + T], v[:, 0, :], PT1[:, b, P:2 * P],
                           start=True, stop=False)
                        mm(prod[r:r + DH, 2, o + P:o + T], v[:, 1, :], PT1[:, b, 2 * P:3 * P],
                           start=False, stop=True).then_inc(head_out, 1)

            def turn(src, b, n):
                for c in range(n):
                    ins = nc.tensor.transpose(prod[:, 1, 512 * b + P * c:512 * b + P * (c + 1)],
                                              src[:, P * c:P * (c + 1)], ident)
                ins.then_inc(p_turned, 1)

            def attention_2():
                NI = 2 * HEADS
                pe.wait_ge(roped, 15)
                pe.wait_ge(drained["dve"], DRAINED[B_OUT - 1][1])
                for i in range(NI + 3):
                    if i < NI:
                        k, off, t = i // 4, (i // 2) % 2, i % 2
                        r, b = 64 * off, i % 2
                        if i >= 2:
                            pe.wait_ge(max_ready, 3 * HEADS + 2 * (i - 2) + 1)
                        mm(prod[:, 0, 512 * b:512 * b + 512], Q[r:r + DH, k, P * t:P * (t + 1)],
                           K2[r:r + DH, k // 4, :], start=True, stop=True).then_inc(scored, 1)
                    if 2 <= i < NI + 2:
                        h = i - 2
                        pe.wait_ge(p_ready, 3 * HEADS + 3 * (h + 1))
                        if h >= 2:
                            pe.wait_ge(pt_copied, HEADS + h - 1)
                        turn(S2[:, h % 3, :], h % 2, 4)
                    if i >= 3:
                        h = i - 3
                        k, off, t, b = h // 4, (h // 2) % 2, h % 2, h % 2
                        r = 64 * off
                        g = 2 * (k // 4) + off
                        pe.wait_ge(pt_copied, HEADS + h + 1)
                        if k >= 2:
                            pe.wait_ge(o_gated, k - 1)
                        o = 512 * (k % 2) + P * t
                        for c in range(4):
                            ins = mm(prod[r:r + DH, 2, o:o + P], V2[:, c, DH * g:DH * (g + 1)],
                                     PT2[:, b, P * c:P * (c + 1)], start=(c == 0), stop=(c == 3))
                        ins.then_inc(head_out, 1)

            def boundary(n):
                if n == 0:
                    sum_squares(0, H)
                elif n == CONV_OUT:
                    sum_tiles(CV, T, lambda k: pe.wait_ge(conv_step, 62 * (k // 2 + 1)))
                    sum_squares(1, H)
                elif n == MLP0:
                    sum_squares(2, H)
                elif n == QKV:
                    sum_squares(3, H)
                elif n == WO:
                    attention_1()
                elif n == MLP1:
                    sum_squares(4, H)
                elif n == MIX_A:
                    pe.wait_ge(params_loaded, 80)
                    pe.wait_ge(mod_step, MOD_DONE[14])
                    for g in range(2):
                        ins = mm(misc[:, g, :], ones, WS[:, 4 * g:4 * (g + 1), :], start=True, stop=True)
                    ins.then_inc(row_sums, 1)
                elif n == MIX_B:
                    for m, (src, dst) in enumerate(((X, H), (C, H2))):
                        if m:
                            pe.wait_ge(var_prep, 2 * 5 + 1)
                        sum_tiles(src, T, lambda k: pe.wait_ge(x_updated, XU_B))
                        sum_squares(5 + m, dst)
                elif n == B_OUT:
                    attention_2()

            pe.wait_ge(params_loaded, 32)
            reduce_vector(0)
            reduce_vector(1)
            for w in range(NW):
                if w in FIRST_OF_SET:
                    boundary(w)
                unit(w)
                for vi in REDUCE_AFTER.get(w, []):
                    reduce_vector(vi)
                after(w)
            sum_tiles(X, T, lambda k: pe.wait_ge(x_updated, XU_B + k + 1))
            sum_squares(7, H)


def _unit(w, r0, c0):
    return w[r0:r0 + D, c0:c0 + UC].reshape(KT, P, UC).transpose(1, 0, 2).reshape(P, UNIT)


def _units(f):
    conv_in, conv_out, qkv, wo = f["conv_w_in"][0], f["conv_w_out"][0], f["attn_w_qkv"][0], f["attn_w_o"][0]
    a_in, a_out, b_in, b_out = f["a_w_in_2"][0], f["a_w_out_2"][0], f["b_w_in_2"][0], f["b_w_out_2"][0]
    order = [h for k in range(KT) for h in (4 * (2 * (k // 4)) + k % 4, 4 * (2 * (k // 4) + 1) + k % 4)]
    rows = np.concatenate([np.arange(DH * h, DH * (h + 1)) for h in order])
    bq = b_in[:, 0:D][:, rows]
    bz = b_in[:, D + 2 * UC:2 * D + 2 * UC][:, rows]
    bo = b_out[rows, :]
    A = 2 * D
    for u in UNITS:
        kind, j = u[0], u[-1]
        yield {
            "conv_a": lambda: _unit(conv_in, 0, UC * j),
            "conv_g": lambda: _unit(conv_in, 0, D + UC * j),
            "conv_out": lambda: _unit(conv_out, 0, UC * j),
            "w1": lambda: _unit(f["mlp_w1"][u[1]], 0, D * u[2] + UC * j),
            "w2": lambda: _unit(f["mlp_w2"][u[1]], D * u[2], UC * j),
            "q": lambda: _unit(qkv, 0, UC * j),
            "k": lambda: _unit(qkv, 0, D + UC * j),
            "v": lambda: _unit(qkv, 0, 2 * D + UC * j),
            "wo": lambda: _unit(wo, 0, UC * j),
            "a_u": lambda: _unit(a_in, 0, UC * j),
            "a_v": lambda: _unit(a_in, 0, A + UC * j),
            "a_z": lambda: _unit(a_in, 0, 2 * A + UC * j),
            "a_out": lambda: _unit(a_out, D * u[1], UC * j),
            "b_q": lambda: _unit(bq, 0, UC * j),
            "b_k": lambda: _unit(b_in, 0, D),
            "b_v": lambda: _unit(b_in, 0, D + UC),
            "b_z": lambda: _unit(bz, 0, UC * j),
            "b_out": lambda: _unit(bo, 0, UC * j),
        }[kind]()


def _stream(f):
    weights = list(_units(f))
    out = np.empty((NS, P, UNIT), np.float32)
    for n, s in enumerate(STREAM):
        if s[0] == "w":
            out[n] = weights[s[1]]
        else:
            block, layer, part = VECTORS[s[1]]
            w = f["ada_w" if block == 1 else "ada_w_2"][layer]
            rows = w[2 * P * s[2]:2 * P * (s[2] + 1), D * part:D * (part + 1)]
            out[n] = rows.reshape(2, P, D).transpose(1, 0, 2).reshape(P, UNIT)
    return out


def _columns(v):
    return v.reshape(-1, P).T


def _params(f):
    parts = {
        "c": f["c"][0], "c_2": f["c_2"][0], "c_ctx": f["c_ctx_2"], "ada_b": f["ada_b"],
        "ada_b_2": f["ada_b_2"], "mix_g": f["mix_norm_g"], "mlp_g": f["mlp_norm_g"],
        "conv_b_in": f["conv_b_in"], "conv_dw": f["conv_dw"], "conv_dw_b": f["conv_dw_b"],
        "conv_ln_g": f["conv_ln_g"], "conv_ln_b": f["conv_ln_b"], "conv_b_out": f["conv_b_out"],
        "ln_g_2": f["ln_g_2"], "ln_b_2": f["ln_b_2"], "a_ln_g": f["a_ln_g_2"], "a_ln_b": f["a_ln_b_2"],
    }
    out = np.empty((P, NCOL), np.float32)
    for name, v in parts.items():
        c = _columns(v)
        out[:, COLS[name]:COLS[name] + c.shape[1]] = c
    for name, key in (("qn_g", "attn_q_norm_g"), ("kn_g", "attn_k_norm_g")):
        out[0:DH, COLS[name]] = f[key][0]
        out[DH:, COLS[name]] = f[key][0]
    out[:, COLS["sink"]:COLS["sink"] + HEADS] = f["b_sink_2"][0][None, :]
    return out


def _constants():
    t = np.zeros((P, NCONST), np.float32)
    p = np.arange(P)

    def put(name, a):
        t[:, CONST[name]:CONST[name] + a.shape[1]] = a

    put("ident", np.eye(P))
    put("ones", np.ones((P, P)))
    put("head_ones", (p[:, None] // DH == p[None, :] // DH).astype(np.float32))
    swap = np.zeros((P, P))
    swap[p ^ 16, p] = np.where(p & 16, 1.0, -1.0)
    put("perm", swap)
    k1, k2 = np.arange(P)[None, :], np.arange(T)[None, :]
    d1, d2 = k1 - p[:, None], k2 - (P + p[:, None])
    put("alibi", np.concatenate([np.where(d1 <= 0, d1, NEG), np.where(d2 <= 0, d2, NEG)], 1))
    far = [np.where(np.abs(k2 - (P * b + p[:, None])) <= 128, 0.0, NEG) for b in range(2)]
    put("window", np.concatenate([far[0], np.zeros((P, T)), far[1], np.zeros((P, T))], 1))
    n = 16
    inv = (10000.0 ** (-np.arange(n, dtype=np.float32) / n)).astype(np.float32)
    tok = np.arange(T)
    axis = np.where((p % 64)[:, None] < 32, (tok // 64)[None, :], (tok % 64)[None, :])
    ang = (axis.astype(np.float32) * inv[p % 16][:, None]).astype(np.float32)
    put("cos", np.cos(ang))
    put("sin", np.sin(ang))
    return t


def _features(x):
    return np.ascontiguousarray(x.T.reshape(KT, P, T).transpose(1, 0, 2))


def kernel(**inputs):
    import concourse.bacc as _bacc
    from concourse.bass_utils import run_bass_kernel_spmd as _run

    f = {k: np.asarray(v) for k, v in inputs.items()}
    arrays = {
        "stream": _stream(f),
        "params": _params(f),
        "constants": _constants(),
        "x_features": _features(f["x"][0]),
        "ctx_features": _features(f["ctx_2"][0]),
        "spatial_w": np.ascontiguousarray(f["a_w_s_2"][0].transpose(2, 0, 1)),
        "spatial_b": np.ascontiguousarray(np.broadcast_to(f["a_b_s_2"][0][None], (P, 8, P))),
    }
    nc = _bacc.Bacc("TRN2", target_bir_lowering=False, num_devices=1, dynamic_dma_scratch_size=1024)
    args = [nc.dram_tensor(k, a.shape, F32, kind="ExternalInput").ap() for k, a in arrays.items()]
    args.append(nc.dram_tensor("out_features", (P, KT, T), F32, kind="ExternalOutput").ap())
    build(nc, *args)
    r = _run(nc, [arrays], core_ids=[0])
    got = np.asarray(r.results[0]["out_features"])
    return np.ascontiguousarray(got.transpose(1, 0, 2).reshape(D, T).T)[None]
```

```python
import math
from contextlib import ExitStack

import numpy as np

import concourse.bass as bass
from concourse import mybir

P = 128
D = 1024
KT = D // P
T = 256
UC = 256
UNIT = KT * UC
RING = 4
SPLITS = 2
PAIRS = 3
HEADS = 16
DH = D // HEADS
KV_HEADS = 4
TAPS = 31
PAD = TAPS - 1
ALPHA = math.sqrt(2.0)
EPS = 1e-6
LN_EPS = 1e-5
NEG = -1e30
SCALE = 1.0 / math.sqrt(DH)

F32 = mybir.dt.float32
F32R = mybir.dt.float32r
ALU = mybir.AluOpType
ACT = mybir.ActivationFunctionType
AX = mybir.AxisListType.X



def mlp_units(m):
    order = [("w1", 0), ("w1", 1), ("w2", 0), ("w1", 2), ("w2", 1), ("w1", 3), ("w2", 2), ("w2", 3)]
    return [(kind, m, q, j) for kind, q in order for j in range(4)]


UNITS = []
for j in range(4):
    UNITS += [("conv_a", j), ("conv_g", j)]
CONV_OUT = len(UNITS)
UNITS += [("conv_out", j) for j in range(4)]
MLP0 = len(UNITS)
UNITS += mlp_units(0)
QKV = len(UNITS)
UNITS += [("q", j) for j in range(4)] + [("k", j) for j in range(4)] + [("v", j) for j in range(4)]
WO = len(UNITS)
UNITS += [("wo", j) for j in range(4)]
MLP1 = len(UNITS)
UNITS += mlp_units(1)
MIX_A = len(UNITS)
UNITS += [("a_v", j) for j in range(8)]
for half in range(2):
    pairs = [(kind, 4 * half + j) for j in range(4) for kind in ("a_u", "a_z")]
    UNITS += pairs + [("a_u", 4)] if half == 0 else pairs[1:]
    if half == 0:
        UNITS += [("a_out", 0, j) for j in range(4)]
UNITS += [("a_out", 1, j) for j in range(4)]
MIX_B = len(UNITS)
UNITS += [("b_q", j) for j in range(4)] + [("b_k", 0), ("b_v", 0)] + [("b_z", j) for j in range(4)]
B_OUT = len(UNITS)
UNITS += [("b_out", j) for j in range(4)]
NW = len(UNITS)

VECTORS = [(1, 0, part) for part in range(6)] + [(2, 0, 0)] + [(1, 1, part) for part in range(6)]
VECTORS += [(2, 0, 1), (2, 0, 2)] + [(2, 1, part) for part in range(3)]
VEC = {v: i for i, v in enumerate(VECTORS)}

MOD_BEFORE = [0] * NW
MOD_BEFORE[0] = 8
for s in (
    *range(0, 12),
    *range(12, 16), *range(20, 24), *range(25, 40, 2),
    44, 45, 46, 47, 48, 49, 54, 55, *range(56, 60),
    *range(60, 64), *range(68, 72), *range(76, 80),
    *range(92, 100), 101, 103, 105, 107,
):
    MOD_BEFORE[s] += 1
assert sum(MOD_BEFORE) == 4 * len(VECTORS)
CTX_AT = 80

STREAM = []
WHERE = []
REDUCE_AFTER = {}
_done = 0
for s in range(NW):
    for _ in range(MOD_BEFORE[s]):
        STREAM.append(("mod", _done // 4, _done % 4))
        _done += 1
        if _done % 4 == 0 and _done > 8:
            REDUCE_AFTER.setdefault(s, []).append(_done // 4 - 1)
    WHERE.append(len(STREAM))
    STREAM.append(("w", s))
NS = len(STREAM)


def mod_ops(vi):
    block, layer, part = VECTORS[vi]
    if block == 2:
        return 8 if (layer, part) == (1, 1) else 2
    return 2 if part in (1, 4) or (layer == 0 and part == 2) else 1


MOD_DONE = [sum(mod_ops(i) for i in range(vi + 1)) for vi in range(len(VECTORS))]

BY_ACT = {"w1", "q", "k", "v", "a_v", "a_u", "b_k", "b_v", "b_q"}
WITH_NEXT = {"conv_a"}
UPDATES = {"conv_out": 2, "w2": 2, "wo": 2, "a_out": 4, "b_out": 2}
DRAINED = []
_n = {"act": 0, "dve": 0, "x": 0}
for u in UNITS:
    who = "act" if u[0] in BY_ACT else "x" if u[0] in UPDATES else "dve"
    if u[0] in WITH_NEXT:
        DRAINED.append((who, _n[who] + 1))
    else:
        _n[who] += UPDATES.get(u[0], 1)
        DRAINED.append((who, _n[who]))

XU_CONV = 0
XU_MLP0 = XU_CONV + 8
XU_WO = XU_MLP0 + 32
XU_MLP1 = XU_WO + 8
XU_A = XU_MLP1 + 32
XU_B = XU_A + 32
XU_END = XU_B + 8

SET = [KT * i for i in range(12)]
FIRST_OF_SET = {0: 0, CONV_OUT: 1, MLP0: 2, QKV: 3, WO: 4, MLP1: 5, MIX_A: 7, MIX_B: 8, B_OUT: 10}

LAST_UPDATE = {}
for _first, _norm in ((CONV_OUT, 2), (QKV - 4, 3), (WO, 4), (MIX_B - 4, 5), (B_OUT, 7)):
    for j in range(4):
        LAST_UPDATE[_first + j] = (_norm, j)

LN_INDEX = {1: 0, 5: 1, 6: 2, 7: 3}
MEAN_DONE = {1: 2, 5: 7, 6: 8, 7: 11}
STAT_DONE = [1, 3, 4, 5, 6, 9, 10, 12]
LAST_XU = {2: XU_CONV, 3: XU_MLP0 + 24, 4: XU_WO}

COLS = {}
_c = 0
for _name, _k in (
    ("c", 8), ("c_2", 8), ("c_ctx", 8), ("ada_b", 96), ("ada_b_2", 48), ("mix_g", 16), ("mlp_g", 16),
    ("conv_b_in", 16), ("conv_dw", TAPS * 8), ("conv_dw_b", 8), ("conv_ln_g", 8), ("conv_ln_b", 8),
    ("conv_b_out", 8), ("qn_g", 1), ("kn_g", 1), ("ln_g_2", 16), ("ln_b_2", 16), ("a_ln_g", 16),
    ("a_ln_b", 16), ("sink", HEADS),
):
    COLS[_name] = _c
    _c += _k
NCOL = _c
CONV_PE = 4
DIAGS = 30
DIAG_GROUP = 10
NDIAG = TAPS * (KT - CONV_PE)

CONST = {}
_c = 0
for _name, _k in (("ident", P), ("ones", P), ("head_ones", P), ("perm", P), ("slopes", HEADS),
                  ("alibi", 3 * P),
                  ("window", 4 * T), ("cos", T), ("sin", T)):
    CONST[_name] = _c
    _c += _k
NCONST = _c
RESIDENT = CONST["alibi"]


def f_index(w):
    return sum(1 for u in UNITS[:w] if u[0] == "w1")


def head_of(i):
    k, off = i // 4, (i // 2) % 2
    return 4 * (2 * (k // 4) + off) + k % 4


def build(nc, stream, cols_in, const_in, x_in, ctx_in, ws_in, bs_in, out):
    with ExitStack() as ctx:
        def sb(name, shape, dt=F32):
            return ctx.enter_context(nc.sbuf_tensor(name, shape, dt))

        def sem(name):
            return ctx.enter_context(nc.semaphore(name))

        raw = sb("raw", [P, RING, UNIT])
        w_hi = sb("w_hi", [P, SPLITS, KT, UC], F32R)
        w_lo = sb("w_lo", [P, SPLITS, KT, UC], F32R)
        X = sb("X", [P, KT, T])
        C = sb("C", [P, KT, T])
        XH = sb("XH", [P, KT, 2 * T], F32R)
        XL = sb("XL", [P, KT, 2 * T], F32R)
        FH = sb("FH", [P, 2 * KT * T], F32R)
        FL = sb("FL", [P, 2 * KT * T], F32R)
        V = sb("V", [P, 8192])
        HT = sb("HT", [P, KT * T])
        acc = sb("acc", [P, 2, D])
        EV = sb("EV", [P, 2, 2 * T])
        WS = sb("WS", [P, 8, P])
        BS = sb("BS", [P, 8, P])
        SM = sb("SM", [P, 2, 2 * T])
        RR = sb("RR", [P, 2, P])
        col = sb("col", [P, NCOL])
        con = sb("con", [P, RESIDENT])
        cond = sb("cond", [P, 24])
        cond_t = sb("cond_t", [P, 24])
        half_b = sb("half_b", [P, 24])
        GX = sb("GX", [P, 1024])
        rq = sb("rq", [P, 2, HEADS])
        gqk = sb("gqk", [P, 1])
        gain3 = sb("gain3", [P, 2, KT])
        shift3 = sb("shift3", [P, 2, KT])
        mod1 = sb("mod1", [P, 12, KT])
        mod2 = sb("mod2", [P, 6, 2, KT])
        gate_b = sb("gate_b", [P, KT])
        rows = sb("rows", [P, 3, T])
        QV = [SM[:, 0, :], GX[:, 0:2 * T]]
        bst = sb("bst", [P, 4, 8, 6])
        mv = sb("mv", [P, 4, 2])
        vr = sb("vr", [P, 4])
        sm = sb("sm", [P, 3, 12])

        prod = ctx.enter_context(nc.psum_tensor("prod", [P, PAIRS, 1024], F32))
        misc = ctx.enter_context(nc.psum_tensor("misc", [P, 2, 512], F32))

        def stat_rows(n):
            if n == 6:
                return GX[:, 0:T], GX[:, T:2 * T], GX[:, 2 * T:3 * T], misc[:, 1, :]
            return rows[:, 0, :], rows[:, 1, :], rows[:, 2, :], misc[:, 0, :]

        ident = con[:, CONST["ident"]:CONST["ident"] + P]
        ones = con[:, CONST["ones"]:CONST["ones"] + P]
        head_ones = con[:, CONST["head_ones"]:CONST["head_ones"] + P]
        slopes = con[:, CONST["slopes"]:CONST["slopes"] + HEADS]
        perm = con[:, CONST["perm"]:CONST["perm"] + P]
        alibi = SM[:, 1, 0:3 * P]
        window = SM[:, :, :]
        cos_t = WS[:, 0:2, :].rearrange("p a b -> p (a b)")
        sin_t = WS[:, 2:4, :].rearrange("p a b -> p (a b)")

        def cl(name, i=0, n=1):
            return col[:, COLS[name] + i:COLS[name] + i + n]

        U = V[:, 0:KT * (T + PAD)].rearrange("p (k t) -> p k t", k=KT)
        CV = V[:, 2304:2304 + 2048].rearrange("p (k t) -> p k t", k=KT)
        TS = V[:, 4352:4352 + 2048].rearrange("p (k t) -> p k t", k=KT)
        DG = V[:, 4352:4352 + DIAGS * P].rearrange("p (n c) -> p n c", n=DIAGS)
        Q = V[:, 0:2048].rearrange("p (k t) -> p k t", k=KT)
        K1 = V[:, 2048:4096].rearrange("p (k t) -> p k t", k=KT)
        V1 = V[:, 4096:6144].rearrange("p (t c) -> p t c", t=2)
        VA = V[:, :].rearrange("p (t c) -> p t c", t=4)
        K2 = V[:, 2048:3072].rearrange("p (k t) -> p k t", k=2)
        V2 = V[:, 3072:4096].rearrange("p (t c) -> p t c", t=4)
        SZ = V[:, 4096:6144].rearrange("p (k t) -> p k t", k=KT)
        H2 = V[:, 6144:8192].rearrange("p (k t) -> p k t", k=KT)
        H = HT[:, :].rearrange("p (k t) -> p k t", k=KT)
        GU = [HT[:, 0:1024], GX[:, :]]
        TZ = HT[:, 1024:2048]
        RSB = EV[:, :, :].rearrange("p a (b c) -> p (a b) c", c=P)
        F_hi = FH[:, :].rearrange("p (b k t) -> p b k t", b=2, k=KT)
        F_lo = FL[:, :].rearrange("p (b k t) -> p b k t", b=2, k=KT)
        G_hi = FH[:, :].rearrange("p (k t) -> p k t", k=KT)
        G_lo = FL[:, :].rearrange("p (k t) -> p k t", k=KT)
        flat = C[:, :, :].rearrange("p k t -> p (k t)")
        S1 = flat[:, 0:3 * 384].rearrange("p (b n) -> p b n", b=3)
        PT1 = flat[:, 1152:1152 + 2 * 384].rearrange("p (b n) -> p b n", b=2)
        S2 = flat[:, 0:3 * 512].rearrange("p (b n) -> p b n", b=3)
        PT2 = V[:, 6144:6144 + 2 * 512].rearrange("p (b n) -> p b n", b=2)

        params_loaded = sem("params_loaded")
        x_loaded = sem("x_loaded")
        ctx_loaded = sem("ctx_loaded")
        tables_loaded = sem("tables_loaded")
        slot_loaded = [sem(f"slot_loaded{r}") for r in range(RING)]
        out_stored = sem("out_stored")
        unit_consumed = sem("unit_consumed")
        weight_hi = sem("weight_hi")
        unit_done = sem("unit_done")
        cond_tanh = sem("cond_tanh")
        cond_ready = sem("cond_ready")
        half_ready = sem("half_ready")
        acc_step = sem("acc_step")
        acc_reduced = sem("acc_reduced")
        mod_step = sem("mod_step")
        sq_ready = sem("sq_ready")
        stat_done = sem("stat_done")
        mean_ready = sem("mean_ready")
        centred = sem("centred")
        var_prep = sem("var_prep")
        rstd_ready = sem("rstd_ready")
        h_scaled = sem("h_scaled")
        h_final = sem("h_final")
        acts_hi = sem("acts_hi")
        acts_lo = sem("acts_lo")
        x_updated = sem("x_updated")
        drained = {"act": sem("drained_act"), "dve": sem("drained_dve"), "x": x_updated}
        x_scaled = sem("x_scaled")
        x_restored = sem("x_restored")
        diag_ready = sem("diag_ready")
        diag_used = sem("diag_used")
        conv_summed = sem("conv_summed")
        conv_copied = sem("conv_copied")
        padded = sem("padded")
        gate_tanh = sem("gate_tanh")
        gate_half = sem("gate_half")
        conv_step = sem("conv_step")
        silu_tanh = sem("silu_tanh")
        silu_step = sem("silu_step")
        y_ready = sem("y_ready")
        f_relu = sem("f_relu")
        f_hi = sem("f_hi")
        f_sq = sem("f_sq")
        f_lo = sem("f_lo")
        q_sum = sem("q_sum")
        q_prep = sem("q_prep")
        q_rstd = sem("q_rstd")
        k_sum = sem("k_sum")
        k_prep = sem("k_prep")
        k_rstd = sem("k_rstd")
        k_final = sem("k_final")
        scored = sem("scored")
        z_ready = sem("z_ready")
        max_ready = sem("max_ready")
        exp_done = sem("exp_done")
        p_ready = sem("p_ready")
        p_turned = sem("p_turned")
        pt_copied = sem("pt_copied")
        head_out = sem("head_out")
        o_gated = sem("o_gated")
        row_sums = sem("row_sums")
        row_copied = sem("row_copied")
        v_stats = sem("v_stats")
        v_prep = sem("v_prep")
        v_rstd = sem("v_rstd")
        v_normed = sem("v_normed")
        mixed = sem("mixed")
        g_act = sem("g_act")
        g_dve = sem("g_dve")
        g_hi = sem("g_hi")
        g_lo = sem("g_lo")
        z_tanh = sem("z_tanh")
        z_half = sem("z_half")
        turned = sem("turned")
        roped = sem("roped")

        block = ctx.enter_context(nc.Block())

        def pair(w):
            return prod[:, w % PAIRS, :]

        def conv_bank(k):
            return tiles(CONV_OUT + (k - CONV_PE) // 2, T)[:, k % 2, :]

        def tiles(w, n):
            return pair(w).rearrange("p (i t) -> p i t", i=2)[:, :, 0:n]

        @block.sync
        def _(sp):
            sp.dma_start(col[:, :], cols_in).then_inc(params_loaded, 16)
            sp.dma_start(con[:, :], const_in[:, 0:RESIDENT]).then_inc(params_loaded, 16)
            for n in range(NS):
                if n >= RING:
                    sp.wait_ge(unit_consumed, n - RING + 1)
                sp.dma_start(raw[:, n % RING, :], stream[n]).then_inc(slot_loaded[n % RING], 16)
                if n == 1:
                    sp.dma_start(X[:, :, :], x_in).then_inc(x_loaded, 16)
                if n == WHERE[MLP1 + RING]:
                    sp.wait_ge(acts_lo, SET[5])
                    sp.dma_start(C[:, :, :], ctx_in).then_inc(ctx_loaded, 16)
                if n == RING:
                    sp.dma_start(WS[:, :, :], ws_in).then_inc(params_loaded, 16)
                    sp.dma_start(BS[:, :, :], bs_in).then_inc(params_loaded, 16)
                    sp.dma_start(alibi, const_in[:, CONST["alibi"]:CONST["window"]])\
                        .then_inc(params_loaded, 16)
                if n == WHERE[MIX_B + 4]:
                    sp.wait_ge(g_lo, 8)
                    sp.dma_start(SM[:, :, :].rearrange("p a b -> p (a b)"),
                                 const_in[:, CONST["window"]:CONST["cos"]]).then_inc(tables_loaded, 16)
                    sp.dma_start(WS[:, 0:4, :].rearrange("p a b -> p (a b)"),
                                 const_in[:, CONST["cos"]:NCONST]).then_inc(tables_loaded, 16)
            sp.wait_ge(h_final, 8)
            sp.dma_start(out, H[:, :, :]).then_inc(out_stored, 16)
            sp.wait_ge(out_stored, 16)

        @block.scalar
        def _(act):
            A = nc.scalar.activation

            def split_hi(w):
                n = WHERE[w]
                act.wait_ge(slot_loaded[n % RING], 16 * (n // RING + 1))
                if w >= SPLITS:
                    act.wait_ge(unit_done, w - SPLITS + 1)
                A(w_hi[:, w % SPLITS, :, :].rearrange("p k c -> p (k c)"), raw[:, n % RING, :],
                  ACT.Copy).then_inc(weight_hi, 1)

            def squares(n, src, dst, ready, tiles_=range(KT)):
                for k in tiles_:
                    ready(k)
                    A(dst[:, k, :], src[:, k, :], ACT.Square).then_inc(sq_ready, 1)

            def rstd(n):
                _, var, rs, _ = stat_rows(n)
                act.wait_ge(var_prep, 2 * (n + 1))
                A(rs, var, ACT.Sqrt).then_inc(rstd_ready, 1)

            def biased_hi(n, s, bias, src=H, c=0, first=None):
                first = 8 * n if first is None else first
                for k in range(KT):
                    act.wait_ge(h_scaled, first + k + 1)
                    A(XH[:, k, c:c + T], src[:, k, :], ACT.Identity, bias=bias(k))\
                        .then_inc(acts_hi, 1)

            def modulated_hi(m, src, c):
                for k in range(KT):
                    A(XH[:, k, c:c + T], src[:, k, :], ACT.Identity, bias=mod2[:, 0, m, k:k + 1],
                      scale=mod2[:, 1, m, k:k + 1]).then_inc(acts_hi, 1)

            def build_diags(a, b):
                for n in range(a, b):
                    k, tap = CONV_PE + n // TAPS, n % TAPS
                    if n >= DIAGS and n % DIAG_GROUP == 0:
                        act.wait_ge(diag_used, (n - DIAGS) // DIAG_GROUP + 1)
                    A(DG[:, n % DIAGS, :], ident, ACT.Copy, scale=cl("conv_dw", 8 * tap + k))\
                        .then_inc(diag_ready, 1)

            def drain(w):
                u = UNITS[w]
                kind = u[0]
                if kind == "conv_a":
                    return
                act.wait_ge(unit_done, w + 1)
                e = EV[:, w % 2, :]
                if kind == "conv_g":
                    j = u[1]
                    for i in range(2):
                        if j >= 1:
                            act.wait_ge(drained["dve"], DRAINED[w - 2][1])
                        A(EV[:, j % 2, i * T:(i + 1) * T], tiles(w, T)[:, i, :], ACT.Tanh,
                          bias=half_b[:, 2 * j + i:2 * j + i + 1], scale=0.5).then_inc(gate_tanh, 1)
                elif kind == "conv_out":
                    j = u[1]
                    act.wait_ge(mod_step, MOD_DONE[2])
                    if j < 2:
                        act.wait_ge(drained["dve"], DRAINED[CONV_OUT - 1][1])
                    for i in range(2):
                        k = 2 * j + i
                        if j >= 2:
                            act.wait_ge(x_updated, XU_CONV + 2 * (j - 1))
                        ins = A(e[:, i * T:(i + 1) * T], tiles(w, T)[:, i, :], ACT.Identity,
                                bias=gate_b[:, k:k + 1], scale=mod1[:, 2, k:k + 1])
                        ins.then_inc(y_ready, 1)
                elif kind == "w1":
                    f = f_index(w)
                    if f >= 2:
                        act.wait_ge(f_lo, f - 1)
                    ei = e.rearrange("p (i t) -> p i t", i=2)
                    A(ei, tiles(w, T), ACT.Relu).then_inc(drained["act"], 1)
                    act.wait_ge(drained["act"], DRAINED[w][1])
                    A(ei, ei, ACT.Square).then_inc(f_sq, 1)
                    act.wait_ge(f_sq, f + 1)
                    A(F_hi[:, u[2] % 2, 2 * u[3]:2 * u[3] + 2, :], ei, ACT.Copy).then_inc(f_hi, 1)
                elif kind in ("q", "k"):
                    j = u[1]
                    dst, sq = (Q, H) if kind == "q" else (K1, C)
                    A(dst[:, 2 * j:2 * j + 2, :], tiles(w, T), ACT.Copy)
                    A(sq[:, 2 * j:2 * j + 2, :], tiles(w, T), ACT.Square).then_inc(drained["act"], 1)
                elif kind == "v":
                    j = u[1]
                    A(V1[:, :, UC * j:UC * (j + 1)],
                      pair(w)[:, 0:2 * UC].rearrange("p (t c) -> p t c", t=2), ACT.Copy)\
                        .then_inc(drained["act"], 1)
                elif kind == "a_v":
                    j = u[1]
                    A(VA[:, :, UC * j:UC * (j + 1)], pair(w).rearrange("p (t c) -> p t c", t=4),
                      ACT.Gelu_apprx_tanh).then_inc(drained["act"], 1)
                    if j == 7:
                        act.wait_ge(v_prep, 6)
                        A(vr[:, :], vr[:, :], ACT.Sqrt).then_inc(v_rstd, 1)
                elif kind == "a_u":
                    j = u[1]
                    if j >= 2:
                        act.wait_ge(g_lo, j - 1)
                    A(GU[j % 2], pair(w), ACT.Gelu_apprx_tanh).then_inc(drained["act"], 1)
                elif kind == "a_z":
                    j = u[1]
                    if j >= 1:
                        act.wait_ge(g_lo, j)
                    A(TZ, pair(w), ACT.Tanh, scale=0.5).then_inc(g_act, 1)
                    act.wait_ge(g_dve, 7 * (j + 1))
                    if j == 4:
                        act.wait_ge(unit_done, UNITS.index(("a_out", 0, 3)) + 1)
                    A(G_hi[:, 2 * (j % 4):2 * (j % 4) + 2, :], GU[j % 2].rearrange("p (i t) -> p i t", i=2),
                      ACT.Copy).then_inc(g_hi, 1)
                elif kind == "b_k":
                    A(K2[:, :, :], tiles(w, 2 * T), ACT.Copy).then_inc(drained["act"], 1)
                elif kind == "b_v":
                    A(V2[:, :, :], pair(w).rearrange("p (t c) -> p t c", t=4), ACT.Copy)\
                        .then_inc(drained["act"], 1)
                elif kind == "b_q":
                    j = u[1]
                    A(Q[:, 2 * j:2 * j + 2, :], tiles(w, T), ACT.Copy).then_inc(drained["act"], 1)
                elif kind == "b_z":
                    j = u[1]
                    if j >= 2:
                        act.wait_ge(drained["dve"], DRAINED[w - 2][1])
                    A(e.rearrange("p (i t) -> p i t", i=2), tiles(w, T), ACT.Tanh, scale=0.5)\
                        .then_inc(z_tanh, 1)
                    if j == 0:
                        for k in range(KT):
                            act.wait_ge(x_restored, k + 1)
                            A(X[:, k, :], X[:, k, :], ACT.Identity, bias=half_b[:, 16 + k:17 + k],
                              scale=ALPHA).then_inc(x_scaled, 1)
                n, j = LAST_UPDATE.get(w, (5, 0))
                if n in (2, 3, 4):
                    squares(n, X, H, lambda k: act.wait_ge(x_updated, LAST_XU[n] + k + 1),
                            (2 * j, 2 * j + 1))
                if kind in ("k", "v"):
                    if w == QKV + 5:
                        act.wait_ge(q_prep, 2)
                        A(rq[:, :, :], rq[:, :, :], ACT.Sqrt).then_inc(q_rstd, 1)
                    b = w - (QKV + 6)
                    if 0 <= b < 4:
                        act.wait_ge(k_prep, 2 * (b + 1))
                        A(QV[b % 2], QV[b % 2], ACT.Sqrt).then_inc(k_rstd, 1)

            def attention_1():
                for i in range(HEADS + 3):
                    if i < HEADS:
                        slope = 2.0 ** (-8.0 * (i + 1) / HEADS)
                        b = i % 3
                        act.wait_ge(max_ready, 3 * (i + 1))
                        for t, (a, c) in enumerate(((0, P), (P, 3 * P))):
                            A(S1[:, b, a:c], S1[:, b, a:c], ACT.Exp, bias=sm[:, b, 2 + t:3 + t],
                              scale=slope, accum_out=sm[:, b, 4 + t:5 + t]).then_inc(exp_done, 1)
                    if 2 <= i < HEADS + 2:
                        h = i - 2
                        act.wait_ge(p_turned, h + 1)
                        A(PT1[:, h % 2, :], prod[:, 1, 512 * (h % 2):512 * (h % 2) + 3 * P],
                          ACT.Copy).then_inc(pt_copied, 1)
                    if i >= 4 and i % 2 == 0:
                        k = (i - 4) // 2
                        act.wait_ge(head_out, 2 * (k + 1))
                        A(XH[:, k, 0:T], prod[:, 2, 512 * (k % 2):512 * (k % 2) + T], ACT.Copy)\
                            .then_inc(acts_hi, 1)

            def attention_2():
                NI = 2 * HEADS
                for i in range(NI + 4):
                    if i < NI:
                        b = i % 3
                        act.wait_ge(max_ready, 3 * HEADS + 2 * (i + 1))
                        A(S2[:, b, :], S2[:, b, :], ACT.Exp, bias=sm[:, b, 2:3],
                          accum_out=sm[:, b, 4:5]).then_inc(exp_done, 1)
                        A(sm[:, b, 5:6], cl("sink", head_of(i)), ACT.Exp, bias=sm[:, b, 2:3])\
                            .then_inc(exp_done, 1)
                    if 2 <= i < NI + 2:
                        h = i - 2
                        act.wait_ge(p_turned, HEADS + h + 1)
                        A(PT2[:, h % 2, :], prod[:, 1, 512 * (h % 2):512 * (h % 2) + 512], ACT.Copy)\
                            .then_inc(pt_copied, 1)
                    if i >= 7 and (i - 7) % 4 == 0:
                        k = (i - 7) // 4
                        act.wait_ge(o_gated, k + 1)
                        A(XH[:, k, 0:T], H[:, k, :], ACT.Copy).then_inc(acts_hi, 1)

            def boundary(n):
                if n in (MLP0, QKV, MLP1):
                    i, s, shift = {MLP0: (2, 2, 3), QKV: (3, 3, 6), MLP1: (4, 5, 9)}[n]
                    rstd(i)
                    act.wait_ge(unit_done, n)
                    biased_hi(i, s, lambda k: mod1[:, shift, k:k + 1])
                elif n == 0:
                    biased_hi(0, 0, lambda k: mod1[:, 0, k:k + 1])
                elif n == CONV_OUT:
                    at = DIAGS
                    for k in range(CONV_PE, KT):
                        to = min(NDIAG, DIAGS + TAPS * (k - CONV_PE + 1))
                        build_diags(at, to)
                        at = to
                        act.wait_ge(conv_summed, k - CONV_PE + 1)
                        A(CV[:, k, :], conv_bank(k), ACT.Identity, bias=cl("conv_dw_b", k))\
                            .then_inc(conv_copied, 1)
                    squares(1, CV, H, lambda k: act.wait_ge(centred, k + 1))
                    rstd(1)
                    for k in range(KT + 2):
                        if k < KT:
                            act.wait_ge(h_scaled, 8 + k + 1)
                            A(TS[:, k, :], H[:, k, :], ACT.Tanh, bias=half_b[:, 8 + k:9 + k], scale=0.5)\
                                .then_inc(silu_tanh, 1)
                        if k >= 2:
                            act.wait_ge(silu_step, 2 * (k - 2) + 2)
                            A(XH[:, k - 2, 0:T], TS[:, k - 2, :], ACT.Copy).then_inc(acts_hi, 1)
                elif n == WO:
                    attention_1()
                elif n == MIX_A:
                    act.wait_ge(row_sums, 1)
                    act.wait_ge(f_lo, 32)
                    A(RSB, misc[:, :, :].rearrange("p a (b c) -> p (a b) c", c=P), ACT.Copy)\
                        .then_inc(row_copied, 1)
                    act.wait_ge(unit_done, MIX_A)
                    act.wait_ge(x_updated, XU_A)
                    modulated_hi(0, X, 0)
                    act.wait_ge(acts_lo, SET[8])
                    A(X[:, :, :], X[:, :, :], ACT.Copy, scale=ALPHA).then_inc(x_scaled, 1)
                elif n == MIX_B:
                    squares(5, X, H, lambda k: act.wait_ge(centred, 8 + k + 1))
                    squares(6, C, H2, lambda k: act.wait_ge(centred, 16 + k + 1))
                    rstd(5)
                    biased_hi(5, 8, lambda k: shift3[:, 0, k:k + 1], H, 0, 56)
                    rstd(6)
                    biased_hi(6, 9, lambda k: shift3[:, 1, k:k + 1], H2, T, 64)
                elif n == B_OUT:
                    attention_2()

            act.wait_ge(params_loaded, 32)
            A(cond_t[:, :], col[:, COLS["c"]:COLS["c"] + 24], ACT.Tanh, scale=0.5)\
                .then_inc(cond_tanh, 1)
            A(half_b[:, 0:8], cl("conv_b_in", 8, 8), ACT.Copy, scale=0.5).then_inc(half_ready, 1)
            A(half_b[:, 8:16], cl("conv_ln_b", 0, 8), ACT.Copy, scale=0.5).then_inc(half_ready, 1)
            A(half_b[:, 16:24], cl("ln_b_2", 0, 8), ACT.Copy, scale=ALPHA).then_inc(half_ready, 1)
            act.wait_ge(half_ready, 3)
            build_diags(0, DIAGS)
            act.wait_ge(x_loaded, 16)
            squares(0, X, H, lambda k: None)
            rstd(0)
            for s in range(NW + 2):
                if s < NW:
                    split_hi(s)
                if s >= 2:
                    drain(s - 2)
                if s - 1 in FIRST_OF_SET:
                    boundary(s - 1)
                if s == CTX_AT:
                    act.wait_ge(mod_step, MOD_DONE[VEC[2, 0, 1]])
                    act.wait_ge(ctx_loaded, 16)
                    modulated_hi(1, C, T)
                    act.wait_ge(acts_lo, SET[7])
                    A(C[:, :, :], C[:, :, :], ACT.Copy, scale=ALPHA).then_inc(x_scaled, 1)
            squares(7, X, H, lambda k: act.wait_ge(centred, 24 + k + 1))
            rstd(7)

        @block.vector
        def _(dve):
            vec = nc.vector
            stt, ts, tt = vec.scalar_tensor_tensor, vec.tensor_scalar, vec.tensor_tensor
            count = {"acc": 0, "x": 0, "mod": 0}
            acc_last = {}

            def split_lo(w):
                n = WHERE[w]
                dve.wait_ge(weight_hi, w + 1)
                tt(w_lo[:, w % SPLITS, :, :].rearrange("p k c -> p (k c)"), raw[:, n % RING, :],
                   w_hi[:, w % SPLITS, :, :].rearrange("p k c -> p (k c)").bitcast(F32),
                   ALU.subtract).then_inc(unit_consumed, 1)

            def accumulate(n):
                _, vi, quarter = STREAM[n]
                block_no = VECTORS[vi][0]
                dve.wait_ge(slot_loaded[n % RING], 16 * (n // RING + 1))
                sums = [(vi % 2, 0)] if block_no == 1 else [(0, 8), (1, 16)]
                if quarter == 0 and vi >= 2:
                    both = 2 in (block_no, VECTORS[vi - 1][0])
                    dve.wait_ge(acc_reduced, vi if both else vi - 1)
                for i in range(2):
                    k = 2 * quarter + i
                    for b, c0 in sums:
                        src = raw[:, n % RING, i * D:(i + 1) * D]
                        c = cond[:, c0 + k:c0 + k + 1]
                        if k == 0:
                            ins = ts(acc[:, b, :], src, c, None, ALU.mult)
                        else:
                            s, v = acc_last[b]
                            dve.wait_ge(s, v)
                            ins = stt(out=acc[:, b, :], in0=src, scalar=c, in1=acc[:, b, :],
                                      op0=ALU.mult, op1=ALU.add)
                        if i == 1 and b == sums[-1][0]:
                            ins.then_inc(unit_consumed, 1)
                            acc_last[b] = (unit_consumed, n + 1)
                        else:
                            ins.then_inc(acc_step, 1)
                            count["acc"] += 1
                            acc_last[b] = (acc_step, count["acc"])

            def step(ins):
                ins.then_inc(mod_step, 1)
                count["mod"] += 1

            def finish_vector(vi):
                block_no, layer, part = VECTORS[vi]
                dve.wait_ge(acc_reduced, vi + 1)
                if block_no == 1:
                    got = misc[:, 1, 0:8]
                    m = mod1[:, 6 * layer + part, :]
                    b = cl("ada_b", 8 * (6 * layer + part), 8)
                    if part in (1, 4):
                        step(stt(out=m, in0=got, scalar=1.0, in1=b, op0=ALU.add, op1=ALU.add))
                        dve.wait_ge(mod_step, count["mod"])
                        step(tt(m, m, cl("mix_g" if part == 1 else "mlp_g", 8 * layer, 8), ALU.mult))
                    else:
                        step(tt(m, got, b, ALU.add))
                    if layer == 0 and part == 2:
                        dve.wait_ge(mod_step, count["mod"])
                        step(tt(gate_b[:, :], m, cl("conv_b_out", 0, 8), ALU.mult))
                else:
                    for i in range(2):
                        got = misc[:, 1, 8 * i:8 * i + 8]
                        b = cl("ada_b_2", 8 * (3 * layer + part), 8)
                        step(stt(out=mod2[:, 3 * layer + part, i, :], in0=got,
                                 scalar=1.0 if part == 1 else 0.0, in1=b, op0=ALU.add, op1=ALU.add))
                    if (layer, part) == (1, 1):
                        dve.wait_ge(mod_step, count["mod"])
                        for i in range(2):
                            step(tt(gain3[:, i, :], mod2[:, 4, i, :], cl("ln_g_2", 0, 8), ALU.mult))
                        for i in range(2):
                            step(tt(shift3[:, i, :], mod2[:, 4, i, :], cl("ln_b_2", 0, 8), ALU.mult))
                        dve.wait_ge(mod_step, count["mod"])
                        for i in range(2):
                            step(tt(shift3[:, i, :], shift3[:, i, :], mod2[:, 3, i, :], ALU.add))
                assert count["mod"] == MOD_DONE[vi]

            def update_x(ins_of):
                if count["x"] >= 1:
                    dve.wait_ge(x_updated, max(1, count["x"] - 7))
                ins_of().then_inc(x_updated, 1)
                count["x"] += 1

            def centre(n, src):
                m = LN_INDEX[n]
                mu, _, _, bank = stat_rows(n)
                dve.wait_ge(stat_done, MEAN_DONE[n])
                ts(mu, bank[:, T:2 * T], 1.0 / D, None, ALU.mult).then_inc(mean_ready, 1)
                dve.wait_ge(mean_ready, m + 1)
                for k in range(KT):
                    tt(src[:, k, :], src[:, k, :], mu, ALU.subtract).then_inc(centred, 1)

            def variance(n, eps):
                _, var, _, bank = stat_rows(n)
                dve.wait_ge(stat_done, STAT_DONE[n])
                ts(var, bank[:, 0:T], 1.0 / D, eps, ALU.mult, ALU.add).then_inc(var_prep, 1)
                dve.wait_ge(var_prep, 2 * n + 1)
                vec.reciprocal(var, var).then_inc(var_prep, 1)

            def scale_tile(n, k, src, dst, gain):
                stt(out=dst[:, k, :], in0=src[:, k, :], scalar=gain(k), in1=stat_rows(n)[2],
                    op0=ALU.mult, op1=ALU.mult).then_inc(h_scaled, 1)

            def scale_and_split(n, s, src, dst, gain, bias, c=0):
                dve.wait_ge(rstd_ready, n + 1)
                for k in range(KT + 1):
                    if k < KT:
                        scale_tile(n, k, src, dst, gain)
                    if k >= 1:
                        dve.wait_ge(acts_hi, SET[s] + k)
                        stt(out=XL[:, k - 1, c:c + T], in0=dst[:, k - 1, :], scalar=bias(k - 1),
                            in1=XH[:, k - 1, c:c + T].bitcast(F32), op0=ALU.add, op1=ALU.subtract)\
                            .then_inc(acts_lo, 1)

            def modulate_and_split(s, m, src, c, first):
                for k in range(KT + 1):
                    if k < KT:
                        ts(H[:, k, :], src[:, k, :], mod2[:, 1, m, k:k + 1],
                           mod2[:, 0, m, k:k + 1], ALU.mult, ALU.add).then_inc(h_scaled, 1)
                    if k >= 1:
                        dve.wait_ge(h_scaled, first + k)
                        dve.wait_ge(acts_hi, SET[s] + k)
                        tt(XL[:, k - 1, c:c + T], H[:, k - 1, :], XH[:, k - 1, c:c + T].bitcast(F32),
                           ALU.subtract).then_inc(acts_lo, 1)

            def conv_pair(j):
                for tap in range(TAPS):
                    for i in range(2):
                        k = 2 * j + i
                        d = cl("conv_dw", 8 * tap + k)
                        if tap == 0:
                            ins = ts(CV[:, k, :], U[:, k, 0:T], d, cl("conv_dw_b", k),
                                     ALU.mult, ALU.add)
                        else:
                            dve.wait_ge(conv_step, 62 * j + 2 * (tap - 1) + i + 1)
                            ins = stt(out=CV[:, k, :], in0=U[:, k, tap:tap + T], scalar=d,
                                      in1=CV[:, k, :], op0=ALU.mult, op1=ALU.add)
                        ins.then_inc(conv_step, 1)

            def drain(w):
                u = UNITS[w]
                kind = u[0]
                if kind == "conv_a":
                    return
                e = EV[:, w % 2, :]
                ei = e.rearrange("p (i t) -> p i t", i=2)
                if kind == "conv_g":
                    j = u[1]
                    g = EV[:, j % 2, :]
                    dve.wait_ge(gate_tanh, 2 * (j + 1))
                    ts(g, g, 0.5, 0.5, ALU.mult, ALU.add).then_inc(gate_half, 1)
                    dve.wait_ge(gate_half, j + 1)
                    for i in range(2):
                        k = 2 * j + i
                        ins = stt(out=U[:, k, PAD:PAD + T], in0=tiles(w - 1, T)[:, i, :],
                                  scalar=cl("conv_b_in", k), in1=g[:, i * T:(i + 1) * T],
                                  op0=ALU.add, op1=ALU.mult)
                    ins.then_inc(drained["dve"], 1)
                elif kind == "conv_out":
                    j = u[1]
                    for i in range(2):
                        k = 2 * j + i
                        dve.wait_ge(y_ready, k + 1)
                        update_x(lambda: tt(X[:, k, :], X[:, k, :], e[:, i * T:(i + 1) * T],
                                                  ALU.add))
                elif kind == "w1":
                    f = f_index(w)
                    dve.wait_ge(f_hi, f + 1)
                    fl = F_lo[:, u[2] % 2, 2 * u[3]:2 * u[3] + 2, :]
                    fh = F_hi[:, u[2] % 2, 2 * u[3]:2 * u[3] + 2, :]
                    tt(fl, ei, fh.bitcast(F32), ALU.subtract).then_inc(f_lo, 1)
                elif kind in ("w2", "wo", "b_out"):
                    dve.wait_ge(unit_done, w + 1)
                    j = u[-1]
                    for i in range(2):
                        k = 2 * j + i
                        if kind == "w2":
                            g = mod1[:, 6 * u[1] + 5, k:k + 1]
                        elif kind == "wo":
                            g = mod1[:, 8, k:k + 1]
                        else:
                            g = mod2[:, 5, 0, k:k + 1]
                            dve.wait_ge(x_scaled, 2 + KT)
                        update_x(lambda: stt(out=X[:, k, :], in0=tiles(w, T)[:, i, :],
                                                   scalar=g, in1=X[:, k, :], op0=ALU.mult,
                                                   op1=ALU.add))
                elif kind in ("k", "v"):
                    qk_norm(w)
                elif kind == "a_v":
                    j = u[1]
                    dve.wait_ge(drained["act"], DRAINED[w][1])
                    for t in range(4):
                        vec.bn_stats(bst[:, t, j, :], VA[:, t, UC * j:UC * (j + 1)])\
                            .then_inc(v_stats, 1)
                    if j == 7:
                        norm_values()
                elif kind == "a_u":
                    if u[1]:
                        mix_values(u[1])
                elif kind == "a_z":
                    if u[1] == 0:
                        mix_values(0)
                    mix_gates(u[1], w)
                elif kind == "a_out":
                    half, j = u[1], u[2]
                    dve.wait_ge(unit_done, w + 1)
                    dve.wait_ge(x_scaled, 2)
                    for m, buf in enumerate((X, C)):
                        for i in range(2):
                            k = 2 * j + i
                            update_x(lambda: stt(
                                out=buf[:, k, :], in0=tiles(w, 2 * T)[:, i, m * T:(m + 1) * T],
                                scalar=mod2[:, 2, m, k:k + 1], in1=buf[:, k, :],
                                op0=ALU.mult, op1=ALU.add))
                elif kind == "b_z":
                    j = u[1]
                    dve.wait_ge(z_tanh, j + 1)
                    ts(e, e, 0.5, 0.5, ALU.mult, ALU.add).then_inc(z_half, 1)
                    dve.wait_ge(z_half, j + 1)
                    tt(SZ[:, 2 * j:2 * j + 2, :], tiles(w, T), ei, ALU.mult)\
                        .then_inc(drained["dve"], 1)
                    rope(0, Q[:, 2 * j:2 * j + 2, :], j, j if j == 0 else j + 1)
                    if j == 0:
                        rope(1, K2[:, :, 0:T], 0, 1)
                        for k in range(KT):
                            stt(out=X[:, k, :], in0=X[:, k, :], scalar=cl("ln_g_2", k),
                                in1=stat_rows(5)[2], op0=ALU.mult, op1=ALU.mult)\
                                .then_inc(x_restored, 1)

            def rope(bank, dst, j, index):
                dve.wait_ge(tables_loaded, 32)
                dve.wait_ge(turned, index + 1)
                r = HT[:, 0:512].rearrange("p (i t) -> p i t", i=2)
                s2 = sin_t.unsqueeze(1).broadcast_to([P, 2, T])
                c2 = cos_t.unsqueeze(1).broadcast_to([P, 2, T])
                tt(r, misc[:, bank, :].rearrange("p (i t) -> p i t", i=2), s2, ALU.mult)\
                    .then_inc(roped, 1)
                tt(dst, dst, c2, ALU.mult).then_inc(roped, 1)
                dve.wait_ge(roped, 3 * index + 2)
                tt(dst, dst, r, ALU.add).then_inc(roped, 1)
                dve.wait_ge(roped, 3 * index + 3)

            def qk_norm(w):
                b = w - (QKV + 6)
                if b == -1:
                    dve.wait_ge(q_sum, 1)
                    r = rq[:, :, :].rearrange("p t h -> p (t h)")
                    ts(r, misc[:, 0, 0:2 * HEADS], 1.0 / DH, EPS, ALU.mult, ALU.add)\
                        .then_inc(q_prep, 1)
                    dve.wait_ge(q_prep, 1)
                    vec.reciprocal(r, r).then_inc(q_prep, 1)
                if 0 <= b < 4:
                    dve.wait_ge(k_sum, b + 1)
                    ts(QV[b % 2], misc[:, 0, :], 1.0 / DH, EPS, ALU.mult, ALU.add).then_inc(k_prep, 1)
                    dve.wait_ge(k_prep, 2 * b + 1)
                    vec.reciprocal(QV[b % 2], QV[b % 2]).then_inc(k_prep, 1)
                if b == 0:
                    dve.wait_ge(q_rstd, 1)
                    for t in range(2):
                        tt(rq[:, t, :], rq[:, t, :], slopes, ALU.mult).then_inc(q_prep, 1)
                if 1 <= b < 5:
                    b -= 1
                    dve.wait_ge(k_rstd, b + 1)
                    dst = K1[:, 2 * b:2 * b + 2, :]
                    stt(out=dst, in0=dst, scalar=gqk[:, 0:1],
                        in1=QV[b % 2].rearrange("p (i t) -> p i t", i=2), op0=ALU.mult,
                        op1=ALU.mult).then_inc(k_final, 1)

            def norm_values():
                dve.wait_ge(v_stats, 32)
                for t in range(4):
                    vec.bn_aggr(mv[:, t, :], bst[:, t, :, :]).then_inc(v_prep, 1)
                dve.wait_ge(v_prep, 4)
                ts(vr[:, :], mv[:, :, 1], LN_EPS, None, ALU.add).then_inc(v_prep, 1)
                dve.wait_ge(v_prep, 5)
                vec.reciprocal(vr[:, :], vr[:, :]).then_inc(v_prep, 1)
                dve.wait_ge(v_rstd, 1)
                for t in range(4):
                    ts(VA[:, t, :], VA[:, t, :], mv[:, t, 0:1], vr[:, t:t + 1], ALU.subtract,
                       ALU.mult).then_inc(v_normed, 1)

            def mix_values(j):
                n = 7 * j
                for i in range(2):
                    stt(out=RR[:, i, :], in0=RSB[:, j, :], scalar=cl("a_ln_b", 2 * j + i),
                        in1=BS[:, j, :], op0=ALU.mult, op1=ALU.add).then_inc(g_dve, 1)
                dve.wait_ge(g_dve, n + 2)
                dve.wait_ge(mixed, j + 1)
                for i in range(2):
                    stt(out=SM[:, i, :].rearrange("p (c q) -> p c q", c=4),
                        in0=misc[:, i, :].rearrange("p (c q) -> p c q", c=4),
                        scalar=cl("a_ln_g", 2 * j + i),
                        in1=RR[:, i, :].unsqueeze(1).broadcast_to([P, 4, P]),
                        op0=ALU.mult, op1=ALU.add).then_inc(g_dve, 1)
                dve.wait_ge(g_dve, n + 4)
                w = UNITS.index(("a_u", j))
                dve.wait_ge(drained["act"], DRAINED[w][1])
                g = GU[j % 2]
                tt(g, g, SM[:, :, :].rearrange("p i t -> p (i t)"), ALU.mult).then_inc(g_dve, 1)

            def mix_gates(j, w):
                n = 7 * j
                g = GU[j % 2]
                dve.wait_ge(g_act, j + 1)
                ts(TZ, TZ, 0.5, 0.5, ALU.mult, ALU.add).then_inc(g_dve, 1)
                dve.wait_ge(g_dve, n + 6)
                tt(TZ, pair(w), TZ, ALU.mult).then_inc(drained["dve"], 1)
                dve.wait_ge(drained["dve"], DRAINED[w][1])
                tt(g, g, TZ, ALU.mult).then_inc(g_dve, 1)
                dve.wait_ge(g_dve, n + 7)
                dve.wait_ge(g_hi, j + 1)
                k = 2 * (j % 4)
                tt(G_lo[:, k:k + 2, :], g.rearrange("p (i t) -> p i t", i=2),
                   G_hi[:, k:k + 2, :].bitcast(F32), ALU.subtract).then_inc(g_lo, 1)

            def attention_1():
                dve.wait_ge(params_loaded, 80)
                for i in range(HEADS + 4):
                    if i < HEADS:
                        slope = 2.0 ** (-8.0 * (i + 1) / HEADS)
                        b = i % 3
                        dve.wait_ge(scored, i + 1)
                        if i >= 3:
                            dve.wait_ge(p_turned, i - 2)
                        o = 512 * (i % 2)
                        for t, (a, c) in enumerate(((0, P), (P, 3 * P))):
                            stt(out=S1[:, b, a:c], in0=prod[:, 0, o + a:o + c],
                                scalar=rq[:, t, i:i + 1], in1=alibi[:, a:c], op0=ALU.mult,
                                op1=ALU.add).then_inc(z_ready, 1)
                        dve.wait_ge(z_ready, 2 * (i + 1))
                        vec.reduce_max(sm[:, b, 0:1], S1[:, b, 0:P], AX).then_inc(max_ready, 1)
                        vec.reduce_max(sm[:, b, 1:2], S1[:, b, P:3 * P], AX).then_inc(max_ready, 1)
                        dve.wait_ge(max_ready, 3 * i + 2)
                        ts(sm[:, b, 2:4], sm[:, b, 0:2], -slope, None, ALU.mult)\
                            .then_inc(max_ready, 1)
                    if 1 <= i <= HEADS:
                        h = i - 1
                        b = h % 3
                        dve.wait_ge(exp_done, 2 * (h + 1))
                        vec.reciprocal(sm[:, b, 6:8], sm[:, b, 4:6]).then_inc(p_ready, 1)
                        dve.wait_ge(p_ready, 3 * h + 1)
                        for t, (a, c) in enumerate(((0, P), (P, 3 * P))):
                            ts(S1[:, b, a:c], S1[:, b, a:c], sm[:, b, 6 + t:7 + t], None, ALU.mult)\
                                .then_inc(p_ready, 1)
                    if i >= 5 and i % 2 == 1:
                        k = (i - 5) // 2
                        dve.wait_ge(acts_hi, SET[4] + k + 1)
                        tt(XL[:, k, 0:T], prod[:, 2, 512 * (k % 2):512 * (k % 2) + T],
                           XH[:, k, 0:T].bitcast(F32), ALU.subtract).then_inc(acts_lo, 1)

            def attention_2():
                NI = 2 * HEADS
                for i in range(NI + 5):
                    if i < NI:
                        b = i % 3
                        dve.wait_ge(scored, HEADS + i + 1)
                        if i >= 3:
                            dve.wait_ge(p_turned, HEADS + i - 2)
                        vec.tensor_tensor_reduce(S2[:, b, :], prod[:, 0, 512 * (i % 2):512 * (i % 2) + 512],
                                                 window[:, i % 2, :], SCALE, cl("sink", head_of(i)),
                                                 ALU.add, ALU.max, sm[:, b, 0:1]).then_inc(max_ready, 1)
                        n = 3 * HEADS + 2 * i
                        dve.wait_ge(max_ready, n + 1)
                        ts(sm[:, b, 2:3], sm[:, b, 0:1], -1.0, None, ALU.mult)\
                            .then_inc(max_ready, 1)
                    if 1 <= i <= NI:
                        h = i - 1
                        b = h % 3
                        n = 3 * HEADS + 3 * h
                        dve.wait_ge(exp_done, 2 * HEADS + 2 * (h + 1))
                        tt(sm[:, b, 6:7], sm[:, b, 4:5], sm[:, b, 5:6], ALU.add)\
                            .then_inc(p_ready, 1)
                        dve.wait_ge(p_ready, n + 1)
                        vec.reciprocal(sm[:, b, 7:8], sm[:, b, 6:7]).then_inc(p_ready, 1)
                        dve.wait_ge(p_ready, n + 2)
                        ts(S2[:, b, :], S2[:, b, :], sm[:, b, 7:8], None, ALU.mult)\
                            .then_inc(p_ready, 1)
                    if i >= 7 and (i - 7) % 4 == 0 and (i - 7) // 4 < KT:
                        k = (i - 7) // 4
                        dve.wait_ge(head_out, HEADS + 4 * (k + 1))
                        tt(H[:, k, :], prod[:, 2, 512 * (k % 2):512 * (k % 2) + T], SZ[:, k, :],
                           ALU.mult).then_inc(o_gated, 1)
                    if i >= 8 and (i - 8) % 4 == 0:
                        k = (i - 8) // 4
                        dve.wait_ge(acts_hi, SET[10] + k + 1)
                        tt(XL[:, k, 0:T], H[:, k, :], XH[:, k, 0:T].bitcast(F32), ALU.subtract)\
                            .then_inc(acts_lo, 1)

            def boundary(n):
                if n in (0, MLP0, QKV, MLP1):
                    i, s, scale, shift = {0: (0, 0, 1, 0), MLP0: (2, 2, 4, 3), QKV: (3, 3, 7, 6),
                                          MLP1: (4, 5, 10, 9)}[n]
                    if n:
                        variance(i, EPS)
                    scale_and_split(i, s, X, H, lambda k: mod1[:, scale, k:k + 1],
                                    lambda k: mod1[:, shift, k:k + 1])
                elif n == CONV_OUT:
                    for j in range(CONV_PE // 2):
                        conv_pair(j)
                    dve.wait_ge(conv_step, TAPS * CONV_PE)
                    centre(1, CV)
                    variance(1, EPS)
                    dve.wait_ge(rstd_ready, 2)
                    for k in range(KT + 3):
                        if k < KT:
                            scale_tile(1, k, CV, H, lambda k: cl("conv_ln_g", k))
                        if 1 <= k < KT + 1:
                            i = k - 1
                            dve.wait_ge(silu_tanh, i + 1)
                            ts(TS[:, i, :], TS[:, i, :], 0.5, 0.5, ALU.mult, ALU.add)\
                                .then_inc(silu_step, 1)
                            dve.wait_ge(silu_step, 2 * i + 1)
                            stt(out=TS[:, i, :], in0=H[:, i, :], scalar=cl("conv_ln_b", i),
                                in1=TS[:, i, :], op0=ALU.add, op1=ALU.mult).then_inc(silu_step, 1)
                        if k >= 3:
                            i = k - 3
                            dve.wait_ge(acts_hi, SET[1] + i + 1)
                            tt(XL[:, i, 0:T], TS[:, i, :], XH[:, i, 0:T].bitcast(F32),
                               ALU.subtract).then_inc(acts_lo, 1)
                elif n == WO:
                    attention_1()
                elif n == MIX_A:
                    dve.wait_ge(x_updated, XU_A)
                    modulate_and_split(7, 0, X, 0, 48)
                elif n == MIX_B:
                    centre(5, X)
                    centre(6, C)
                    variance(5, LN_EPS)
                    scale_and_split(5, 8, X, H, lambda k: gain3[:, 0, k:k + 1],
                                    lambda k: shift3[:, 0, k:k + 1])
                    variance(6, LN_EPS)
                    scale_and_split(6, 9, C, H2, lambda k: gain3[:, 1, k:k + 1],
                                    lambda k: shift3[:, 1, k:k + 1], T)
                elif n == B_OUT:
                    attention_2()

            vec.memset(U[:, :, 0:PAD], 0.0).then_inc(padded, 1)
            dve.wait_ge(padded, 1)
            dve.wait_ge(params_loaded, 32)
            dve.wait_ge(cond_tanh, 1)
            ts(cond_t[:, :], cond_t[:, :], 0.5, 0.5, ALU.mult, ALU.add).then_inc(cond_ready, 1)
            dve.wait_ge(cond_ready, 1)
            tt(cond[:, :], cond_t[:, :], col[:, COLS["c"]:COLS["c"] + 24], ALU.mult)\
                .then_inc(cond_ready, 1)
            tt(gqk[:, :], cl("qn_g"), cl("kn_g"), ALU.mult).then_inc(cond_ready, 1)
            dve.wait_ge(cond_ready, 3)
            dve.wait_ge(x_loaded, 16)
            variance(0, EPS)
            at = 0
            for s in range(NW + 2):
                if s < NW:
                    while at < WHERE[s]:
                        accumulate(at)
                        at += 1
                        if at in (4, 8):
                            finish_vector(at // 4 - 1)
                    split_lo(s)
                    at += 1
                if s >= 2:
                    drain(s - 2)
                    for vi in REDUCE_AFTER.get(s - 2, []):
                        finish_vector(vi)
                if s - 1 in FIRST_OF_SET:
                    dve.wait_ge(mod_step, max(1, count["mod"]))
                    if s > 2:
                        dve.wait_ge(unit_done, s - 1)
                    boundary(s - 1)
                if s == CTX_AT:
                    dve.wait_ge(ctx_loaded, 16)
                    modulate_and_split(6, 1, C, T, 40)
            centre(7, X)
            variance(7, LN_EPS)
            dve.wait_ge(rstd_ready, 8)
            for k in range(KT + 1):
                if k < KT:
                    scale_tile(7, k, X, H, lambda k: cl("ln_g_2", 8 + k))
                if k >= 1:
                    dve.wait_ge(h_scaled, 72 + k)
                    ts(H[:, k - 1, :], H[:, k - 1, :], cl("ln_b_2", 8 + k - 1), None, ALU.add)\
                        .then_inc(h_final, 1)

        @block.tensor
        def _(pe):
            mm = nc.tensor.matmul

            def reduce_vector(vi):
                last = max(n for n, s in enumerate(STREAM) if s[0] == "mod" and s[1] == vi)
                pe.wait_ge(unit_consumed, last + 1)
                if vi:
                    pe.wait_ge(mod_step, MOD_DONE[vi - 1])
                reduced[0] = vi
                if vi == VEC[2, 1, 0]:
                    pe.wait_ge(row_copied, 1)
                if mixed_now[0]:
                    pe.wait_ge(g_dve, 7 * mixed_now[0] - 3)
                sums = [vi % 2] if VECTORS[vi][0] == 1 else [0, 1]
                for i, b in enumerate(sums):
                    for k in range(KT):
                        ins = mm(misc[:, 1, 8 * i + k:8 * i + k + 1], acc[:, b, P * k:P * (k + 1)],
                                 ones[:, 0:1], start=True, stop=True)
                ins.then_inc(acc_reduced, 1)

            def sum_tiles(bank, c, src, ready, which=range(KT)):
                for k in which:
                    ready(k)
                    ins = mm(misc[:, bank, c:c + T], ones, src[:, k, :], start=(k == 0),
                             stop=(k == KT - 1), skip_group_check=True)
                if k == KT - 1:
                    ins.then_inc(stat_done, 1)

            def sum_squares(n, src, which=range(KT)):
                sum_tiles(1 if n == 6 else 0, 0, src, lambda k: pe.wait_ge(sq_ready, 8 * n + k + 1), which)

            def early_sums(n, j):
                which = (2 * j, 2 * j + 1)
                if n == 5:
                    if j == 0:
                        pe.wait_ge(mod_step, MOD_DONE[-1])
                    for m, src in enumerate((X, C)):
                        sum_tiles(m, T, src, lambda k: pe.wait_ge(x_updated, XU_A + 16 + 4 * (j + 1)), which)
                elif n == 7:
                    sum_tiles(0, T, X, lambda k: pe.wait_ge(x_updated, XU_B + k + 1), which)
                else:
                    sum_squares(n, H, which)

            def three(out, lhs_hi, lhs_lo, rhs_hi, rhs_lo, start, stop):
                mm(out, lhs_hi, rhs_hi, start=start, stop=False)
                mm(out, lhs_hi, rhs_lo, start=False, stop=False)
                return mm(out, lhs_lo, rhs_hi, start=False, stop=stop)

            def unit(w):
                u = UNITS[w]
                kind = u[0]
                pe.wait_ge(unit_consumed, WHERE[w] + 1)
                if w >= PAIRS:
                    who, n = DRAINED[w - PAIRS]
                    pe.wait_ge(drained[who], n)
                wh, wl = w_hi[:, w % SPLITS], w_lo[:, w % SPLITS]
                s = FIRST_OF_SET.get(w)
                if w in (WO, B_OUT):
                    pe.wait_ge(acts_lo, SET[s + 1])

                if w == MIX_B + 4:
                    pe.wait_ge(acts_lo, SET[10])

                def ready(k):
                    if s is not None:
                        pe.wait_ge(acts_lo, SET[s] + k + 1)

                if kind in ("v", "a_v", "b_v"):
                    nt = 2 if kind == "v" else 4
                    order = [(t, k) for t in range(nt) for k in range(KT)]
                    if s is not None:
                        order = [(t, k) for a in range(2) for k in range(KT) for t in (a, a + 2)]
                    for t, k in order:
                            if t == 0:
                                ready(k)
                            ins = three(pair(w)[:, t * UC:(t + 1) * UC],
                                        XH[:, k, t * P:(t + 1) * P], XL[:, k, t * P:(t + 1) * P],
                                        wh[:, k, :], wl[:, k, :], k == 0, k == KT - 1)
                else:
                    if kind == "w2":
                        pe.wait_ge(f_lo, 16 * u[1] + 4 * (u[2] + 1))
                        hi, lo, nt = F_hi[:, u[2] % 2], F_lo[:, u[2] % 2], T
                    elif kind == "a_out":
                        pe.wait_ge(g_lo, 4 * (u[1] + 1))
                        hi, lo, nt = G_hi, G_lo, 2 * T
                    else:
                        nt = 2 * T if kind in ("a_u", "a_z", "b_k") else T
                        hi, lo = XH, XL
                    order = [(i, k) for i in range(2) for k in range(KT)]
                    if s is not None:
                        order = [(i, k) for k in range(KT) for i in range(2)]
                    for i, k in order:
                            if i == 0:
                                ready(k)
                            ins = three(tiles(w, nt)[:, i, :], wh[:, k, P * i:P * (i + 1)],
                                        wl[:, k, P * i:P * (i + 1)], hi[:, k, 0:nt], lo[:, k, 0:nt],
                                        k == 0, k == KT - 1)
                ins.then_inc(unit_done, 1)

            mixed_now = [0]
            reduced = [0]

            def after(w):
                kind = UNITS[w][0]
                b = w - (QKV + 6)
                if b == -1:
                    pe.wait_ge(drained["act"], DRAINED[QKV + 3][1])
                    pe.wait_ge(acts_lo, SET[4])
                    for t in range(2):
                        for k in range(KT):
                            c = HEADS * t + 2 * k
                            ins = mm(misc[:, 0, c:c + 2], H[:, k, P * t:P * (t + 1)],
                                     head_ones[:, 0:P:DH], start=True, stop=True)
                    ins.then_inc(q_sum, 1)
                if 0 <= b < 4:
                    pe.wait_ge(drained["act"], DRAINED[QKV + 4 + b][1])
                    if b == 0:
                        pe.wait_ge(q_prep, 1)
                    else:
                        pe.wait_ge(k_prep, 2 * b - 1)
                    mm(misc[:, 0, :], head_ones, C[:, 2 * b:2 * b + 2, :], start=True, stop=True)\
                        .then_inc(k_sum, 1)
                if (kind == "a_u" and UNITS[w][1]) or UNITS[w] == ("a_z", 0):
                    j = UNITS[w][1]
                    pe.wait_ge(v_normed, 4)
                    pe.wait_ge(mod_step, MOD_DONE[reduced[0]])
                    if j >= 1:
                        pe.wait_ge(g_dve, 7 * (j - 1) + 4)
                    for i in range(2):
                        for t in range(4):
                            c = UC * j + P * i
                            ins = mm(misc[:, i, P * t:P * (t + 1)], VA[:, t, c:c + P], WS[:, j, :],
                                     start=True, stop=True)
                    ins.then_inc(mixed, 1)
                    mixed_now[0] = j + 1
                if kind == "b_z":
                    j = UNITS[w][1]
                    if j == 0:
                        pe.wait_ge(drained["act"], DRAINED[MIX_B + 5][1])
                    else:
                        pe.wait_ge(roped, 3 * (j + (j > 1)) - 2)
                    mm(misc[:, 0, :], perm, Q[:, 2 * j:2 * j + 2, :], start=True, stop=True)\
                        .then_inc(turned, 1)
                    if j == 0:
                        mm(misc[:, 1, :], perm, K2[:, :, 0:T], start=True, stop=True)\
                            .then_inc(turned, 1)

            def attention_1():
                pe.wait_ge(k_final, 4)
                pe.wait_ge(q_prep, 4)
                pe.wait_ge(drained["act"], DRAINED[WO - 1][1])
                for i in range(HEADS + 3):
                    if i < HEADS:
                        k, r = i // 2, 64 * (i % 2)
                        if i >= 2:
                            pe.wait_ge(z_ready, 2 * (i - 1))
                        o = 512 * (i % 2)
                        q = Q[r:r + DH, k, :]
                        mm(prod[:, 0, o:o + P], q[:, 0:P], K1[r:r + DH, k, 0:P], start=True, stop=True)
                        mm(prod[:, 0, o + P:o + 3 * P], q[:, P:2 * P], K1[r:r + DH, k, :],
                           start=True, stop=True).then_inc(scored, 1)
                    if 2 <= i < HEADS + 2:
                        h = i - 2
                        pe.wait_ge(p_ready, 3 * (h + 1))
                        if h >= 2:
                            pe.wait_ge(pt_copied, h - 1)
                        turn(S1[:, h % 3, :], h % 2, 3)
                    if i >= 3:
                        h = i - 3
                        k, r, b = h // 2, 64 * (h % 2), h % 2
                        pe.wait_ge(pt_copied, h + 1)
                        if k >= 2:
                            pe.wait_ge(acts_lo, SET[4] + k - 1)
                        o = 512 * (k % 2)
                        v = V1[:, :, DH * h:DH * (h + 1)]
                        mm(prod[r:r + DH, 2, o:o + P], v[:, 0, :], PT1[:, b, 0:P], start=True, stop=True)
                        mm(prod[r:r + DH, 2, o + P:o + T], v[:, 0, :], PT1[:, b, P:2 * P],
                           start=True, stop=False)
                        mm(prod[r:r + DH, 2, o + P:o + T], v[:, 1, :], PT1[:, b, 2 * P:3 * P],
                           start=False, stop=True).then_inc(head_out, 1)

            def turn(src, b, n):
                for c in range(n):
                    ins = nc.tensor.transpose(prod[:, 1, 512 * b + P * c:512 * b + P * (c + 1)],
                                              src[:, P * c:P * (c + 1)], ident)
                ins.then_inc(p_turned, 1)

            def attention_2():
                NI = 2 * HEADS
                pe.wait_ge(roped, 15)
                pe.wait_ge(drained["dve"], DRAINED[B_OUT - 1][1])
                pe.wait_ge(x_restored, 8)
                for i in range(NI + 3):
                    if i < NI:
                        k, off, t = i // 4, (i // 2) % 2, i % 2
                        r, b = 64 * off, i % 2
                        if i >= 2:
                            pe.wait_ge(max_ready, 3 * HEADS + 2 * (i - 2) + 1)
                        mm(prod[:, 0, 512 * b:512 * b + 512], Q[r:r + DH, k, P * t:P * (t + 1)],
                           K2[r:r + DH, k // 4, :], start=True, stop=True).then_inc(scored, 1)
                    if 2 <= i < NI + 2:
                        h = i - 2
                        pe.wait_ge(p_ready, 3 * HEADS + 3 * (h + 1))
                        if h >= 2:
                            pe.wait_ge(pt_copied, HEADS + h - 1)
                        turn(S2[:, h % 3, :], h % 2, 4)
                    if i >= 3:
                        h = i - 3
                        k, off, t, b = h // 4, (h // 2) % 2, h % 2, h % 2
                        r = 64 * off
                        g = 2 * (k // 4) + off
                        pe.wait_ge(pt_copied, HEADS + h + 1)
                        if k >= 2:
                            pe.wait_ge(o_gated, k - 1)
                        o = 512 * (k % 2) + P * t
                        for c in range(4):
                            ins = mm(prod[r:r + DH, 2, o:o + P], V2[:, c, DH * g:DH * (g + 1)],
                                     PT2[:, b, P * c:P * (c + 1)], start=(c == 0), stop=(c == 3))
                        ins.then_inc(head_out, 1)

            def boundary(n):
                if n in (MLP0, QKV, MLP1):
                    for j in (2, 3):
                        early_sums({MLP0: 2, QKV: 3, MLP1: 4}[n], j)
                elif n == CONV_OUT:
                    pe.wait_ge(drained["dve"], DRAINED[n - 1][1])
                    for i in range(NDIAG):
                        k, tap = CONV_PE + i // TAPS, i % TAPS
                        if i % DIAG_GROUP == 0:
                            pe.wait_ge(diag_ready, min(i + DIAG_GROUP, NDIAG))
                        ins = mm(conv_bank(k), DG[:, i % DIAGS, :], U[:, k, tap:tap + T],
                                 start=(tap == 0), stop=(tap == TAPS - 1))
                        if tap == TAPS - 1:
                            ins.then_inc(conv_summed, 1)
                        if i % DIAG_GROUP == DIAG_GROUP - 1:
                            assert tap != TAPS - 1
                            ins.then_inc(diag_used, 1)
                    sum_tiles(0, T, CV, lambda k: pe.wait_ge(conv_step, 2 * TAPS * (k // 2 + 1))
                              if k < CONV_PE else pe.wait_ge(conv_copied, k - CONV_PE + 1))
                    sum_squares(1, H)
                elif n == WO:
                    attention_1()
                elif n == MIX_A:
                    pe.wait_ge(params_loaded, 80)
                    pe.wait_ge(mod_step, MOD_DONE[reduced[0]])
                    for g in range(2):
                        ins = mm(misc[:, g, :], ones, WS[:, 4 * g:4 * (g + 1), :], start=True, stop=True)
                    ins.then_inc(row_sums, 1)
                elif n == MIX_B:
                    for j in (2, 3):
                        early_sums(5, j)
                    sum_squares(5, H)
                    sum_squares(6, H2)
                elif n == B_OUT:
                    attention_2()

            pe.wait_ge(params_loaded, 32)
            sum_squares(0, H)
            reduce_vector(0)
            reduce_vector(1)
            for w in range(NW):
                if w in FIRST_OF_SET:
                    boundary(w)
                unit(w)
                for vi in REDUCE_AFTER.get(w, []):
                    reduce_vector(vi)
                after(w)
                if w - 2 in LAST_UPDATE and LAST_UPDATE[w - 2][1] < 2:
                    early_sums(*LAST_UPDATE[w - 2])
            early_sums(7, 2)
            early_sums(7, 3)
            sum_squares(7, H)


def _unit(w, r0, c0):
    return w[r0:r0 + D, c0:c0 + UC].reshape(KT, P, UC).transpose(1, 0, 2).reshape(P, UNIT)


def _units(f):
    conv_in, conv_out, qkv, wo = f["conv_w_in"][0], f["conv_w_out"][0], f["attn_w_qkv"][0], f["attn_w_o"][0]
    a_in, a_out, b_in, b_out = f["a_w_in_2"][0], f["a_w_out_2"][0], f["b_w_in_2"][0], f["b_w_out_2"][0]
    order = [h for k in range(KT) for h in (4 * (2 * (k // 4)) + k % 4, 4 * (2 * (k // 4) + 1) + k % 4)]
    rows = np.concatenate([np.arange(DH * h, DH * (h + 1)) for h in order])
    bq = b_in[:, 0:D][:, rows]
    bz = b_in[:, D + 2 * UC:2 * D + 2 * UC][:, rows]
    bo = b_out[rows, :]
    A = 2 * D
    for u in UNITS:
        kind, j = u[0], u[-1]
        yield {
            "conv_a": lambda: _unit(conv_in, 0, UC * j),
            "conv_g": lambda: _unit(conv_in, 0, D + UC * j),
            "conv_out": lambda: _unit(conv_out, 0, UC * j),
            "w1": lambda: _unit(f["mlp_w1"][u[1]], 0, D * u[2] + UC * j),
            "w2": lambda: _unit(f["mlp_w2"][u[1]], D * u[2], UC * j),
            "q": lambda: _unit(qkv, 0, UC * j),
            "k": lambda: _unit(qkv, 0, D + UC * j),
            "v": lambda: _unit(qkv, 0, 2 * D + UC * j),
            "wo": lambda: _unit(wo, 0, UC * j),
            "a_u": lambda: _unit(a_in, 0, UC * j),
            "a_v": lambda: _unit(a_in, 0, A + UC * j),
            "a_z": lambda: _unit(a_in, 0, 2 * A + UC * j),
            "a_out": lambda: _unit(a_out, D * u[1], UC * j),
            "b_q": lambda: _unit(bq, 0, UC * j),
            "b_k": lambda: _unit(b_in, 0, D),
            "b_v": lambda: _unit(b_in, 0, D + UC),
            "b_z": lambda: _unit(bz, 0, UC * j),
            "b_out": lambda: _unit(bo, 0, UC * j),
        }[kind]()


def _stream(f):
    weights = list(_units(f))
    out = np.empty((NS, P, UNIT), np.float32)
    for n, s in enumerate(STREAM):
        if s[0] == "w":
            out[n] = weights[s[1]]
        else:
            block, layer, part = VECTORS[s[1]]
            w = f["ada_w" if block == 1 else "ada_w_2"][layer]
            rows = w[2 * P * s[2]:2 * P * (s[2] + 1), D * part:D * (part + 1)]
            out[n] = rows.reshape(2, P, D).transpose(1, 0, 2).reshape(P, UNIT)
    return out


def _columns(v):
    return v.reshape(-1, P).T


def _params(f):
    parts = {
        "c": f["c"][0], "c_2": f["c_2"][0], "c_ctx": f["c_ctx_2"], "ada_b": f["ada_b"],
        "ada_b_2": f["ada_b_2"], "mix_g": f["mix_norm_g"], "mlp_g": f["mlp_norm_g"],
        "conv_b_in": f["conv_b_in"], "conv_dw": f["conv_dw"], "conv_dw_b": f["conv_dw_b"],
        "conv_ln_g": f["conv_ln_g"], "conv_ln_b": f["conv_ln_b"], "conv_b_out": f["conv_b_out"],
        "ln_g_2": f["ln_g_2"], "ln_b_2": f["ln_b_2"], "a_ln_g": f["a_ln_g_2"], "a_ln_b": f["a_ln_b_2"],
    }
    out = np.empty((P, NCOL), np.float32)
    for name, v in parts.items():
        c = _columns(v)
        out[:, COLS[name]:COLS[name] + c.shape[1]] = c
    for name, key in (("qn_g", "attn_q_norm_g"), ("kn_g", "attn_k_norm_g")):
        out[0:DH, COLS[name]] = f[key][0]
        out[DH:, COLS[name]] = f[key][0]
    out[:, COLS["sink"]:COLS["sink"] + HEADS] = f["b_sink_2"][0][None, :]
    return out


def _constants():
    t = np.zeros((P, NCONST), np.float32)
    p = np.arange(P)

    def put(name, a):
        t[:, CONST[name]:CONST[name] + a.shape[1]] = a

    put("ident", np.eye(P))
    put("ones", np.ones((P, P)))
    put("head_ones", (p[:, None] // DH == p[None, :] // DH).astype(np.float32))
    swap = np.zeros((P, P))
    swap[p ^ 16, p] = np.where(p & 16, 1.0, -1.0)
    put("perm", swap)
    put("slopes", np.broadcast_to(SCALE * 2.0 ** (8.0 * np.arange(1, HEADS + 1) / HEADS), (P, HEADS)))
    k1, k2 = np.arange(P)[None, :], np.arange(T)[None, :]
    d1, d2 = k1 - p[:, None], k2 - (P + p[:, None])
    put("alibi", np.concatenate([np.where(d1 <= 0, d1, NEG), np.where(d2 <= 0, d2, NEG)], 1))
    far = [np.where(np.abs(k2 - (P * b + p[:, None])) <= 128, 0.0, NEG) for b in range(2)]
    put("window", np.concatenate([far[0], np.zeros((P, T)), far[1], np.zeros((P, T))], 1))
    n = 16
    inv = (10000.0 ** (-np.arange(n, dtype=np.float32) / n)).astype(np.float32)
    tok = np.arange(T)
    axis = np.where((p % 64)[:, None] < 32, (tok // 64)[None, :], (tok % 64)[None, :])
    ang = (axis.astype(np.float32) * inv[p % 16][:, None]).astype(np.float32)
    put("cos", np.cos(ang))
    put("sin", np.sin(ang))
    return t


def _features(x):
    return np.ascontiguousarray(x.T.reshape(KT, P, T).transpose(1, 0, 2))


def kernel(**inputs):
    import concourse.bacc as _bacc
    from concourse.bass_utils import run_bass_kernel_spmd as _run

    f = {k: np.asarray(v) for k, v in inputs.items()}
    arrays = {
        "stream": _stream(f),
        "params": _params(f),
        "constants": _constants(),
        "x_features": _features(f["x"][0]),
        "ctx_features": _features(f["ctx_2"][0]),
        "spatial_w": np.ascontiguousarray(f["a_w_s_2"][0].transpose(2, 0, 1)),
        "spatial_b": np.ascontiguousarray(np.broadcast_to(f["a_b_s_2"][0][None], (P, 8, P))),
    }
    nc = _bacc.Bacc("TRN2", target_bir_lowering=False, num_devices=1, dynamic_dma_scratch_size=1024)
    args = [nc.dram_tensor(k, a.shape, F32, kind="ExternalInput").ap() for k, a in arrays.items()]
    args.append(nc.dram_tensor("out_features", (P, KT, T), F32, kind="ExternalOutput").ap())
    build(nc, *args)
    r = _run(nc, [arrays], core_ids=[0])
    got = np.asarray(r.results[0]["out_features"])
    return np.ascontiguousarray(got.transpose(1, 0, 2).reshape(D, T).T)[None]
```

```python
import math
from contextlib import ExitStack

import numpy as np

import concourse.bass as bass
from concourse import mybir

P = 128
D = 1024
KT = D // P
T = 256
UC = 256
UNIT = KT * UC
RING = 4
SPLITS = 2
PAIRS = 3
HEADS = 16
DH = D // HEADS
TAPS = 31
PAD = TAPS - 1
ALPHA = math.sqrt(2.0)
EPS = 1e-6
LN_EPS = 1e-5
NEG = -1e30
SCALE = 1.0 / math.sqrt(DH)

F32 = mybir.dt.float32
F32R = mybir.dt.float32r
ALU = mybir.AluOpType
ACT = mybir.ActivationFunctionType
AX = mybir.AxisListType.X



def mlp_units(m):
    order = [("w1", 0), ("w1", 1), ("w2", 0), ("w1", 2), ("w2", 1), ("w1", 3), ("w2", 2), ("w2", 3)]
    return [(kind, m, q, j) for kind, q in order for j in range(4)]


UNITS = []
for j in range(4):
    UNITS += [("conv_a", j), ("conv_g", j)]
CONV_OUT = len(UNITS)
UNITS += [("conv_out", j) for j in range(4)]
MLP0 = len(UNITS)
UNITS += mlp_units(0)
QKV = len(UNITS)
UNITS += [("q", j) for j in range(4)] + [("k", j) for j in range(4)] + [("v", j) for j in range(4)]
WO = len(UNITS)
UNITS += [("wo", j) for j in range(4)]
MLP1 = len(UNITS)
UNITS += mlp_units(1)
MIX_A = len(UNITS)
UNITS += [("a_v", j) for j in range(8)]
for half in range(2):
    pairs = [(kind, 4 * half + j) for j in range(4) for kind in ("a_u", "a_z")]
    UNITS += pairs + [("a_u", 4)] if half == 0 else pairs[1:]
    if half == 0:
        UNITS += [("a_out", 0, j) for j in range(4)]
UNITS += [("a_out", 1, j) for j in range(4)]
MIX_B = len(UNITS)
UNITS += [("b_q", j) for j in range(4)] + [("b_z", 0), ("b_z", 1), ("b_k", 0), ("b_v", 0)]
UNITS += [("b_z", 2), ("b_z", 3)]
B_OUT = len(UNITS)
UNITS += [("b_out", j) for j in range(4)]
NW = len(UNITS)

VECTORS = [(block, layer, part) for block, parts in ((1, 6), (2, 3)) for layer in range(2)
           for part in range(parts)]
VEC = {v: i for i, v in enumerate(VECTORS)}

MOD_BEFORE = [0] * NW
MOD_BEFORE[0] = 8
MOD_BEFORE[CONV_OUT + 2] = 8
for s in (
    10, 10, 11, 11,
    14, 15, 17, 19,
    21, 23, 25, 27, 29, 31, 33, 35,
    37, 39, 41, 42,
    44, 46, 47, 48, 49, 50, 51, 52,
    55, 56, 62, 64,
    66, 68, 71, 73, 76, 78, 81, 83,
    94, 95, 96, 97,
    99, 101, 103, 105, 109, 110, 111, 112,
    115, 117, 119, 120,
):
    MOD_BEFORE[s] += 1
assert sum(MOD_BEFORE) == 4 * len(VECTORS)
CTX_AT = 86

STREAM = []
WHERE = []
REDUCE_AFTER = {}
_done = 0
for s in range(NW):
    for _ in range(MOD_BEFORE[s]):
        STREAM.append(("mod", _done // 4, _done % 4))
        _done += 1
        if _done % 4 == 0 and _done > 16:
            REDUCE_AFTER.setdefault(s, []).append(_done // 4 - 1)
    WHERE.append(len(STREAM))
    STREAM.append(("w", s))
NS = len(STREAM)


def mod_ops(vi):
    block, layer, part = VECTORS[vi]
    if block == 2:
        return 8 if (layer, part) == (1, 1) else 2
    return 2 if part in (1, 4) or (layer == 0 and part == 2) else 1


MOD_DONE = [sum(mod_ops(i) for i in range(vi + 1)) for vi in range(len(VECTORS))]

BY_ACT = {"w1", "q", "k", "v", "a_v", "a_u", "b_k", "b_v", "b_q"}
WITH_NEXT = {"conv_a"}
UPDATES = {"conv_out": 2, "w2": 2, "wo": 2, "a_out": 4, "b_out": 2}
DRAINED = []
_n = {"act": 0, "dve": 0, "x": 0}
for u in UNITS:
    who = "act" if u[0] in BY_ACT else "x" if u[0] in UPDATES else "dve"
    if u[0] in WITH_NEXT:
        DRAINED.append((who, _n[who] + 1))
    else:
        _n[who] += UPDATES.get(u[0], 1)
        DRAINED.append((who, _n[who]))

XU_CONV = 0
XU_MLP0 = XU_CONV + 8
XU_WO = XU_MLP0 + 32
XU_MLP1 = XU_WO + 8
XU_A = XU_MLP1 + 32
XU_B = XU_A + 32

SET = [KT * i for i in range(12)]
FIRST_OF_SET = {0: 0, CONV_OUT: 1, MLP0: 2, QKV: 3, WO: 4, MLP1: 5, MIX_A: 7, MIX_B: 8, B_OUT: 10}

LAST_UPDATE = {}
for _first, _norm in ((CONV_OUT, 2), (QKV - 4, 3), (WO, 4), (MIX_B - 4, 5), (B_OUT, 7)):
    for j in range(4):
        LAST_UPDATE[_first + j] = (_norm, j)

LN_INDEX = {1: 0, 5: 1, 6: 2, 7: 3}
MEAN_DONE = {1: 2, 5: 7, 6: 8, 7: 11}
STAT_DONE = [1, 3, 4, 5, 6, 9, 10, 12]
LAST_XU = {2: XU_CONV, 3: XU_MLP0 + 24, 4: XU_WO}

COLS = {}
_c = 0
for _name, _k in (
    ("c", 8), ("c_2", 8), ("c_ctx", 8), ("ada_b", 96), ("ada_b_2", 48), ("mix_g", 16), ("mlp_g", 16),
    ("conv_b_in", 16), ("conv_dw", TAPS * 8), ("conv_dw_b", 8), ("conv_ln_g", 8), ("conv_ln_b", 8),
    ("conv_b_out", 8), ("qn_g", 1), ("kn_g", 1), ("ln_g_2", 16), ("ln_b_2", 16), ("a_ln_g", 16),
    ("a_ln_b", 16), ("sink", HEADS),
):
    COLS[_name] = _c
    _c += _k
NCOL = _c
CONV_PE = 4
CONV_EARLY = 6
DIAGS = 30
DIAG_GROUP = 10
NDIAG = TAPS * (KT - CONV_PE)

CONST = {}
_c = 0
for _name, _k in (("ident", P), ("ones", P), ("head_ones", P), ("perm", P), ("slopes", HEADS),
                  ("alibi", 3 * P), ("by_head", KT * HEADS), ("spread", KT * P),
                  ("window", 4 * T), ("cos", T), ("sin", T)):
    CONST[_name] = _c
    _c += _k
NCONST = _c
RESIDENT = CONST["alibi"]


def f_index(w):
    return sum(1 for u in UNITS[:w] if u[0] == "w1")


def head_of(i):
    k, off = i // 4, (i // 2) % 2
    return 4 * (2 * (k // 4) + off) + k % 4


def build(nc, stream, cols_in, const_in, x_in, ctx_in, ws_in, bs_in, out):
    with ExitStack() as ctx:
        def sb(name, shape, dt=F32):
            return ctx.enter_context(nc.sbuf_tensor(name, shape, dt))

        def sem(name):
            return ctx.enter_context(nc.semaphore(name))

        raw = sb("raw", [P, RING, UNIT])
        w_hi = sb("w_hi", [P, SPLITS, KT, UC], F32R)
        w_lo = sb("w_lo", [P, SPLITS, KT, UC], F32R)
        X = sb("X", [P, KT, T])
        C = sb("C", [P, KT, T])
        XH = sb("XH", [P, KT, 2 * T], F32R)
        XL = sb("XL", [P, KT, 2 * T], F32R)
        FH = sb("FH", [P, 2 * KT * T], F32R)
        FL = sb("FL", [P, 2 * KT * T], F32R)
        V = sb("V", [P, 8192])
        HT = sb("HT", [P, KT * T])
        acc = sb("acc", [P, 2, D])
        EV = sb("EV", [P, 2, 2 * T])
        WS = sb("WS", [P, 8, P])
        BS = sb("BS", [P, 8, P])
        SM = sb("SM", [P, 2, 2 * T])
        RR = sb("RR", [P, 2, P])
        col = sb("col", [P, NCOL])
        con = sb("con", [P, RESIDENT])
        cond = sb("cond", [P, 24])
        cond_t = sb("cond_t", [P, 24])
        half_b = sb("half_b", [P, 24])
        GX = sb("GX", [P, 1024])
        rq = sb("rq", [P, 2, HEADS])
        gqk = sb("gqk", [P, 1])
        gain3 = sb("gain3", [P, 2, KT])
        shift3 = sb("shift3", [P, 2, KT])
        mod1 = sb("mod1", [P, 12, KT])
        mod2 = sb("mod2", [P, 6, 2, KT])
        gate_b = sb("gate_b", [P, KT])
        rows = sb("rows", [P, 3, T])
        bst = sb("bst", [P, 4, 8, 6])
        mv = sb("mv", [P, 4, 2])
        vr = sb("vr", [P, 4])
        sm = sb("sm", [P, 3, 12])

        prod = ctx.enter_context(nc.psum_tensor("prod", [P, PAIRS, 1024], F32))
        misc = ctx.enter_context(nc.psum_tensor("misc", [P, 2, 512], F32))

        def stat_rows(n):
            if n == 6:
                return GX[:, 0:T], GX[:, T:2 * T], GX[:, 2 * T:3 * T], misc[:, 1, :]
            return rows[:, 0, :], rows[:, 1, :], rows[:, 2, :], misc[:, 0, :]

        ident = con[:, CONST["ident"]:CONST["ident"] + P]
        ones = con[:, CONST["ones"]:CONST["ones"] + P]
        head_ones = con[:, CONST["head_ones"]:CONST["head_ones"] + P]
        slopes = con[:, CONST["slopes"]:CONST["slopes"] + HEADS]
        perm = con[:, CONST["perm"]:CONST["perm"] + P]
        alibi = SM[:, 1, 0:3 * P]
        by_head = SM[:, 0, 0:KT * HEADS]
        spread = GX[0:HEADS, :]
        rk = SM[0:HEADS, 0, T:2 * T]
        window = SM[:, :, :]
        cos_t = WS[:, 0:2, :].rearrange("p a b -> p (a b)")
        sin_t = WS[:, 2:4, :].rearrange("p a b -> p (a b)")

        def cl(name, i=0, n=1):
            return col[:, COLS[name] + i:COLS[name] + i + n]

        U = V[:, 0:KT * (T + PAD)].rearrange("p (k t) -> p k t", k=KT)
        CV = V[:, 2304:2304 + 2048].rearrange("p (k t) -> p k t", k=KT)
        TS = V[:, 4352:4352 + 2048].rearrange("p (k t) -> p k t", k=KT)
        DG = V[:, 4352:4352 + DIAGS * P].rearrange("p (n c) -> p n c", n=DIAGS)
        Q = V[:, 0:2048].rearrange("p (k t) -> p k t", k=KT)
        K1 = V[:, 2048:4096].rearrange("p (k t) -> p k t", k=KT)
        V1 = V[:, 4096:6144].rearrange("p (t c) -> p t c", t=2)
        VA = V[:, :].rearrange("p (t c) -> p t c", t=4)
        K2 = V[:, 2048:3072].rearrange("p (k t) -> p k t", k=2)
        V2 = V[:, 3072:4096].rearrange("p (t c) -> p t c", t=4)
        Q_hi = FH[:, 0:2048].rearrange("p (k t) -> p k t", k=KT)
        Q_lo = FL[:, 0:2048].rearrange("p (k t) -> p k t", k=KT)
        K_hi = FH[:, 2048:3072].rearrange("p (k t) -> p k t", k=2)
        K_lo = FL[:, 2048:3072].rearrange("p (k t) -> p k t", k=2)
        ROPED = [(Q[:, 2 * j:2 * j + 2, :], Q_hi[:, 2 * j:2 * j + 2, :], Q_lo[:, 2 * j:2 * j + 2, :])
                 for j in range(4)]
        ROPED.insert(3, (K2, K_hi, K_lo))
        SZ = V[:, 4096:6144].rearrange("p (k t) -> p k t", k=KT)
        H2 = V[:, 6144:8192].rearrange("p (k t) -> p k t", k=KT)
        H = HT[:, :].rearrange("p (k t) -> p k t", k=KT)
        GU = [HT[:, 0:1024], GX[:, :]]
        TZ = HT[:, 1024:2048]
        RSB = EV[:, :, :].rearrange("p a (b c) -> p (a b) c", c=P)
        F_hi = FH[:, :].rearrange("p (b k t) -> p b k t", b=2, k=KT)
        F_lo = FL[:, :].rearrange("p (b k t) -> p b k t", b=2, k=KT)
        G_hi = FH[:, :].rearrange("p (k t) -> p k t", k=KT)
        G_lo = FL[:, :].rearrange("p (k t) -> p k t", k=KT)
        flat = C[:, :, :].rearrange("p k t -> p (k t)")
        S1 = flat[:, 0:3 * 384].rearrange("p (b n) -> p b n", b=3)
        PT1 = flat[:, 1152:1152 + 2 * 384].rearrange("p (b n) -> p b n", b=2)
        S2 = flat[:, 0:3 * 512].rearrange("p (b n) -> p b n", b=3)
        PT2 = V[:, 6144:6144 + 2 * 512].rearrange("p (b n) -> p b n", b=2)

        params_loaded = sem("params_loaded")
        x_loaded = sem("x_loaded")
        ctx_loaded = sem("ctx_loaded")
        tables_loaded = sem("tables_loaded")
        slot_loaded = [sem(f"slot_loaded{r}") for r in range(RING)]
        out_stored = sem("out_stored")
        unit_consumed = sem("unit_consumed")
        weight_hi = sem("weight_hi")
        unit_done = sem("unit_done")
        cond_tanh = sem("cond_tanh")
        cond_ready = sem("cond_ready")
        half_ready = sem("half_ready")
        acc_step = sem("acc_step")
        acc_reduced = sem("acc_reduced")
        mod_step = sem("mod_step")
        sq_ready = sem("sq_ready")
        stat_done = sem("stat_done")
        mean_ready = sem("mean_ready")
        centred = sem("centred")
        var_prep = sem("var_prep")
        rstd_ready = sem("rstd_ready")
        h_scaled = sem("h_scaled")
        h_final = sem("h_final")
        acts_hi = sem("acts_hi")
        acts_lo = sem("acts_lo")
        x_updated = sem("x_updated")
        drained = {"act": sem("drained_act"), "dve": sem("drained_dve"), "x": x_updated}
        x_scaled = sem("x_scaled")
        x_restored = sem("x_restored")
        diag_ready = sem("diag_ready")
        diag_used = sem("diag_used")
        conv_summed = sem("conv_summed")
        conv_copied = sem("conv_copied")
        padded = sem("padded")
        gate_tanh = sem("gate_tanh")
        gate_half = sem("gate_half")
        conv_step = sem("conv_step")
        silu_tanh = sem("silu_tanh")
        silu_step = sem("silu_step")
        y_ready = sem("y_ready")
        f_hi = sem("f_hi")
        f_sq = sem("f_sq")
        f_lo = sem("f_lo")
        q_sum = sem("q_sum")
        q_prep = sem("q_prep")
        q_rstd = sem("q_rstd")
        k_sum = sem("k_sum")
        k_prep = sem("k_prep")
        k_rstd = sem("k_rstd")
        k_spread = sem("k_spread")
        k_final = sem("k_final")
        scored = sem("scored")
        z_ready = sem("z_ready")
        max_ready = sem("max_ready")
        exp_done = sem("exp_done")
        p_ready = sem("p_ready")
        p_turned = sem("p_turned")
        pt_copied = sem("pt_copied")
        head_out = sem("head_out")
        o_gated = sem("o_gated")
        row_sums = sem("row_sums")
        row_copied = sem("row_copied")
        v_stats = sem("v_stats")
        v_prep = sem("v_prep")
        v_rstd = sem("v_rstd")
        v_normed = sem("v_normed")
        mixed = sem("mixed")
        g_act = sem("g_act")
        g_dve = sem("g_dve")
        g_hi = sem("g_hi")
        g_lo = sem("g_lo")
        z_tanh = sem("z_tanh")
        z_half = sem("z_half")
        turned = sem("turned")
        roped = sem("roped")
        roped_hi = sem("roped_hi")
        roped_lo = sem("roped_lo")

        block = ctx.enter_context(nc.Block())

        def pair(w):
            return prod[:, w % PAIRS, :]

        def conv_bank(k):
            return tiles(CONV_OUT + (k - CONV_PE) // 2, T)[:, k % 2, :]

        def tiles(w, n):
            return pair(w).rearrange("p (i t) -> p i t", i=2)[:, :, 0:n]

        A_OUT_2 = UNITS.index(("a_out", 1, 0))

        @block.sync
        def _(sp):
            sp.dma_start(col[:, :], cols_in).then_inc(params_loaded, 16)
            sp.dma_start(con[:, :], const_in[:, 0:RESIDENT]).then_inc(params_loaded, 16)
            for n in range(NS):
                if n >= RING:
                    sp.wait_ge(unit_consumed, n - RING + 1)
                sp.dma_start(raw[:, n % RING, :], stream[n]).then_inc(slot_loaded[n % RING], 16)
                if n == 1:
                    sp.dma_start(X[:, :, :], x_in).then_inc(x_loaded, 16)
                if n == WHERE[MLP1 + RING]:
                    sp.wait_ge(acts_lo, SET[5])
                    sp.dma_start(C[:, :, :], ctx_in).then_inc(ctx_loaded, 16)
                if n == WHERE[CONV_OUT]:
                    sp.dma_start(WS[:, :, :], ws_in).then_inc(params_loaded, 16)
                    sp.dma_start(BS[:, :, :], bs_in).then_inc(params_loaded, 16)
                    for dst, name in ((alibi, "alibi"), (by_head, "by_head"), (spread, "spread")):
                        rows_, width = dst.shape
                        sp.dma_start(dst, const_in[0:rows_, CONST[name]:CONST[name] + width])\
                            .then_inc(params_loaded, 16)
                if n == WHERE[MIX_B + 4]:
                    sp.wait_ge(g_lo, 8)
                    sp.dma_start(SM[:, :, :].rearrange("p a b -> p (a b)"),
                                 const_in[:, CONST["window"]:CONST["cos"]]).then_inc(tables_loaded, 16)
                    sp.dma_start(WS[:, 0:4, :].rearrange("p a b -> p (a b)"),
                                 const_in[:, CONST["cos"]:NCONST]).then_inc(tables_loaded, 16)
            for k in range(0, KT, 2):
                sp.wait_ge(h_final, k + 2)
                sp.dma_start(out[:, k:k + 2, :], H[:, k:k + 2, :]).then_inc(out_stored, 16)
            sp.wait_ge(out_stored, 16 * (KT // 2))

        @block.scalar
        def _(act):
            A = nc.scalar.activation

            def split_hi(w):
                n = WHERE[w]
                act.wait_ge(slot_loaded[n % RING], 16 * (n // RING + 1))
                if w >= SPLITS:
                    act.wait_ge(unit_done, w - SPLITS + 1)
                A(w_hi[:, w % SPLITS, :, :].rearrange("p k c -> p (k c)"), raw[:, n % RING, :],
                  ACT.Copy).then_inc(weight_hi, 1)

            def squares(n, src, dst, ready, tiles_=range(KT)):
                for k in tiles_:
                    ready(k)
                    A(dst[:, k, :], src[:, k, :], ACT.Square).then_inc(sq_ready, 1)

            def rstd(n):
                _, var, rs, _ = stat_rows(n)
                nc.scalar.preload_act_table(ACT.Sqrt)
                act.wait_ge(var_prep, 2 * (n + 1))
                A(rs, var, ACT.Sqrt).then_inc(rstd_ready, 1)

            def biased_hi(n, s, bias, src=H, c=0, first=None, which=range(KT)):
                first = 8 * n if first is None else first
                for k in which:
                    act.wait_ge(h_scaled, first + k + 1)
                    A(XH[:, k, c:c + T], src[:, k, :], ACT.Identity, bias=bias(k))\
                        .then_inc(acts_hi, 1)

            def modulated_hi(m, src, c, which):
                for k in which:
                    A(XH[:, k, c:c + T], src[:, k, :], ACT.Identity, bias=mod2[:, 0, m, k:k + 1],
                      scale=mod2[:, 1, m, k:k + 1]).then_inc(acts_hi, 1)

            def build_diags(a, b):
                for n in range(a, b):
                    k, tap = CONV_PE + n // TAPS, n % TAPS
                    if n >= DIAGS and n % DIAG_GROUP == 0:
                        act.wait_ge(diag_used, (n - DIAGS) // DIAG_GROUP + 1)
                    A(DG[:, n % DIAGS, :], ident, ACT.Copy, scale=cl("conv_dw", 8 * tap + k))\
                        .then_inc(diag_ready, 1)

            def drain(w):
                u = UNITS[w]
                kind = u[0]
                if kind == "conv_a":
                    return
                act.wait_ge(unit_done, w + 1)
                e = EV[:, w % 2, :]
                if kind == "conv_g":
                    j = u[1]
                    for i in range(2):
                        if j >= 1:
                            act.wait_ge(drained["dve"], DRAINED[w - 2][1])
                        A(EV[:, j % 2, i * T:(i + 1) * T], tiles(w, T)[:, i, :], ACT.Tanh,
                          bias=half_b[:, 2 * j + i:2 * j + i + 1], scale=0.5).then_inc(gate_tanh, 1)
                elif kind == "conv_out":
                    j = u[1]
                    act.wait_ge(mod_step, MOD_DONE[2])
                    if j < 2:
                        act.wait_ge(drained["dve"], DRAINED[CONV_OUT - 1][1])
                    for i in range(2):
                        k = 2 * j + i
                        if j >= 2:
                            act.wait_ge(x_updated, XU_CONV + 2 * (j - 1))
                        ins = A(e[:, i * T:(i + 1) * T], tiles(w, T)[:, i, :], ACT.Identity,
                                bias=gate_b[:, k:k + 1], scale=mod1[:, 2, k:k + 1])
                        ins.then_inc(y_ready, 1)
                elif kind == "w1":
                    f = f_index(w)
                    if f >= 2:
                        act.wait_ge(f_lo, f - 1)
                    ei = e.rearrange("p (i t) -> p i t", i=2)
                    A(ei, tiles(w, T), ACT.Relu).then_inc(drained["act"], 1)
                    act.wait_ge(drained["act"], DRAINED[w][1])
                    A(ei, ei, ACT.Square).then_inc(f_sq, 1)
                    act.wait_ge(f_sq, f + 1)
                    A(F_hi[:, u[2] % 2, 2 * u[3]:2 * u[3] + 2, :], ei, ACT.Copy).then_inc(f_hi, 1)
                elif kind in ("q", "k"):
                    j = u[1]
                    dst, sq = (Q, H) if kind == "q" else (K1, C)
                    A(dst[:, 2 * j:2 * j + 2, :], tiles(w, T), ACT.Copy)
                    A(sq[:, 2 * j:2 * j + 2, :], tiles(w, T), ACT.Square).then_inc(drained["act"], 1)
                elif kind == "v":
                    j = u[1]
                    A(V1[:, :, UC * j:UC * (j + 1)],
                      pair(w)[:, 0:2 * UC].rearrange("p (t c) -> p t c", t=2), ACT.Copy)\
                        .then_inc(drained["act"], 1)
                elif kind == "a_v":
                    j = u[1]
                    A(VA[:, :, UC * j:UC * (j + 1)], pair(w).rearrange("p (t c) -> p t c", t=4),
                      ACT.Gelu_apprx_tanh).then_inc(drained["act"], 1)
                    if j == 7:
                        act.wait_ge(v_prep, 6)
                        A(vr[:, :], vr[:, :], ACT.Sqrt).then_inc(v_rstd, 1)
                elif kind == "a_u":
                    j = u[1]
                    if j >= 2:
                        act.wait_ge(g_lo, j - 1)
                    A(GU[j % 2], pair(w), ACT.Gelu_apprx_tanh).then_inc(drained["act"], 1)
                elif kind == "a_z":
                    j = u[1]
                    if j >= 1:
                        act.wait_ge(g_lo, j)
                    A(TZ, pair(w), ACT.Tanh, scale=0.5).then_inc(g_act, 1)
                    act.wait_ge(g_dve, 7 * (j + 1))
                    if j == 4:
                        act.wait_ge(unit_done, UNITS.index(("a_out", 0, 3)) + 1)
                    A(G_hi[:, 2 * (j % 4):2 * (j % 4) + 2, :], GU[j % 2].rearrange("p (i t) -> p i t", i=2),
                      ACT.Copy).then_inc(g_hi, 1)
                elif kind == "b_k":
                    A(K2[:, :, :], tiles(w, 2 * T), ACT.Copy).then_inc(drained["act"], 1)
                elif kind == "b_v":
                    A(V2[:, :, :], pair(w).rearrange("p (t c) -> p t c", t=4), ACT.Copy)\
                        .then_inc(drained["act"], 1)
                elif kind == "b_q":
                    j = u[1]
                    A(Q[:, 2 * j:2 * j + 2, :], tiles(w, T), ACT.Copy).then_inc(drained["act"], 1)
                elif kind == "b_z":
                    j = u[1]
                    if j >= 2:
                        act.wait_ge(drained["dve"], DRAINED[UNITS.index(("b_z", j - 2))][1])
                    A(e.rearrange("p (i t) -> p i t", i=2), tiles(w, T), ACT.Tanh, scale=0.5)\
                        .then_inc(z_tanh, 1)
                    if j >= 1:
                        roped_tiles_hi(j - 1, j if j < 3 else 4)
                n, j = LAST_UPDATE.get(w, (5, 0))
                if n in (2, 3, 4):
                    squares(n, X, H, lambda k: act.wait_ge(x_updated, LAST_XU[n] + k + 1),
                            (2 * j, 2 * j + 1))
                if kind in ("k", "v"):
                    if w == QKV + 5:
                        act.wait_ge(q_prep, 2)
                        A(rq[:, :, :], rq[:, :, :], ACT.Sqrt).then_inc(q_rstd, 1)
                    if kind == "v" and u[1] == 0:
                        act.wait_ge(k_prep, 2)
                        A(rk, rk, ACT.Sqrt).then_inc(k_rstd, 1)

            def attention_1():
                for i in range(HEADS + 5):
                    if i < HEADS:
                        slope = 2.0 ** (-8.0 * (i + 1) / HEADS)
                        b = i % 3
                        act.wait_ge(max_ready, 3 * (i + 1))
                        for t, (a, c) in enumerate(((0, P), (P, 3 * P))):
                            A(S1[:, b, a:c], S1[:, b, a:c], ACT.Exp, bias=sm[:, b, 2 + t:3 + t],
                              scale=slope, accum_out=sm[:, b, 4 + t:5 + t]).then_inc(exp_done, 1)
                    if 2 <= i < HEADS + 2:
                        h = i - 2
                        act.wait_ge(p_turned, h + 1)
                        A(PT1[:, h % 2, :], prod[:, 1, 512 * (h % 2):512 * (h % 2) + 3 * P],
                          ACT.Copy).then_inc(pt_copied, 1)
                    if i >= 6 and i % 2 == 0:
                        k = (i - 6) // 2
                        act.wait_ge(head_out, 2 * (k + 1))
                        A(XH[:, k, 0:T], prod[:, 2, 512 * (k % 2):512 * (k % 2) + T], ACT.Copy)\
                            .then_inc(acts_hi, 1)

            def roped_tiles_hi(a, b):
                for n in range(a, b):
                    src, hi, _ = ROPED[n]
                    act.wait_ge(roped, 3 * (n + 1))
                    A(hi, src, ACT.Copy).then_inc(roped_hi, 1)

            def attention_2():
                NI = 2 * HEADS
                roped_tiles_hi(4, 5)
                for i in range(NI + 5):
                    if i < NI:
                        b = i % 3
                        act.wait_ge(max_ready, 3 * HEADS + 2 * (i + 1))
                        A(S2[:, b, :], S2[:, b, :], ACT.Exp, bias=sm[:, b, 2:3],
                          accum_out=sm[:, b, 4:5]).then_inc(exp_done, 1)
                        A(sm[:, b, 5:6], cl("sink", head_of(i)), ACT.Exp, bias=sm[:, b, 2:3])\
                            .then_inc(exp_done, 1)
                    if 2 <= i < NI + 2:
                        h = i - 2
                        act.wait_ge(p_turned, HEADS + h + 1)
                        A(PT2[:, h % 2, :], prod[:, 1, 512 * (h % 2):512 * (h % 2) + 512], ACT.Copy)\
                            .then_inc(pt_copied, 1)
                    if 3 <= i < 3 + KT:
                        k = i - 3
                        act.wait_ge(x_restored, k + 1)
                        A(X[:, k, :], X[:, k, :], ACT.Identity, bias=half_b[:, 16 + k:17 + k],
                          scale=ALPHA).then_inc(x_scaled, 1)
                    if i >= 8 and i % 4 == 0:
                        k = (i - 8) // 4
                        act.wait_ge(o_gated, k + 1)
                        A(XH[:, k, 0:T], H[:, k, :], ACT.Copy).then_inc(acts_hi, 1)

            def boundary(n):
                if n in (MLP0, QKV, MLP1):
                    i, s, shift = {MLP0: (2, 2, 3), QKV: (3, 3, 6), MLP1: (4, 5, 9)}[n]
                    rstd(i)
                    act.wait_ge(unit_done, n)
                    biased_hi(i, s, lambda k: mod1[:, shift, k:k + 1])
                elif n == 0:
                    biased_hi(0, 0, lambda k: mod1[:, 0, k:k + 1])
                elif n == CONV_OUT:
                    at = DIAGS
                    for k in range(CONV_PE, KT):
                        to = min(NDIAG, DIAGS + TAPS * (k - CONV_PE + 1))
                        build_diags(at, to)
                        at = to
                        act.wait_ge(conv_summed, k - CONV_PE + 1)
                        A(CV[:, k, :], conv_bank(k), ACT.Identity, bias=cl("conv_dw_b", k))\
                            .then_inc(conv_copied, 1)
                    squares(1, CV, H, lambda k: act.wait_ge(centred, k + 1))
                    rstd(1)
                    for k in range(KT + 2):
                        if k < KT:
                            act.wait_ge(h_scaled, 8 + k + 1)
                            A(TS[:, k, :], H[:, k, :], ACT.Tanh, bias=half_b[:, 8 + k:9 + k], scale=0.5)\
                                .then_inc(silu_tanh, 1)
                        if k >= 2:
                            act.wait_ge(silu_step, 2 * (k - 2) + 2)
                            A(XH[:, k - 2, 0:T], TS[:, k - 2, :], ACT.Copy).then_inc(acts_hi, 1)
                elif n == WO:
                    attention_1()
                elif n == MIX_A:
                    act.wait_ge(row_sums, 1)
                    act.wait_ge(f_lo, 32)
                    A(RSB, misc[:, :, :].rearrange("p a (b c) -> p (a b) c", c=P), ACT.Copy)\
                        .then_inc(row_copied, 1)
                    act.wait_ge(acts_lo, SET[8])
                    A(X[:, :, :], X[:, :, :], ACT.Copy, scale=ALPHA).then_inc(x_scaled, 1)
                elif n == MIX_B:
                    squares(5, X, H, lambda k: act.wait_ge(centred, 8 + k + 1))
                    rstd(5)
                    biased_hi(5, 8, lambda k: shift3[:, 0, k:k + 1], H, 0, 56)
                elif n == B_OUT:
                    attention_2()

            act.wait_ge(params_loaded, 32)
            A(cond_t[:, :], col[:, COLS["c"]:COLS["c"] + 24], ACT.Tanh, scale=0.5)\
                .then_inc(cond_tanh, 1)
            A(half_b[:, 0:8], cl("conv_b_in", 8, 8), ACT.Copy, scale=0.5).then_inc(half_ready, 1)
            A(half_b[:, 8:16], cl("conv_ln_b", 0, 8), ACT.Copy, scale=0.5).then_inc(half_ready, 1)
            A(half_b[:, 16:24], cl("ln_b_2", 0, 8), ACT.Copy, scale=ALPHA).then_inc(half_ready, 1)
            act.wait_ge(half_ready, 3)
            build_diags(0, DIAGS)
            act.wait_ge(x_loaded, 16)
            squares(0, X, H, lambda k: None)
            rstd(0)
            for s in range(NW + 2):
                if s - 1 == A_OUT_2:
                    drain(s - 2)
                if s < NW:
                    split_hi(s)
                if s == 0:
                    boundary(0)
                if s >= 2 and s - 1 != A_OUT_2:
                    drain(s - 2)
                if s == MIX_B + 2:
                    squares(6, C, H2, lambda k: act.wait_ge(centred, 16 + k + 1))
                if s == MIX_B + 3:
                    rstd(6)
                if s in (MIX_B + 4, MIX_B + 5):
                    a = 4 * (s - (MIX_B + 4))
                    biased_hi(6, 9, lambda k: shift3[:, 1, k:k + 1], H2, T, 64, range(a, a + 4))
                if 0 <= s - CTX_AT < 4:
                    act.wait_ge(mod_step, MOD_DONE[VEC[2, 0, 1]])
                    act.wait_ge(ctx_loaded, 16)
                    modulated_hi(1, C, T, (2 * (s - CTX_AT), 2 * (s - CTX_AT) + 1))
                if s == CTX_AT + 4:
                    act.wait_ge(acts_lo, SET[7])
                    A(C[:, :, :], C[:, :, :], ACT.Copy, scale=ALPHA).then_inc(x_scaled, 1)
                    act.wait_ge(unit_done, UNITS.index(("w1", 1, 3, 3)) + 1)
                if 0 <= s - (CTX_AT + 4) < 4:
                    j = s - (CTX_AT + 4)
                    act.wait_ge(x_updated, XU_A - 8 + 2 * (j + 1))
                    modulated_hi(0, X, 0, (2 * j, 2 * j + 1))
                if s > 1 and s - 1 in FIRST_OF_SET:
                    boundary(s - 1)
            squares(7, X, H, lambda k: act.wait_ge(centred, 24 + k + 1))
            rstd(7)
            for k in range(KT):
                act.wait_ge(h_scaled, 72 + k + 1)
                A(H[:, k, :], H[:, k, :], ACT.Identity, bias=cl("ln_b_2", 8 + k)).then_inc(h_final, 1)

        @block.vector
        def _(dve):
            vec = nc.vector
            stt, ts, tt = vec.scalar_tensor_tensor, vec.tensor_scalar, vec.tensor_tensor
            count = {"acc": 0, "x": 0, "mod": 0}
            acc_last = {}

            def split_lo(w):
                n = WHERE[w]
                dve.wait_ge(weight_hi, w + 1)
                tt(w_lo[:, w % SPLITS, :, :].rearrange("p k c -> p (k c)"), raw[:, n % RING, :],
                   w_hi[:, w % SPLITS, :, :].rearrange("p k c -> p (k c)").bitcast(F32),
                   ALU.subtract).then_inc(unit_consumed, 1)

            def accumulate(n):
                _, vi, quarter = STREAM[n]
                block_no = VECTORS[vi][0]
                dve.wait_ge(slot_loaded[n % RING], 16 * (n // RING + 1))
                sums = [(vi % 2, 0)] if block_no == 1 else [(0, 8), (1, 16)]
                if quarter == 0 and vi >= 2:
                    both = 2 in (block_no, VECTORS[vi - 1][0])
                    dve.wait_ge(acc_reduced, vi if both else vi - 1)
                for i in range(2):
                    k = 2 * quarter + i
                    for b, c0 in sums:
                        src = raw[:, n % RING, i * D:(i + 1) * D]
                        c = cond[:, c0 + k:c0 + k + 1]
                        if k == 0:
                            ins = ts(acc[:, b, :], src, c, None, ALU.mult)
                        else:
                            s, v = acc_last[b]
                            dve.wait_ge(s, v)
                            ins = stt(out=acc[:, b, :], in0=src, scalar=c, in1=acc[:, b, :],
                                      op0=ALU.mult, op1=ALU.add)
                        if i == 1 and b == sums[-1][0]:
                            ins.then_inc(unit_consumed, 1)
                            acc_last[b] = (unit_consumed, n + 1)
                        else:
                            ins.then_inc(acc_step, 1)
                            count["acc"] += 1
                            acc_last[b] = (acc_step, count["acc"])

            def step(ins):
                ins.then_inc(mod_step, 1)
                count["mod"] += 1

            def finish_vector(vi):
                block_no, layer, part = VECTORS[vi]
                dve.wait_ge(acc_reduced, vi + 1)
                if block_no == 1:
                    got = misc[:, 1, 0:8]
                    m = mod1[:, 6 * layer + part, :]
                    b = cl("ada_b", 8 * (6 * layer + part), 8)
                    if part in (1, 4):
                        step(stt(out=m, in0=got, scalar=1.0, in1=b, op0=ALU.add, op1=ALU.add))
                        dve.wait_ge(mod_step, count["mod"])
                        step(tt(m, m, cl("mix_g" if part == 1 else "mlp_g", 8 * layer, 8), ALU.mult))
                    else:
                        step(tt(m, got, b, ALU.add))
                    if layer == 0 and part == 2:
                        dve.wait_ge(mod_step, count["mod"])
                        step(tt(gate_b[:, :], m, cl("conv_b_out", 0, 8), ALU.mult))
                else:
                    for i in range(2):
                        got = misc[:, 1, 8 * i:8 * i + 8]
                        b = cl("ada_b_2", 8 * (3 * layer + part), 8)
                        step(stt(out=mod2[:, 3 * layer + part, i, :], in0=got,
                                 scalar=1.0 if part == 1 else 0.0, in1=b, op0=ALU.add, op1=ALU.add))
                    if (layer, part) == (1, 1):
                        dve.wait_ge(mod_step, count["mod"])
                        for i in range(2):
                            step(tt(gain3[:, i, :], mod2[:, 4, i, :], cl("ln_g_2", 0, 8), ALU.mult))
                        for i in range(2):
                            step(tt(shift3[:, i, :], mod2[:, 4, i, :], cl("ln_b_2", 0, 8), ALU.mult))
                        dve.wait_ge(mod_step, count["mod"])
                        for i in range(2):
                            step(tt(shift3[:, i, :], shift3[:, i, :], mod2[:, 3, i, :], ALU.add))
                assert count["mod"] == MOD_DONE[vi]

            def update_x(ins_of):
                if count["x"] >= 1:
                    dve.wait_ge(x_updated, max(1, count["x"] - 7))
                ins_of().then_inc(x_updated, 1)
                count["x"] += 1

            def centre(n, src):
                m = LN_INDEX[n]
                mu, _, _, bank = stat_rows(n)
                dve.wait_ge(stat_done, MEAN_DONE[n])
                ts(mu, bank[:, T:2 * T], 1.0 / D, None, ALU.mult).then_inc(mean_ready, 1)
                dve.wait_ge(mean_ready, m + 1)
                for k in range(KT):
                    tt(src[:, k, :], src[:, k, :], mu, ALU.subtract).then_inc(centred, 1)

            def variance(n, eps):
                _, var, _, bank = stat_rows(n)
                dve.wait_ge(stat_done, STAT_DONE[n])
                ts(var, bank[:, 0:T], 1.0 / D, eps, ALU.mult, ALU.add).then_inc(var_prep, 1)
                dve.wait_ge(var_prep, 2 * n + 1)
                vec.reciprocal(var, var).then_inc(var_prep, 1)

            def scale_tile(n, k, src, dst, gain):
                stt(out=dst[:, k, :], in0=src[:, k, :], scalar=gain(k), in1=stat_rows(n)[2],
                    op0=ALU.mult, op1=ALU.mult).then_inc(h_scaled, 1)

            def scale_and_split(n, s, src, dst, gain, bias, c=0, a=0, b=KT):
                dve.wait_ge(rstd_ready, n + 1)
                for k in range(a, b + 1):
                    if k < b:
                        scale_tile(n, k, src, dst, gain)
                    if k >= a + 1:
                        dve.wait_ge(acts_hi, SET[s] + k)
                        stt(out=XL[:, k - 1, c:c + T], in0=dst[:, k - 1, :], scalar=bias(k - 1),
                            in1=XH[:, k - 1, c:c + T].bitcast(F32), op0=ALU.add, op1=ALU.subtract)\
                            .then_inc(acts_lo, 1)

            def modulate_and_split(s, m, src, c, first, a):
                for k in range(a, a + 3):
                    if k < a + 2:
                        ts(H[:, k, :], src[:, k, :], mod2[:, 1, m, k:k + 1],
                           mod2[:, 0, m, k:k + 1], ALU.mult, ALU.add).then_inc(h_scaled, 1)
                    if k >= a + 1:
                        dve.wait_ge(h_scaled, first + k)
                        dve.wait_ge(acts_hi, SET[s] + k)
                        tt(XL[:, k - 1, c:c + T], H[:, k - 1, :], XH[:, k - 1, c:c + T].bitcast(F32),
                           ALU.subtract).then_inc(acts_lo, 1)

            def conv_taps(a, b):
                for n in range(a, b):
                    j, tap, i = n // (2 * TAPS), n // 2 % TAPS, n % 2
                    k = 2 * j + i
                    d = cl("conv_dw", 8 * tap + k)
                    if tap == 0:
                        ins = ts(CV[:, k, :], U[:, k, 0:T], d, cl("conv_dw_b", k),
                                 ALU.mult, ALU.add)
                    else:
                        dve.wait_ge(conv_step, n - 1)
                        ins = stt(out=CV[:, k, :], in0=U[:, k, tap:tap + T], scalar=d,
                                  in1=CV[:, k, :], op0=ALU.mult, op1=ALU.add)
                    ins.then_inc(conv_step, 1)

            def drain(w):
                u = UNITS[w]
                kind = u[0]
                if kind == "conv_a":
                    return
                e = EV[:, w % 2, :]
                ei = e.rearrange("p (i t) -> p i t", i=2)
                if kind == "conv_g":
                    j = u[1]
                    g = EV[:, j % 2, :]
                    dve.wait_ge(gate_tanh, 2 * (j + 1))
                    ts(g, g, 0.5, 0.5, ALU.mult, ALU.add).then_inc(gate_half, 1)
                    dve.wait_ge(gate_half, j + 1)
                    for i in range(2):
                        k = 2 * j + i
                        ins = stt(out=U[:, k, PAD:PAD + T], in0=tiles(w - 1, T)[:, i, :],
                                  scalar=cl("conv_b_in", k), in1=g[:, i * T:(i + 1) * T],
                                  op0=ALU.add, op1=ALU.mult)
                    ins.then_inc(drained["dve"], 1)
                elif kind == "conv_out":
                    j = u[1]
                    for i in range(2):
                        k = 2 * j + i
                        dve.wait_ge(y_ready, k + 1)
                        update_x(lambda: tt(X[:, k, :], X[:, k, :], e[:, i * T:(i + 1) * T],
                                                  ALU.add))
                elif kind == "w1":
                    f = f_index(w)
                    dve.wait_ge(f_hi, f + 1)
                    fl = F_lo[:, u[2] % 2, 2 * u[3]:2 * u[3] + 2, :]
                    fh = F_hi[:, u[2] % 2, 2 * u[3]:2 * u[3] + 2, :]
                    tt(fl, ei, fh.bitcast(F32), ALU.subtract).then_inc(f_lo, 1)
                elif kind in ("w2", "wo", "b_out"):
                    gate = {"w2": (1, u[1], 5), "wo": (1, 1, 2), "b_out": (2, 1, 2)}[kind]
                    dve.wait_ge(mod_step, MOD_DONE[VEC[gate]])
                    dve.wait_ge(unit_done, w + 1)
                    j = u[-1]
                    for i in range(2):
                        k = 2 * j + i
                        if kind == "w2":
                            g = mod1[:, 6 * u[1] + 5, k:k + 1]
                        elif kind == "wo":
                            g = mod1[:, 8, k:k + 1]
                        else:
                            g = mod2[:, 5, 0, k:k + 1]
                            dve.wait_ge(x_scaled, 2 + KT)
                        update_x(lambda: stt(out=X[:, k, :], in0=tiles(w, T)[:, i, :],
                                                   scalar=g, in1=X[:, k, :], op0=ALU.mult,
                                                   op1=ALU.add))
                elif kind in ("k", "v"):
                    qk_norm(w)
                elif kind == "a_v":
                    j = u[1]
                    dve.wait_ge(drained["act"], DRAINED[w][1])
                    for t in range(4):
                        vec.bn_stats(bst[:, t, j, :], VA[:, t, UC * j:UC * (j + 1)])\
                            .then_inc(v_stats, 1)
                    if j == 7:
                        norm_values()
                elif kind == "a_u":
                    if u[1]:
                        mix_values(u[1])
                elif kind == "a_z":
                    if u[1] == 0:
                        mix_values(0)
                    mix_gates(u[1], w)
                elif kind == "a_out":
                    half, j = u[1], u[2]
                    dve.wait_ge(mod_step, MOD_DONE[VEC[2, 0, 2]])
                    dve.wait_ge(unit_done, w + 1)
                    dve.wait_ge(x_scaled, 2)
                    for m, buf in enumerate((X, C)):
                        for i in range(2):
                            k = 2 * j + i
                            update_x(lambda: stt(
                                out=buf[:, k, :], in0=tiles(w, 2 * T)[:, i, m * T:(m + 1) * T],
                                scalar=mod2[:, 2, m, k:k + 1], in1=buf[:, k, :],
                                op0=ALU.mult, op1=ALU.add))
                elif kind == "b_z":
                    j = u[1]
                    dve.wait_ge(z_tanh, j + 1)
                    ts(e, e, 0.5, 0.5, ALU.mult, ALU.add).then_inc(z_half, 1)
                    dve.wait_ge(z_half, j + 1)
                    tt(SZ[:, 2 * j:2 * j + 2, :], tiles(w, T), ei, ALU.mult)\
                        .then_inc(drained["dve"], 1)
                    if j >= 1:
                        roped_tiles_lo(j - 1, j if j < 3 else 4)
                    rope(0, Q[:, 2 * j:2 * j + 2, :], j + (j > 2))
                    if j == 2:
                        rope(1, K2[:, :, 0:T], 3)

            def rope(bank, dst, index):
                dve.wait_ge(tables_loaded, 32)
                dve.wait_ge(turned, index + 1)
                r = HT[:, 0:512].rearrange("p (i t) -> p i t", i=2)
                s2 = sin_t.unsqueeze(1).broadcast_to([P, 2, T])
                c2 = cos_t.unsqueeze(1).broadcast_to([P, 2, T])
                tt(r, misc[:, bank, :].rearrange("p (i t) -> p i t", i=2), s2, ALU.mult)\
                    .then_inc(roped, 1)
                tt(dst, dst, c2, ALU.mult).then_inc(roped, 1)
                dve.wait_ge(roped, 3 * index + 2)
                tt(dst, dst, r, ALU.add).then_inc(roped, 1)
                dve.wait_ge(roped, 3 * index + 3)

            def roped_tiles_lo(a, b):
                for n in range(a, b):
                    src, hi, lo = ROPED[n]
                    dve.wait_ge(roped_hi, n + 1)
                    tt(lo, src, hi.bitcast(F32), ALU.subtract).then_inc(roped_lo, 1)

            def qk_norm(w):
                if w == QKV + 5:
                    dve.wait_ge(q_sum, 1)
                    r = rq[:, :, :].rearrange("p t h -> p (t h)")
                    ts(r, misc[:, 0, 0:2 * HEADS], 1.0 / DH, EPS, ALU.mult, ALU.add)\
                        .then_inc(q_prep, 1)
                    dve.wait_ge(q_prep, 1)
                    vec.reciprocal(r, r).then_inc(q_prep, 1)
                if w == QKV + 6:
                    dve.wait_ge(q_rstd, 1)
                    for t in range(2):
                        tt(rq[:, t, :], rq[:, t, :], slopes, ALU.mult).then_inc(q_prep, 1)
                if w == QKV + 8:
                    dve.wait_ge(k_sum, 1)
                    ts(rk, misc[0:HEADS, 0, 0:T], 1.0 / DH, EPS, ALU.mult, ALU.add).then_inc(k_prep, 1)
                    dve.wait_ge(k_prep, 1)
                    vec.reciprocal(rk, rk).then_inc(k_prep, 1)
                if w in (QKV + 9, QKV + 10):
                    for b in range(2):
                        n = 2 * (w - (QKV + 9)) + b
                        dve.wait_ge(k_spread, n + 1)
                        dst = K1[:, 2 * n:2 * n + 2, :]
                        stt(out=dst, in0=dst, scalar=gqk[:, 0:1],
                            in1=misc[:, b, :].rearrange("p (i t) -> p i t", i=2), op0=ALU.mult,
                            op1=ALU.mult).then_inc(k_final, 1)

            def norm_values():
                dve.wait_ge(v_stats, 32)
                for t in range(4):
                    vec.bn_aggr(mv[:, t, :], bst[:, t, :, :]).then_inc(v_prep, 1)
                dve.wait_ge(v_prep, 4)
                ts(vr[:, :], mv[:, :, 1], LN_EPS, None, ALU.add).then_inc(v_prep, 1)
                dve.wait_ge(v_prep, 5)
                vec.reciprocal(vr[:, :], vr[:, :]).then_inc(v_prep, 1)
                dve.wait_ge(v_rstd, 1)
                for t in range(4):
                    ts(VA[:, t, :], VA[:, t, :], mv[:, t, 0:1], vr[:, t:t + 1], ALU.subtract,
                       ALU.mult).then_inc(v_normed, 1)

            def mix_values(j):
                n = 7 * j
                for i in range(2):
                    stt(out=RR[:, i, :], in0=RSB[:, j, :], scalar=cl("a_ln_b", 2 * j + i),
                        in1=BS[:, j, :], op0=ALU.mult, op1=ALU.add).then_inc(g_dve, 1)
                dve.wait_ge(g_dve, n + 2)
                dve.wait_ge(mixed, j + 1)
                for i in range(2):
                    stt(out=SM[:, i, :].rearrange("p (c q) -> p c q", c=4),
                        in0=misc[:, i, :].rearrange("p (c q) -> p c q", c=4),
                        scalar=cl("a_ln_g", 2 * j + i),
                        in1=RR[:, i, :].unsqueeze(1).broadcast_to([P, 4, P]),
                        op0=ALU.mult, op1=ALU.add).then_inc(g_dve, 1)
                dve.wait_ge(g_dve, n + 4)
                w = UNITS.index(("a_u", j))
                dve.wait_ge(drained["act"], DRAINED[w][1])
                g = GU[j % 2]
                tt(g, g, SM[:, :, :].rearrange("p i t -> p (i t)"), ALU.mult).then_inc(g_dve, 1)

            def mix_gates(j, w):
                n = 7 * j
                g = GU[j % 2]
                dve.wait_ge(g_act, j + 1)
                ts(TZ, TZ, 0.5, 0.5, ALU.mult, ALU.add).then_inc(g_dve, 1)
                dve.wait_ge(g_dve, n + 6)
                tt(TZ, pair(w), TZ, ALU.mult).then_inc(drained["dve"], 1)
                dve.wait_ge(drained["dve"], DRAINED[w][1])
                tt(g, g, TZ, ALU.mult).then_inc(g_dve, 1)
                dve.wait_ge(g_dve, n + 7)
                dve.wait_ge(g_hi, j + 1)
                k = 2 * (j % 4)
                tt(G_lo[:, k:k + 2, :], g.rearrange("p (i t) -> p i t", i=2),
                   G_hi[:, k:k + 2, :].bitcast(F32), ALU.subtract).then_inc(g_lo, 1)

            def attention_1():
                dve.wait_ge(params_loaded, 112)
                for i in range(HEADS + 6):
                    if i < HEADS:
                        slope = 2.0 ** (-8.0 * (i + 1) / HEADS)
                        b = i % 3
                        dve.wait_ge(scored, i + 1)
                        if i >= 3:
                            dve.wait_ge(p_turned, i - 2)
                        o = 512 * (i % 2)
                        for t, (a, c) in enumerate(((0, P), (P, 3 * P))):
                            stt(out=S1[:, b, a:c], in0=prod[:, 0, o + a:o + c],
                                scalar=rq[:, t, i:i + 1], in1=alibi[:, a:c], op0=ALU.mult,
                                op1=ALU.add).then_inc(z_ready, 1)
                    if 1 <= i <= HEADS:
                        h = i - 1
                        dve.wait_ge(exp_done, 2 * (h + 1))
                        vec.reciprocal(sm[:, h % 3, 6:8], sm[:, h % 3, 4:6]).then_inc(p_ready, 1)
                    if i < HEADS:
                        dve.wait_ge(z_ready, 2 * (i + 1))
                        vec.reduce_max(sm[:, b, 0:1], S1[:, b, 0:P], AX).then_inc(max_ready, 1)
                        vec.reduce_max(sm[:, b, 1:2], S1[:, b, P:3 * P], AX).then_inc(max_ready, 1)
                    for t, (a, c) in enumerate(((0, P), (P, 3 * P))):
                        if 1 <= i <= HEADS:
                            h = i - 1
                            dve.wait_ge(p_ready, 3 * h + 1)
                            ts(S1[:, h % 3, a:c], S1[:, h % 3, a:c], sm[:, h % 3, 6 + t:7 + t], None,
                               ALU.mult).then_inc(p_ready, 1)
                        if i < HEADS and t == 0:
                            dve.wait_ge(max_ready, 3 * i + 2)
                            ts(sm[:, b, 2:4], sm[:, b, 0:2], -slope, None, ALU.mult)\
                                .then_inc(max_ready, 1)
                    if i >= 7 and i % 2 == 1:
                        k = (i - 7) // 2
                        dve.wait_ge(acts_hi, SET[4] + k + 1)
                        tt(XL[:, k, 0:T], prod[:, 2, 512 * (k % 2):512 * (k % 2) + T],
                           XH[:, k, 0:T].bitcast(F32), ALU.subtract).then_inc(acts_lo, 1)

            def attention_2():
                NI = 2 * HEADS
                for i in range(NI + 6):
                    if i == 2:
                        roped_tiles_lo(4, 5)
                    if i < NI:
                        b = i % 3
                        dve.wait_ge(scored, HEADS + i + 1)
                        if i >= 3:
                            dve.wait_ge(p_turned, HEADS + i - 2)
                        vec.tensor_tensor_reduce(S2[:, b, :], prod[:, 0, 512 * (i % 2):512 * (i % 2) + 512],
                                                 window[:, i % 2, :], SCALE, cl("sink", head_of(i)),
                                                 ALU.add, ALU.max, sm[:, b, 0:1]).then_inc(max_ready, 1)
                    if 1 <= i <= NI:
                        e = (i - 1) % 3
                        dve.wait_ge(exp_done, 2 * HEADS + 2 * i)
                        tt(sm[:, e, 6:7], sm[:, e, 4:5], sm[:, e, 5:6], ALU.add)\
                            .then_inc(p_ready, 1)
                    if i < NI:
                        dve.wait_ge(max_ready, 3 * HEADS + 2 * i + 1)
                        ts(sm[:, b, 2:3], sm[:, b, 0:1], -1.0, None, ALU.mult)\
                            .then_inc(max_ready, 1)
                    if 1 <= i <= NI:
                        h = i - 1
                        b = h % 3
                        n = 3 * HEADS + 3 * h
                        dve.wait_ge(p_ready, n + 1)
                        vec.reciprocal(sm[:, b, 7:8], sm[:, b, 6:7]).then_inc(p_ready, 1)
                        dve.wait_ge(p_ready, n + 2)
                        ts(S2[:, b, :], S2[:, b, :], sm[:, b, 7:8], None, ALU.mult)\
                            .then_inc(p_ready, 1)
                    if 2 <= i < 2 + KT:
                        k = i - 2
                        stt(out=X[:, k, :], in0=X[:, k, :], scalar=cl("ln_g_2", k),
                            in1=stat_rows(5)[2], op0=ALU.mult, op1=ALU.mult)\
                            .then_inc(x_restored, 1)
                    if i >= 8 and i % 4 == 0:
                        k = (i - 8) // 4
                        dve.wait_ge(head_out, HEADS + 4 * (k + 1))
                        tt(H[:, k, :], prod[:, 2, 512 * (k % 2):512 * (k % 2) + T], SZ[:, k, :],
                           ALU.mult).then_inc(o_gated, 1)
                    if i >= 9 and i % 4 == 1:
                        k = (i - 9) // 4
                        dve.wait_ge(acts_hi, SET[10] + k + 1)
                        tt(XL[:, k, 0:T], H[:, k, :], XH[:, k, 0:T].bitcast(F32), ALU.subtract)\
                            .then_inc(acts_lo, 1)

            def boundary(n):
                if n in (0, MLP0, QKV, MLP1):
                    i, s, scale, shift = {0: (0, 0, 1, 0), MLP0: (2, 2, 4, 3), QKV: (3, 3, 7, 6),
                                          MLP1: (4, 5, 10, 9)}[n]
                    if n:
                        variance(i, EPS)
                    scale_and_split(i, s, X, H, lambda k: mod1[:, scale, k:k + 1],
                                    lambda k: mod1[:, shift, k:k + 1])
                elif n == CONV_OUT:
                    conv_taps(CONV_EARLY * (CONV_OUT - 2), TAPS * CONV_PE)
                    for n in range(8):
                        accumulate(WHERE[CONV_OUT + 1] + 1 + n)
                    dve.wait_ge(conv_step, TAPS * CONV_PE)
                    centre(1, CV)
                    finish_vector(2)
                    variance(1, EPS)
                    finish_vector(3)
                    dve.wait_ge(rstd_ready, 2)
                    for k in range(KT + 3):
                        if k < KT:
                            scale_tile(1, k, CV, H, lambda k: cl("conv_ln_g", k))
                        if 1 <= k < KT + 1:
                            i = k - 1
                            dve.wait_ge(silu_tanh, i + 1)
                            ts(TS[:, i, :], TS[:, i, :], 0.5, 0.5, ALU.mult, ALU.add)\
                                .then_inc(silu_step, 1)
                            dve.wait_ge(silu_step, 2 * i + 1)
                            stt(out=TS[:, i, :], in0=H[:, i, :], scalar=cl("conv_ln_b", i),
                                in1=TS[:, i, :], op0=ALU.add, op1=ALU.mult).then_inc(silu_step, 1)
                        if k >= 3:
                            i = k - 3
                            dve.wait_ge(acts_hi, SET[1] + i + 1)
                            tt(XL[:, i, 0:T], TS[:, i, :], XH[:, i, 0:T].bitcast(F32),
                               ALU.subtract).then_inc(acts_lo, 1)
                elif n == WO:
                    attention_1()
                elif n == MIX_B:
                    centre(5, X)
                    variance(5, LN_EPS)
                    scale_and_split(5, 8, X, H, lambda k: gain3[:, 0, k:k + 1],
                                    lambda k: shift3[:, 0, k:k + 1])
                elif n == B_OUT:
                    attention_2()

            vec.memset(U[:, :, 0:PAD], 0.0).then_inc(padded, 1)
            dve.wait_ge(padded, 1)
            dve.wait_ge(params_loaded, 32)
            dve.wait_ge(cond_tanh, 1)
            ts(cond_t[:, :], cond_t[:, :], 0.5, 0.5, ALU.mult, ALU.add).then_inc(cond_ready, 1)
            dve.wait_ge(cond_ready, 1)
            tt(cond[:, :], cond_t[:, :], col[:, COLS["c"]:COLS["c"] + 24], ALU.mult)\
                .then_inc(cond_ready, 1)
            tt(gqk[:, :], cl("qn_g"), cl("kn_g"), ALU.mult).then_inc(cond_ready, 1)
            dve.wait_ge(cond_ready, 3)
            at = 0
            for s in range(NW + 2):
                if s - 1 == A_OUT_2 or s > 1 and s - 1 in FIRST_OF_SET:
                    drain(s - 2)
                if s < NW:
                    while at < WHERE[s]:
                        accumulate(at)
                        at += 1
                        if at == 5:
                            variance(0, EPS)
                        if at == 6:
                            finish_vector(0)
                    split_lo(s)
                    at += 1
                if s == 0:
                    finish_vector(1)
                    dve.wait_ge(mod_step, count["mod"])
                    boundary(0)
                if s >= 2:
                    if s - 1 != A_OUT_2 and s - 1 not in FIRST_OF_SET:
                        drain(s - 2)
                    for vi in REDUCE_AFTER.get(s - 2, []):
                        finish_vector(vi)
                if s == MIX_B + 2:
                    centre(6, C)
                if s == MIX_B + 3:
                    variance(6, LN_EPS)
                if s in (MIX_B + 4, MIX_B + 5):
                    a = 4 * (s - (MIX_B + 4))
                    scale_and_split(6, 9, C, H2, lambda k: gain3[:, 1, k:k + 1],
                                    lambda k: shift3[:, 1, k:k + 1], T, a, a + 4)
                if 3 <= s <= CONV_OUT:
                    dve.wait_ge(drained["dve"], DRAINED[1][1])
                    conv_taps(CONV_EARLY * (s - 3), CONV_EARLY * (s - 2))
                if s > 1 and s - 1 in FIRST_OF_SET:
                    dve.wait_ge(mod_step, max(1, count["mod"]))
                    dve.wait_ge(unit_done, s - 1)
                    boundary(s - 1)
                    if s - 1 == CONV_OUT:
                        at = WHERE[s + 1] - 2
                if 0 <= s - CTX_AT < 4:
                    dve.wait_ge(mod_step, MOD_DONE[VEC[2, 0, 1]])
                    dve.wait_ge(ctx_loaded, 16)
                    modulate_and_split(6, 1, C, T, 40, 2 * (s - CTX_AT))
                if 0 <= s - (CTX_AT + 4) < 4:
                    j = s - (CTX_AT + 4)
                    dve.wait_ge(x_updated, XU_A - 8 + 2 * (j + 1))
                    dve.wait_ge(unit_done, UNITS.index(("w1", 1, 3, 3)) + 1)
                    modulate_and_split(7, 0, X, 0, 48, 2 * j)
            centre(7, X)
            variance(7, LN_EPS)
            dve.wait_ge(rstd_ready, 8)
            for k in range(KT):
                scale_tile(7, k, X, H, lambda k: cl("ln_g_2", 8 + k))

        @block.tensor
        def _(pe):
            mm = nc.tensor.matmul

            def reduce_vector(vi):
                last = max(n for n, s in enumerate(STREAM) if s[0] == "mod" and s[1] == vi)
                pe.wait_ge(unit_consumed, last + 1)
                if vi:
                    pe.wait_ge(mod_step, MOD_DONE[vi - 1])
                reduced[0] = vi
                if vi == VEC[2, 0, 2]:
                    pe.wait_ge(row_copied, 1)
                if mixed_now[0]:
                    pe.wait_ge(g_dve, 7 * mixed_now[0] - 3)
                sums = [vi % 2] if VECTORS[vi][0] == 1 else [0, 1]
                for i, b in enumerate(sums):
                    for k in range(KT):
                        ins = mm(misc[:, 1, 8 * i + k:8 * i + k + 1], acc[:, b, P * k:P * (k + 1)],
                                 ones[:, 0:1], start=True, stop=True)
                ins.then_inc(acc_reduced, 1)

            def sum_tiles(bank, c, src, ready, which=range(KT)):
                for k in which:
                    ready(k)
                    ins = mm(misc[:, bank, c:c + T], ones, src[:, k, :], start=(k == 0),
                             stop=(k == KT - 1), skip_group_check=True)
                if k == KT - 1:
                    ins.then_inc(stat_done, 1)

            def sum_squares(n, src, which=range(KT)):
                sum_tiles(1 if n == 6 else 0, 0, src,
                          lambda k: pe.wait_ge(sq_ready, 8 * n + k + 1), which)

            def early_sums(n, j):
                which = (2 * j, 2 * j + 1)
                if n == 5:
                    if j == 0:
                        pe.wait_ge(mod_step, MOD_DONE[-1])
                    for m, src in enumerate((X, C)):
                        sum_tiles(m, T, src,
                                  lambda k: pe.wait_ge(x_updated, XU_A + 16 + 4 * (j + 1)), which)
                elif n == 7:
                    sum_tiles(0, T, X, lambda k: pe.wait_ge(x_updated, XU_B + k + 1), which)
                else:
                    sum_squares(n, H, which)

            def three(out, lhs_hi, lhs_lo, rhs_hi, rhs_lo, start, stop):
                mm(out, lhs_hi, rhs_hi, start=start, stop=False)
                mm(out, lhs_hi, rhs_lo, start=False, stop=False)
                return mm(out, lhs_lo, rhs_hi, start=False, stop=stop)

            def unit(w):
                u = UNITS[w]
                kind = u[0]
                pe.wait_ge(unit_consumed, WHERE[w] + 1)
                if w >= PAIRS:
                    who, n = DRAINED[w - PAIRS]
                    pe.wait_ge(drained[who], n)
                wh, wl = w_hi[:, w % SPLITS], w_lo[:, w % SPLITS]
                s = FIRST_OF_SET.get(w)
                if w in (WO, B_OUT):
                    pe.wait_ge(acts_lo, SET[s + 1])

                if kind == "b_k":
                    pe.wait_ge(acts_lo, SET[10])

                def ready(k):
                    if s is not None:
                        pe.wait_ge(acts_lo, SET[s] + k + 1)

                if kind in ("v", "a_v", "b_v"):
                    nt = 2 if kind == "v" else 4
                    order = [(t, k) for t in range(nt) for k in range(KT)]
                    if s is not None:
                        order = [(t, k) for a in range(2) for k in range(KT) for t in (a, a + 2)]
                    for t, k in order:
                        if t == 0:
                            ready(k)
                        ins = three(pair(w)[:, t * UC:(t + 1) * UC],
                                    XH[:, k, t * P:(t + 1) * P], XL[:, k, t * P:(t + 1) * P],
                                    wh[:, k, :], wl[:, k, :], k == 0, k == KT - 1)
                else:
                    if kind == "w2":
                        pe.wait_ge(f_lo, 16 * u[1] + 4 * (u[2] + 1))
                        hi, lo, nt = F_hi[:, u[2] % 2], F_lo[:, u[2] % 2], T
                    elif kind == "a_out":
                        pe.wait_ge(g_lo, 4 * (u[1] + 1) - (u[2] == 0))
                        hi, lo, nt = G_hi, G_lo, 2 * T
                    else:
                        nt = 2 * T if kind in ("a_u", "a_z", "b_k") else T
                        hi, lo = XH, XL
                    order = [(i, k) for i in range(2) for k in range(KT)]
                    if s is not None or u[-1] == 0:
                        order = [(i, k) for k in range(KT) for i in range(2)]
                    for i, k in order:
                        if i == 0:
                            ready(k)
                        if kind == "a_out" and u[2] == 0 and (i, k) == (0, 6):
                            pe.wait_ge(g_lo, 4 * (u[1] + 1))
                        ins = three(tiles(w, nt)[:, i, :], wh[:, k, P * i:P * (i + 1)],
                                    wl[:, k, P * i:P * (i + 1)], hi[:, k, 0:nt], lo[:, k, 0:nt],
                                    k == 0, k == KT - 1)
                ins.then_inc(unit_done, 1)

            mixed_now = [0]
            reduced = [0]

            def after(w):
                kind = UNITS[w][0]
                if w == QKV + 5:
                    pe.wait_ge(drained["act"], DRAINED[QKV + 3][1])
                    pe.wait_ge(acts_lo, SET[4])
                    for t in range(2):
                        for k in range(KT):
                            c = HEADS * t + 2 * k
                            ins = mm(misc[:, 0, c:c + 2], H[:, k, P * t:P * (t + 1)],
                                     head_ones[:, 0:P:DH], start=True, stop=True)
                    ins.then_inc(q_sum, 1)
                if w == QKV + 8:
                    pe.wait_ge(params_loaded, 112)
                    pe.wait_ge(drained["act"], DRAINED[QKV + 7][1])
                    pe.wait_ge(q_prep, 1)
                    for k in range(KT):
                        ins = mm(misc[0:HEADS, 0, 0:T], by_head[:, HEADS * k:HEADS * (k + 1)],
                                 C[:, k, :], start=(k == 0), stop=(k == KT - 1))
                    ins.then_inc(k_sum, 1)
                if w in (QKV + 9, QKV + 10):
                    pe.wait_ge(k_rstd, 1)
                    pe.wait_ge(mod_step, MOD_DONE[reduced[0]])
                    for b in range(2):
                        n = 2 * (w - (QKV + 9)) + b
                        if n >= 2:
                            pe.wait_ge(k_final, n - 1)
                        for i in range(2):
                            k = 2 * n + i
                            ins = mm(misc[:, b, T * i:T * (i + 1)], spread[:, P * k:P * (k + 1)], rk,
                                     start=True, stop=True)
                        ins.then_inc(k_spread, 1)
                if (kind == "a_u" and UNITS[w][1]) or UNITS[w] == ("a_z", 0):
                    j = UNITS[w][1]
                    pe.wait_ge(v_normed, 4)
                    pe.wait_ge(mod_step, MOD_DONE[reduced[0]])
                    if j >= 1:
                        pe.wait_ge(g_dve, 7 * (j - 1) + 4)
                    for i in range(2):
                        for t in range(4):
                            c = UC * j + P * i
                            ins = mm(misc[:, i, P * t:P * (t + 1)], VA[:, t, c:c + P], WS[:, j, :],
                                     start=True, stop=True)
                    ins.then_inc(mixed, 1)
                    mixed_now[0] = j + 1
                if kind == "b_z":
                    j = UNITS[w][1]
                    if j == 0:
                        pe.wait_ge(drained["act"], DRAINED[MIX_B + 3][1])
                    else:
                        pe.wait_ge(roped, 3 * (j - 1) + 1)
                    mm(misc[:, 0, :], perm, Q[:, 2 * j:2 * j + 2, :], start=True, stop=True)\
                        .then_inc(turned, 1)
                    if j == 2:
                        pe.wait_ge(drained["act"], DRAINED[UNITS.index(("b_v", 0))][1])
                        mm(misc[:, 1, :], perm, K2[:, :, 0:T], start=True, stop=True)\
                            .then_inc(turned, 1)

            def attention_1():
                pe.wait_ge(k_final, 4)
                pe.wait_ge(q_prep, 4)
                pe.wait_ge(drained["act"], DRAINED[WO - 1][1])
                for i in range(HEADS + 4):
                    if i < HEADS:
                        k, r = i // 2, 64 * (i % 2)
                        if i >= 2:
                            pe.wait_ge(z_ready, 2 * (i - 1))
                        o = 512 * (i % 2)
                        q = Q[r:r + DH, k, :]
                        mm(prod[:, 0, o:o + P], q[:, 0:P], K1[r:r + DH, k, 0:P], start=True, stop=True)
                        mm(prod[:, 0, o + P:o + 3 * P], q[:, P:2 * P], K1[r:r + DH, k, :],
                           start=True, stop=True).then_inc(scored, 1)
                    if i >= 4:
                        h = i - 4
                        k, r, b = h // 2, 64 * (h % 2), h % 2
                        pe.wait_ge(pt_copied, h + 1)
                        if k >= 2:
                            pe.wait_ge(acts_lo, SET[4] + k - 1)
                        o = 512 * (k % 2)
                        v = V1[:, :, DH * h:DH * (h + 1)]
                        mm(prod[r:r + DH, 2, o:o + P], v[:, 0, :], PT1[:, b, 0:P], start=True, stop=True)
                        mm(prod[r:r + DH, 2, o + P:o + T], v[:, 0, :], PT1[:, b, P:2 * P],
                           start=True, stop=False)
                        mm(prod[r:r + DH, 2, o + P:o + T], v[:, 1, :], PT1[:, b, 2 * P:3 * P],
                           start=False, stop=True).then_inc(head_out, 1)
                    if 2 <= i < HEADS + 2:
                        h = i - 2
                        pe.wait_ge(p_ready, 3 * (h + 1))
                        if h >= 2:
                            pe.wait_ge(pt_copied, h - 1)
                        turn(S1[:, h % 3, :], h % 2, 3)

            def turn(src, b, n):
                for c in range(n):
                    ins = nc.tensor.transpose(prod[:, 1, 512 * b + P * c:512 * b + P * (c + 1)],
                                              src[:, P * c:P * (c + 1)], ident)
                ins.then_inc(p_turned, 1)

            def attention_2():
                NI = 2 * HEADS
                pe.wait_ge(drained["dve"], DRAINED[B_OUT - 1][1])
                for i in range(NI + 4):
                    if i < NI:
                        k, off, t = i // 4, (i // 2) % 2, i % 2
                        r, b = 64 * off, i % 2
                        if i >= 2:
                            pe.wait_ge(max_ready, 3 * HEADS + 2 * (i - 2) + 1)
                        if i in (0, 4 * (KT - 2)):
                            pe.wait_ge(roped_lo, 4 if i == 0 else 5)
                        q_at = (slice(r, r + DH), k, slice(P * t, P * (t + 1)))
                        k_at = (slice(r, r + DH), k // 4)
                        three(prod[:, 0, 512 * b:512 * b + 512], Q_hi[q_at], Q_lo[q_at],
                              K_hi[k_at], K_lo[k_at], True, True).then_inc(scored, 1)
                    if i >= 4:
                        h = i - 4
                        k, off, t, b = h // 4, (h // 2) % 2, h % 2, h % 2
                        r = 64 * off
                        g = 2 * (k // 4) + off
                        pe.wait_ge(pt_copied, HEADS + h + 1)
                        if k >= 2:
                            pe.wait_ge(o_gated, k - 1)
                        o = 512 * (k % 2) + P * t
                        for c in range(4):
                            ins = mm(prod[r:r + DH, 2, o:o + P], V2[:, c, DH * g:DH * (g + 1)],
                                     PT2[:, b, P * c:P * (c + 1)], start=(c == 0), stop=(c == 3))
                        ins.then_inc(head_out, 1)
                    if 2 <= i < NI + 2:
                        h = i - 2
                        pe.wait_ge(p_ready, 3 * HEADS + 3 * (h + 1))
                        if h >= 2:
                            pe.wait_ge(pt_copied, HEADS + h - 1)
                        turn(S2[:, h % 3, :], h % 2, 4)

            def boundary(n):
                if n in (MLP0, QKV, MLP1):
                    for j in (2, 3):
                        early_sums({MLP0: 2, QKV: 3, MLP1: 4}[n], j)
                elif n == CONV_OUT:
                    pe.wait_ge(drained["dve"], DRAINED[n - 1][1])
                    for i in range(NDIAG):
                        k, tap = CONV_PE + i // TAPS, i % TAPS
                        if i % DIAG_GROUP == 0:
                            pe.wait_ge(diag_ready, min(i + DIAG_GROUP, NDIAG))
                        ins = mm(conv_bank(k), DG[:, i % DIAGS, :], U[:, k, tap:tap + T],
                                 start=(tap == 0), stop=(tap == TAPS - 1))
                        if tap == TAPS - 1:
                            ins.then_inc(conv_summed, 1)
                        if i % DIAG_GROUP == DIAG_GROUP - 1:
                            assert tap != TAPS - 1
                            ins.then_inc(diag_used, 1)
                    sum_tiles(0, T, CV, lambda k: pe.wait_ge(conv_step, 2 * TAPS * (k // 2 + 1))
                              if k < CONV_PE else pe.wait_ge(conv_copied, k - CONV_PE + 1))
                    reduce_vector(2)
                    sum_squares(1, H)
                    reduce_vector(3)
                elif n == WO:
                    attention_1()
                elif n == MIX_A:
                    pe.wait_ge(params_loaded, 112)
                    pe.wait_ge(mod_step, MOD_DONE[reduced[0]])
                    for g in range(2):
                        ins = mm(misc[:, g, :], ones, WS[:, 4 * g:4 * (g + 1), :], start=True, stop=True)
                    ins.then_inc(row_sums, 1)
                elif n == MIX_B:
                    for j in (2, 3):
                        early_sums(5, j)
                    sum_squares(5, H)
                elif n == B_OUT:
                    attention_2()

            pe.wait_ge(params_loaded, 32)
            sum_squares(0, H)
            reduce_vector(0)
            reduce_vector(1)
            for w in range(NW):
                if w in FIRST_OF_SET:
                    boundary(w)
                unit(w)
                for vi in REDUCE_AFTER.get(w, []):
                    reduce_vector(vi)
                if w == MIX_B + 1:
                    sum_squares(6, H2)
                after(w)
                if w - 2 in LAST_UPDATE and LAST_UPDATE[w - 2][1] < 2:
                    early_sums(*LAST_UPDATE[w - 2])
            early_sums(7, 2)
            early_sums(7, 3)
            sum_squares(7, H)


def _unit(w, r0, c0):
    return w[r0:r0 + D, c0:c0 + UC].reshape(KT, P, UC).transpose(1, 0, 2).reshape(P, UNIT)


def _units(f):
    conv_in, conv_out, qkv, wo = f["conv_w_in"][0], f["conv_w_out"][0], f["attn_w_qkv"][0], f["attn_w_o"][0]
    a_in, a_out, b_in, b_out = f["a_w_in_2"][0], f["a_w_out_2"][0], f["b_w_in_2"][0], f["b_w_out_2"][0]
    order = [h for k in range(KT) for h in (4 * (2 * (k // 4)) + k % 4, 4 * (2 * (k // 4) + 1) + k % 4)]
    rows = np.concatenate([np.arange(DH * h, DH * (h + 1)) for h in order])
    bq = b_in[:, 0:D][:, rows]
    bz = b_in[:, D + 2 * UC:2 * D + 2 * UC][:, rows]
    bo = b_out[rows, :]
    A = 2 * D
    for u in UNITS:
        kind, j = u[0], u[-1]
        yield {
            "conv_a": lambda: _unit(conv_in, 0, UC * j),
            "conv_g": lambda: _unit(conv_in, 0, D + UC * j),
            "conv_out": lambda: _unit(conv_out, 0, UC * j),
            "w1": lambda: _unit(f["mlp_w1"][u[1]], 0, D * u[2] + UC * j),
            "w2": lambda: _unit(f["mlp_w2"][u[1]], D * u[2], UC * j),
            "q": lambda: _unit(qkv, 0, UC * j),
            "k": lambda: _unit(qkv, 0, D + UC * j),
            "v": lambda: _unit(qkv, 0, 2 * D + UC * j),
            "wo": lambda: _unit(wo, 0, UC * j),
            "a_u": lambda: _unit(a_in, 0, UC * j),
            "a_v": lambda: _unit(a_in, 0, A + UC * j),
            "a_z": lambda: _unit(a_in, 0, 2 * A + UC * j),
            "a_out": lambda: _unit(a_out, D * u[1], UC * j),
            "b_q": lambda: _unit(bq, 0, UC * j),
            "b_k": lambda: _unit(b_in, 0, D),
            "b_v": lambda: _unit(b_in, 0, D + UC),
            "b_z": lambda: _unit(bz, 0, UC * j),
            "b_out": lambda: _unit(bo, 0, UC * j),
        }[kind]()


def _stream(f):
    weights = list(_units(f))
    out = np.empty((NS, P, UNIT), np.float32)
    for n, s in enumerate(STREAM):
        if s[0] == "w":
            out[n] = weights[s[1]]
        else:
            block, layer, part = VECTORS[s[1]]
            w = f["ada_w" if block == 1 else "ada_w_2"][layer]
            rows = w[2 * P * s[2]:2 * P * (s[2] + 1), D * part:D * (part + 1)]
            out[n] = rows.reshape(2, P, D).transpose(1, 0, 2).reshape(P, UNIT)
    return out


def _columns(v):
    return v.reshape(-1, P).T


def _params(f):
    parts = {
        "c": f["c"][0], "c_2": f["c_2"][0], "c_ctx": f["c_ctx_2"], "ada_b": f["ada_b"],
        "ada_b_2": f["ada_b_2"], "mix_g": f["mix_norm_g"], "mlp_g": f["mlp_norm_g"],
        "conv_b_in": f["conv_b_in"], "conv_dw": f["conv_dw"], "conv_dw_b": f["conv_dw_b"],
        "conv_ln_g": f["conv_ln_g"], "conv_ln_b": f["conv_ln_b"], "conv_b_out": f["conv_b_out"],
        "ln_g_2": f["ln_g_2"], "ln_b_2": f["ln_b_2"], "a_ln_g": f["a_ln_g_2"], "a_ln_b": f["a_ln_b_2"],
    }
    out = np.empty((P, NCOL), np.float32)
    for name, v in parts.items():
        c = _columns(v)
        out[:, COLS[name]:COLS[name] + c.shape[1]] = c
    for name, key in (("qn_g", "attn_q_norm_g"), ("kn_g", "attn_k_norm_g")):
        out[0:DH, COLS[name]] = f[key][0]
        out[DH:, COLS[name]] = f[key][0]
    out[:, COLS["sink"]:COLS["sink"] + HEADS] = f["b_sink_2"][0][None, :]
    return out


def _constants():
    t = np.zeros((P, NCONST), np.float32)
    p = np.arange(P)

    def put(name, a):
        t[:, CONST[name]:CONST[name] + a.shape[1]] = a

    put("ident", np.eye(P))
    put("ones", np.ones((P, P)))
    put("head_ones", (p[:, None] // DH == p[None, :] // DH).astype(np.float32))
    swap = np.zeros((P, P))
    swap[p ^ 16, p] = np.where(p & 16, 1.0, -1.0)
    put("perm", swap)
    by_head, spread = np.zeros((P, KT, HEADS)), np.zeros((P, KT, P))
    for k in range(KT):
        by_head[p, k, 2 * k + p // DH] = 1.0
        spread[2 * k + p // DH, k, p] = 1.0
    put("by_head", by_head.reshape(P, KT * HEADS))
    put("spread", spread.reshape(P, KT * P))
    put("slopes", np.broadcast_to(SCALE * 2.0 ** (8.0 * np.arange(1, HEADS + 1) / HEADS), (P, HEADS)))
    k1, k2 = np.arange(P)[None, :], np.arange(T)[None, :]
    d1, d2 = k1 - p[:, None], k2 - (P + p[:, None])
    put("alibi", np.concatenate([np.where(d1 <= 0, d1, NEG), np.where(d2 <= 0, d2, NEG)], 1))
    far = [np.where(np.abs(k2 - (P * b + p[:, None])) <= 128, 0.0, NEG) for b in range(2)]
    put("window", np.concatenate([far[0], np.zeros((P, T)), far[1], np.zeros((P, T))], 1))
    n = 16
    inv = (10000.0 ** (-np.arange(n, dtype=np.float32) / n)).astype(np.float32)
    tok = np.arange(T)
    axis = np.where((p % 64)[:, None] < 32, (tok // 64)[None, :], (tok % 64)[None, :])
    ang = (axis.astype(np.float32) * inv[p % 16][:, None]).astype(np.float32)
    put("cos", np.cos(ang))
    put("sin", np.sin(ang))
    return t


def _features(x):
    return np.ascontiguousarray(x.T.reshape(KT, P, T).transpose(1, 0, 2))


def kernel(**inputs):
    import concourse.bacc as _bacc
    from concourse.bass_utils import run_bass_kernel_spmd as _run

    f = {k: np.asarray(v) for k, v in inputs.items()}
    arrays = {
        "stream": _stream(f),
        "params": _params(f),
        "constants": _constants(),
        "x_features": _features(f["x"][0]),
        "ctx_features": _features(f["ctx_2"][0]),
        "spatial_w": np.ascontiguousarray(f["a_w_s_2"][0].transpose(2, 0, 1)),
        "spatial_b": np.ascontiguousarray(np.broadcast_to(f["a_b_s_2"][0][None], (P, 8, P))),
    }
    nc = _bacc.Bacc("TRN2", target_bir_lowering=False, num_devices=1, dynamic_dma_scratch_size=1024)
    args = [nc.dram_tensor(k, a.shape, F32, kind="ExternalInput").ap() for k, a in arrays.items()]
    args.append(nc.dram_tensor("out_features", (P, KT, T), F32, kind="ExternalOutput").ap())
    build(nc, *args)
    r = _run(nc, [arrays], core_ids=[0])
    got = np.asarray(r.results[0]["out_features"])
    return np.ascontiguousarray(got.transpose(1, 0, 2).reshape(D, T).T)[None]
```
